# Optimizing a Trainium2 kernel written in Bass

```python
import jax, jax.numpy as jnp
from jax import lax
import numpy as np
import math

D_MODEL = 1024
BATCH = 1
SEQ = 256
DEPTH = 2

GRID_W = 64
CTX_LEN = 256
N_MIXERS = 4
D_FF = -(-8 * D_MODEL // (3 * 256)) * 256
DEEPNORM_ALPHA = (2 * DEPTH) ** 0.25
DEEPNORM_BETA = (8 * DEPTH) ** -0.25
LN_EPS = 1e-5
RMS_EPS = 1e-6
ROPE_BASE = 10000.0
CHUNK = 64
NEG_INF = -1e30

RET_HEADS = 4
RET_DK = D_MODEL // RET_HEADS
RET_DV = 2 * RET_DK
NA_HEADS = 16
NA_DH = D_MODEL // NA_HEADS
NA_WIN_ROWS = 8
NA_WIN_COLS = 16
NA_QBLOCK_W = 16
NA_BAND_W = NA_QBLOCK_W + NA_WIN_COLS
MLA_HEADS = 16
MLA_NOPE = 64
MLA_ROPE = 32
MLA_V = 64
MLA_Q_LORA = 512
MLA_KV_LORA = 256
MLA_QBLOCK = 128
HG_EXPAND = 128
HG_HEADS = D_MODEL // HG_EXPAND
HG_DI = D_MODEL // HG_HEADS
HG_FDIM = HG_HEADS * HG_EXPAND


def layer_norm(x, g, b):
    xf = x.astype(jnp.float32)
    xc = xf - jnp.mean(xf, -1, keepdims=True)
    var = jnp.mean(xc * xc, -1, keepdims=True)
    return (xc * lax.rsqrt(var + LN_EPS) * g.astype(jnp.float32) + b.astype(jnp.float32)).astype(x.dtype)

def rms_norm(x, g=None):
    xf = x.astype(jnp.float32)
    y = xf * lax.rsqrt(jnp.mean(xf * xf, -1, keepdims=True) + RMS_EPS)
    if g is not None:
        y = y * g.astype(jnp.float32)
    return y.astype(x.dtype)

def modulate(h, shift, scale):
    return h * (1 + scale) + shift

def axial_rope(n_tokens, rot_dim):
    t = jnp.arange(n_tokens)
    rows = (t // GRID_W).astype(jnp.float32)
    cols = (t % GRID_W).astype(jnp.float32)
    n_freq = rot_dim // 4
    inv = ROPE_BASE ** (-jnp.arange(n_freq, dtype=jnp.float32) / n_freq)
    ang = jnp.concatenate([rows[:, None] * inv, cols[:, None] * inv], -1)
    return jnp.cos(ang)[:, None, :], jnp.sin(ang)[:, None, :]

def apply_rope(x, cos, sin):
    x1, x2 = jnp.split(x.astype(jnp.float32), 2, axis=-1)
    return jnp.concatenate([x1 * cos - x2 * sin, x1 * sin + x2 * cos], -1).astype(x.dtype)

def chunk_gla(q, k, v, log_f, s0):
    B, H, L, dk = q.shape
    dv = v.shape[-1]
    n = L // CHUNK

    def to_chunks(a):
        return a.astype(jnp.float32).reshape(B, H, n, CHUNK, a.shape[-1]).transpose(2, 0, 1, 3, 4)

    mask = jnp.tril(jnp.ones((CHUNK, CHUNK), bool))

    def step(S, inp):
        qi, ki, vi, gi = inp
        b = jnp.cumsum(gi, axis=-2)
        b_last = b[..., -1:, :]
        q_d = qi * jnp.exp(b)
        att = jnp.where(mask, jnp.einsum('bhtk,bhsk->bhts', q_d, ki * jnp.exp(-b)), 0.0)
        o = jnp.einsum('bhts,bhsv->bhtv', att, vi) + jnp.einsum('bhtk,bhkv->bhtv', q_d, S)
        S_new = jnp.exp(b_last[..., 0, :])[..., None] * S + jnp.einsum('bhsk,bhsv->bhkv', ki * jnp.exp(b_last - b), vi)
        return S_new, o

    S_fin, oc = lax.scan(step, s0, (to_chunks(q), to_chunks(k), to_chunks(v), to_chunks(log_f)))
    return oc.transpose(1, 2, 0, 3, 4).reshape(B, H, L, dv), S_fin

def bidirectional_scan(ctx_terms, lat_terms):
    qc, kcf, kcb, vc, gcf, gcb = ctx_terms
    ql, klf, klb, vl, glf, glb = lat_terms
    B, H, _, dk = qc.shape
    s0 = jnp.zeros((B, H, dk, vc.shape[-1]), jnp.float32)
    flip = lambda t: jnp.flip(t, axis=2)
    o_cf, s_cf = chunk_gla(qc, kcf, vc, gcf, s0)
    o_cb, s_cb = chunk_gla(flip(qc), flip(kcb), flip(vc), flip(gcb), s0)
    o_lf, _ = chunk_gla(ql, klf, vl, glf, s_cf)
    o_lb, _ = chunk_gla(flip(ql), flip(klb), flip(vl), flip(glb), s_cb)
    return o_cf + flip(o_cb), o_lf + flip(o_lb)

def retention_mixer(a_ctx, a_lat, w_in, decay_param, w_out, want_ctx):
    B, L, _ = a_lat.shape
    hk, hv = RET_HEADS * RET_DK, RET_HEADS * RET_DV
    log_gamma = -jnp.exp(decay_param.astype(jnp.float32))

    def project(a, rope):
        n = a.shape[1]
        q, k, v, g = jnp.split(a @ w_in, [hk, 2 * hk, 2 * hk + hv], axis=-1)
        q = q.reshape(B, n, RET_HEADS, RET_DK)
        k = k.reshape(B, n, RET_HEADS, RET_DK)
        if rope is not None:
            q, k = apply_rope(q, *rope), apply_rope(k, *rope)
        k = k * RET_DK ** -0.5
        v = v.reshape(B, n, RET_HEADS, RET_DV)
        decay = lambda lg: jnp.broadcast_to(lg[None, :, None, None], (B, RET_HEADS, n, RET_DK))
        qh, kh, vh = (t.transpose(0, 2, 1, 3) for t in (q, k, v))
        return (qh, kh, kh, vh, decay(log_gamma[0]), decay(log_gamma[1])), g

    ctx_terms, g_ctx = project(a_ctx, None)
    lat_terms, g_lat = project(a_lat, axial_rope(L, RET_DK))
    o_ctx, o_lat = bidirectional_scan(ctx_terms, lat_terms)

    def readout(o, g):
        n = o.shape[2]
        y = rms_norm(o).transpose(0, 2, 1, 3).reshape(B, n, hv).astype(g.dtype)
        return (jax.nn.silu(g) * y) @ w_out

    return (readout(o_ctx, g_ctx) if want_ctx else None), readout(o_lat, g_lat)

def neighbourhood_mixer(a_ctx, a_lat, w_qkv, rpb, w_out, want_ctx):
    B, L, _ = a_lat.shape
    Lc = a_ctx.shape[1]
    rows = L // GRID_W
    wr = min(NA_WIN_ROWS, rows)
    scale = NA_DH ** -0.5
    q, k, v = jnp.split(a_lat @ w_qkv, 3, axis=-1)
    grid = lambda t: t.reshape(B, rows, GRID_W, NA_HEADS, NA_DH)
    q, k, v = grid(q * scale), grid(k), grid(v)
    qc, kc, vc = (t.reshape(B, Lc, NA_HEADS, NA_DH) for t in jnp.split(a_ctx @ w_qkv, 3, axis=-1))

    n_cb = GRID_W // NA_QBLOCK_W
    band0 = np.clip(np.arange(n_cb) * NA_QBLOCK_W - NA_WIN_COLS // 2, 0, GRID_W - NA_BAND_W)
    kcol = band0[:, None] + np.arange(NA_BAND_W)
    qcol = np.arange(GRID_W).reshape(n_cb, NA_QBLOCK_W)
    wstart = np.clip(qcol - NA_WIN_COLS // 2, 0, GRID_W - NA_WIN_COLS)
    kc3 = kcol[:, None, :]
    col_ok = (kc3 >= wstart[..., None]) & (kc3 < wstart[..., None] + NA_WIN_COLS)
    c_idx = np.clip(kc3 - qcol[..., None] + NA_WIN_COLS - 1, 0, 2 * NA_WIN_COLS - 2)

    def row(r):
        rs = jnp.clip(r - wr // 2, 0, rows - wr)
        qr = lax.dynamic_index_in_dim(q, r, axis=1, keepdims=False).reshape(B, n_cb, NA_QBLOCK_W, NA_HEADS, NA_DH)
        kb = lax.dynamic_slice_in_dim(k, rs, wr, axis=1)[:, :, kcol]
        vb = lax.dynamic_slice_in_dim(v, rs, wr, axis=1)[:, :, kcol]
        r_idx = rs + jnp.arange(wr) - r + NA_WIN_ROWS - 1
        bias = rpb[:, r_idx[None, None, :, None], c_idx[:, :, None, :]]
        s_lat = jnp.einsum('bnqhd,brnkhd->bhnqrk', qr, kb).astype(jnp.float32) + bias[None].astype(jnp.float32)
        s_lat = jnp.where(col_ok[:, :, None, :], s_lat, NEG_INF).reshape(B, NA_HEADS, n_cb, NA_QBLOCK_W, wr * NA_BAND_W)
        s_ctx = jnp.einsum('bnqhd,bchd->bhnqc', qr, kc).astype(jnp.float32)
        p = jax.nn.softmax(jnp.concatenate([s_lat, s_ctx], -1), -1).astype(v.dtype)
        p_lat = p[..., :wr * NA_BAND_W].reshape(B, NA_HEADS, n_cb, NA_QBLOCK_W, wr, NA_BAND_W)
        o = jnp.einsum('bhnqrk,brnkhd->bnqhd', p_lat, vb) + jnp.einsum('bhnqc,bchd->bnqhd', p[..., wr * NA_BAND_W:], vc)
        return o.reshape(B, GRID_W, NA_HEADS * NA_DH)

    o_lat = lax.map(row, jnp.arange(rows)).transpose(1, 0, 2, 3).reshape(B, L, NA_HEADS * NA_DH)
    y_ctx = None
    if want_ctx:
        s = jnp.einsum('bqhd,bkhd->bhqk', qc * scale, kc).astype(jnp.float32)
        p = jax.nn.softmax(s, -1).astype(vc.dtype)
        y_ctx = jnp.einsum('bhqk,bkhd->bqhd', p, vc).reshape(B, Lc, NA_HEADS * NA_DH) @ w_out
    return y_ctx, o_lat @ w_out

def mla_mixer(a_ctx, a_lat, w_down, q_norm, kv_norm, w_uq, w_ukv, w_out, want_ctx):
    B, L, _ = a_lat.shape
    scale = (MLA_NOPE + MLA_ROPE) ** -0.5

    def project(a, rope):
        n = a.shape[1]
        cq, ckv, kr = jnp.split(a @ w_down, [MLA_Q_LORA, MLA_Q_LORA + MLA_KV_LORA], axis=-1)
        q = (rms_norm(cq, q_norm) @ w_uq).reshape(B, n, MLA_HEADS, MLA_NOPE + MLA_ROPE)
        kv = (rms_norm(ckv, kv_norm) @ w_ukv).reshape(B, n, MLA_HEADS, MLA_NOPE + MLA_V)
        q_nope, q_rope = jnp.split(q, [MLA_NOPE], axis=-1)
        k_nope, v = jnp.split(kv, [MLA_NOPE], axis=-1)
        kr = kr[:, :, None, :]
        if rope is not None:
            q_rope, kr = apply_rope(q_rope, *rope), apply_rope(kr, *rope)
        q = jnp.concatenate([q_nope, q_rope], -1) * scale
        k = jnp.concatenate([k_nope, jnp.broadcast_to(kr, (B, n, MLA_HEADS, MLA_ROPE))], -1)
        return q, k, v

    qc, kc, vc = project(a_ctx, None)
    ql, kl, vl = project(a_lat, axial_rope(L, MLA_ROPE))
    k_all = jnp.concatenate([kc, kl], axis=1)
    v_all = jnp.concatenate([vc, vl], axis=1)

    def attend(qb, keys, vals):
        s = jnp.einsum('bqhd,bkhd->bhqk', qb, keys).astype(jnp.float32)
        p = jax.nn.softmax(s, -1).astype(vals.dtype)
        return jnp.einsum('bhqk,bkhd->bqhd', p, vals)

    nb = L // MLA_QBLOCK
    qblocks = ql.reshape(B, nb, MLA_QBLOCK, MLA_HEADS, MLA_NOPE + MLA_ROPE).transpose(1, 0, 2, 3, 4)
    o = lax.map(lambda qb: attend(qb, k_all, v_all), qblocks)
    o_lat = o.transpose(1, 0, 2, 3, 4).reshape(B, L, MLA_HEADS * MLA_V)
    y_ctx = attend(qc, kc, vc).reshape(B, -1, MLA_HEADS * MLA_V) @ w_out if want_ctx else None
    return y_ctx, o_lat @ w_out

def hgrn2_mixer(a_ctx, a_lat, w_in, lower_bounds, norm_g, w_out, layer_idx, want_ctx):
    B = a_lat.shape[0]
    lb_soft = jax.nn.softmax(lower_bounds.astype(jnp.float32), axis=0)
    lb = (jnp.cumsum(lb_soft, axis=0) - lb_soft[0])[layer_idx]

    def project(a):
        n = a.shape[1]
        q, f_f, f_b, i, g = jnp.split(a @ w_in, [HG_FDIM, 2 * HG_FDIM, 3 * HG_FDIM, 3 * HG_FDIM + HG_HEADS * HG_DI], axis=-1)
        heads = lambda t, d: t.reshape(B, n, HG_HEADS, d).transpose(0, 2, 1, 3)
        q = heads(jax.nn.silu(q), HG_EXPAND) * HG_EXPAND ** -0.5

        def gate(f):
            forget = lb + (1 - lb) * jax.nn.sigmoid(f.astype(jnp.float32))
            return heads(1 - forget, HG_EXPAND), heads(jnp.log(forget), HG_EXPAND)

        kf, gf = gate(f_f)
        kb, gb = gate(f_b)
        return (q, kf, kb, heads(i, HG_DI), gf, gb), g

    ctx_terms, g_ctx = project(a_ctx)
    lat_terms, g_lat = project(a_lat)
    o_ctx, o_lat = bidirectional_scan(ctx_terms, lat_terms)

    def readout(o, g):
        n = o.shape[2]
        y = rms_norm(o, norm_g).transpose(0, 2, 1, 3).reshape(B, n, HG_HEADS * HG_DI).astype(g.dtype)
        return (y * jax.nn.silu(g)) @ w_out

    return (readout(o_ctx, g_ctx) if want_ctx else None), readout(o_lat, g_lat)

def swiglu(a, w13, w2):
    gate, up = jnp.split(a @ w13, 2, axis=-1)
    return (jax.nn.silu(gate) * up) @ w2

def first_inputs(seed: int = 0) -> dict:
    key = jax.random.key(seed)
    ks = iter(jax.random.split(key, 32))
    nrm = lambda shape, std: std * jax.random.normal(next(ks), shape, jnp.float32)
    D, F, beta = D_MODEL, D_FF, DEEPNORM_BETA
    ret_decay_base = jnp.log(-jnp.log1p(-(2.0 ** (-5.0 - jnp.arange(RET_HEADS, dtype=jnp.float32)))))
    return {
        'x': nrm((BATCH, SEQ, D), 1.0),
        'c': nrm((BATCH, D), 1.0),
        'ctx': nrm((BATCH, CTX_LEN, D), 1.0),
        'c_ctx': nrm((D,), 1.0),
        'ada_w': nrm((DEPTH, D, 6 * D), D ** -0.5),
        'ada_b': nrm((DEPTH, 6 * D), 0.01),
        'ln_g': 1.0 + nrm((DEPTH, 2, D), 0.01),
        'ln_b': nrm((DEPTH, 2, D), 0.01),
        'ffn_w13': nrm((DEPTH, D, 2 * F), D ** -0.5),
        'ffn_w2': nrm((DEPTH, F, D), beta * F ** -0.5),
        'ret_w_in': nrm((D, 2 * RET_HEADS * RET_DK + 2 * RET_HEADS * RET_DV), D ** -0.5),
        'ret_decay': ret_decay_base[None, :] + nrm((2, RET_HEADS), 0.01),
        'ret_w_out': nrm((RET_HEADS * RET_DV, D), beta * (RET_HEADS * RET_DV) ** -0.5),
        'na_w_qkv': nrm((D, 3 * NA_HEADS * NA_DH), D ** -0.5),
        'na_rpb': nrm((NA_HEADS, 2 * NA_WIN_ROWS - 1, 2 * NA_WIN_COLS - 1), 0.02),
        'na_w_out': nrm((NA_HEADS * NA_DH, D), beta * (NA_HEADS * NA_DH) ** -0.5),
        'mla_w_down': nrm((D, MLA_Q_LORA + MLA_KV_LORA + MLA_ROPE), D ** -0.5),
        'mla_q_norm': 1.0 + nrm((MLA_Q_LORA,), 0.01),
        'mla_kv_norm': 1.0 + nrm((MLA_KV_LORA,), 0.01),
        'mla_w_uq': nrm((MLA_Q_LORA, MLA_HEADS * (MLA_NOPE + MLA_ROPE)), MLA_Q_LORA ** -0.5),
        'mla_w_ukv': nrm((MLA_KV_LORA, MLA_HEADS * (MLA_NOPE + MLA_V)), MLA_KV_LORA ** -0.5),
        'mla_w_out': nrm((MLA_HEADS * MLA_V, D), beta * (MLA_HEADS * MLA_V) ** -0.5),
        'hg_w_in': nrm((D, 3 * HG_FDIM + 2 * HG_HEADS * HG_DI), D ** -0.5),
        'hg_lower_bounds': nrm((DEPTH, HG_FDIM), 0.1),
        'hg_norm_g': 1.0 + nrm((HG_DI,), 0.01),
        'hg_w_out': nrm((HG_HEADS * HG_DI, D), beta * (HG_HEADS * HG_DI) ** -0.5),
    }

def first_block(x, c, ctx, c_ctx, ada_w, ada_b, ln_g, ln_b, ffn_w13, ffn_w2,
              ret_w_in, ret_decay, ret_w_out,
              na_w_qkv, na_rpb, na_w_out,
              mla_w_down, mla_q_norm, mla_kv_norm, mla_w_uq, mla_w_ukv, mla_w_out,
              hg_w_in, hg_lower_bounds, hg_norm_g, hg_w_out):
    h_lat, h_ctx = x, ctx
    cond_lat = jax.nn.silu(c)[:, None, :]
    cond_ctx = jax.nn.silu(c_ctx)[None, None, :]
    for i in range(DEPTH):
        want_ctx = i < DEPTH - 1
        m_lat = jnp.split(cond_lat @ ada_w[i] + ada_b[i], 6, axis=-1)
        m_ctx = jnp.split(cond_ctx @ ada_w[i] + ada_b[i], 6, axis=-1)
        a_lat = modulate(h_lat, m_lat[0], m_lat[1])
        a_ctx = modulate(h_ctx, m_ctx[0], m_ctx[1])
        kind = i % N_MIXERS
        if kind == 0:
            y_ctx, y_lat = retention_mixer(a_ctx, a_lat, ret_w_in, ret_decay, ret_w_out, want_ctx)
        elif kind == 1:
            y_ctx, y_lat = neighbourhood_mixer(a_ctx, a_lat, na_w_qkv, na_rpb, na_w_out, want_ctx)
        elif kind == 2:
            y_ctx, y_lat = mla_mixer(a_ctx, a_lat, mla_w_down, mla_q_norm, mla_kv_norm, mla_w_uq, mla_w_ukv, mla_w_out, want_ctx)
        else:
            y_ctx, y_lat = hgrn2_mixer(a_ctx, a_lat, hg_w_in, hg_lower_bounds, hg_norm_g, hg_w_out, i, want_ctx)
        h_lat = layer_norm(DEEPNORM_ALPHA * h_lat + m_lat[2] * y_lat, ln_g[i, 0], ln_b[i, 0])
        f_lat = swiglu(modulate(h_lat, m_lat[3], m_lat[4]), ffn_w13[i], ffn_w2[i])
        h_lat = layer_norm(DEEPNORM_ALPHA * h_lat + m_lat[5] * f_lat, ln_g[i, 1], ln_b[i, 1])
        if want_ctx:
            h_ctx = layer_norm(DEEPNORM_ALPHA * h_ctx + m_ctx[2] * y_ctx, ln_g[i, 0], ln_b[i, 0])
            f_ctx = swiglu(modulate(h_ctx, m_ctx[3], m_ctx[4]), ffn_w13[i], ffn_w2[i])
            h_ctx = layer_norm(DEEPNORM_ALPHA * h_ctx + m_ctx[5] * f_ctx, ln_g[i, 1], ln_b[i, 1])
    return h_lat


DN_HEADS = 8
DN_HEAD_DIM = 128
DN_WIDTH = DN_HEADS * DN_HEAD_DIM
DN_CONV = 4
DN_CHUNK = 64
DA_HEADS = 12
DA_HEAD_DIM = 64
DA_WIDTH = DA_HEADS * DA_HEAD_DIM
DA_PATTERNS = ((128, 1), (512, 4), (2048, 16))
DA_BLOCK = 128
ALIBI_MAX_EXP = 8.0
D_FF_2 = 2816
MACARON_WEIGHT = 0.5
NORM_EPS = 1e-6
N_ADA = 9
IN_SPLITS = (3 * DN_WIDTH, DN_WIDTH, DN_HEADS, DN_HEADS,
             DA_WIDTH, DA_WIDTH, DA_WIDTH, D_MODEL, D_MODEL)
IN_COLS = 3 * DN_WIDTH + DN_WIDTH + 2 * DN_HEADS + 3 * DA_WIDTH + 2 * D_MODEL


def rmsnorm(x, g):
    xf = x.astype(jnp.float32)
    y = xf * lax.rsqrt(jnp.mean(xf * xf, axis=-1, keepdims=True) + NORM_EPS)
    return (y * g.astype(jnp.float32)).astype(x.dtype)

def l2norm(x):
    xf = x.astype(jnp.float32)
    return xf * lax.rsqrt(jnp.sum(xf * xf, axis=-1, keepdims=True) + NORM_EPS)

def modulate_2(x, shift, scale):
    return x * (1.0 + scale[:, None, :]) + shift[:, None, :]

def swiglu_2(x, w_gate, w_up, w_down):
    return (jax.nn.silu(x @ w_gate) * (x @ w_up)) @ w_down

def causal_depthwise_conv(x, w):
    K = w.shape[0]
    S = x.shape[1]
    xp = jnp.pad(x, ((0, 0), (K - 1, 0), (0, 0)))
    y = xp[:, 0:S] * w[0]
    for j in range(1, K):
        y = y + xp[:, j:j + S] * w[j]
    return y

def gated_delta_rule(q, k, v, g, beta):
    B, S, H, dk = q.shape
    dv = v.shape[-1]
    C = DN_CHUNK
    N = S // C
    f32 = jnp.float32

    def chunks(t):
        t = t.astype(f32).reshape((B, N, C, H) + t.shape[3:])
        return t.transpose((1, 0, 3, 2) + tuple(range(4, t.ndim)))

    qc, kc, vc = chunks(q), chunks(k), chunks(v)
    gc = jnp.cumsum(chunks(g), axis=-1)
    bc = chunks(beta)
    kb = kc * bc[..., None]
    vb = vc * bc[..., None]
    incl = jnp.tril(jnp.ones((C, C), dtype=bool))
    strict = jnp.tril(jnp.ones((C, C), dtype=bool), -1)
    decay = jnp.exp(jnp.where(incl, gc[..., :, None] - gc[..., None, :], -jnp.inf))
    m = jnp.where(strict, jnp.einsum('nbhid,nbhjd->nbhij', kb, kc) * decay, 0.0)
    a = m + jnp.eye(C, dtype=f32)
    u_c = lax.linalg.triangular_solve(a, vb, left_side=True, lower=True, unit_diagonal=True)
    w_c = lax.linalg.triangular_solve(a, kb * jnp.exp(gc)[..., None], left_side=True,
                                      lower=True, unit_diagonal=True)
    qk = jnp.einsum('nbhid,nbhjd->nbhij', qc, kc) * decay

    def step(state, xs):
        q_i, k_i, u_i, w_i, g_i, qk_i = xs
        v_new = u_i - jnp.einsum('bhcd,bhde->bhce', w_i, state)
        o_i = (jnp.einsum('bhcd,bhde->bhce', q_i * jnp.exp(g_i)[..., None], state)
               + jnp.einsum('bhij,bhje->bhie', qk_i, v_new))
        g_last = g_i[..., -1]
        state = (state * jnp.exp(g_last)[..., None, None]
                 + jnp.einsum('bhcd,bhce->bhde',
                              k_i * jnp.exp(g_last[..., None] - g_i)[..., None], v_new))
        return state, o_i

    state0 = jnp.zeros((B, H, dk, dv), f32)
    _, o = lax.scan(step, state0, (qc, kc, u_c, w_c, gc, qk))
    return o.transpose(1, 0, 3, 2, 4).reshape(B, S, H, dv)

def dilated_window_branch(q, k, v, slopes, window, dilation):
    B, S, H, dh = q.shape
    r = dilation
    n = S // r
    span = window // r
    nb = -(-n // DA_BLOCK)
    n_pad = nb * DA_BLOCK
    z = B * r

    def to_sub(t):
        t = t.reshape(B, n, r, H, dh).transpose(0, 2, 1, 3, 4).reshape(z, n, H, dh)
        return jnp.pad(t, ((0, 0), (0, n_pad - n), (0, 0), (0, 0)))

    def band(t):
        tp = jnp.pad(t, ((0, 0), (DA_BLOCK, 0), (0, 0), (0, 0)))
        prev = tp[:, :n_pad].reshape(z, nb, DA_BLOCK, H, dh)
        cur = t.reshape(z, nb, DA_BLOCK, H, dh)
        return jnp.concatenate([prev, cur], axis=2)

    qs, ks, vs = to_sub(q), to_sub(k), to_sub(v)
    qb = qs.reshape(z, nb, DA_BLOCK, H, dh)
    kb, vb = band(ks), band(vs)
    s = jnp.einsum('znqhd,znkhd->znhqk', qb, kb).astype(jnp.float32) * (dh ** -0.5)
    qi = jnp.arange(DA_BLOCK)[:, None]
    ki = jnp.arange(2 * DA_BLOCK)[None, :]
    dist = qi + DA_BLOCK - ki
    key_pos = jnp.arange(nb)[:, None, None] * DA_BLOCK + ki[None] - DA_BLOCK
    valid = (dist[None] >= 0) & (dist[None] <= span) & (key_pos >= 0)
    bias = -slopes[:, None, None] * (dist * r).astype(jnp.float32)[None]
    s = jnp.where(valid[None, :, None], s + bias[None, None], -jnp.inf)
    mx = jnp.max(s, axis=-1, keepdims=True)
    p = jnp.exp(s - mx)
    l = jnp.sum(p, axis=-1, keepdims=True)
    o = jnp.einsum('znhqk,znkhd->znqhd', (p / l).astype(v.dtype), vb).astype(jnp.float32)
    lse = (mx + jnp.log(l))[..., 0]
    o = o.reshape(z, n_pad, H, dh)[:, :n].reshape(B, r, n, H, dh)
    o = o.transpose(0, 2, 1, 3, 4).reshape(B, S, H, dh)
    lse = lse.transpose(0, 1, 3, 2).reshape(z, n_pad, H)[:, :n].reshape(B, r, n, H)
    lse = lse.transpose(0, 2, 1, 3).reshape(B, S, H)
    return o, lse

def hybrid_mixer(u, w_in, conv_w, a_log, dt_bias, dn_norm, w_a, w_b, w_o):
    B, S, _ = u.shape
    proj = u @ w_in
    idx = np.cumsum(IN_SPLITS)[:-1].tolist()
    dn_qkv, dn_z, dn_b, dn_a, da_q, da_k, da_v, gate_a, gate_b = jnp.split(proj, idx, axis=-1)

    qkv = jax.nn.silu(causal_depthwise_conv(dn_qkv, conv_w))
    q, k, v = jnp.split(qkv, 3, axis=-1)
    q = l2norm(q.reshape(B, S, DN_HEADS, DN_HEAD_DIM)) * (DN_HEAD_DIM ** -0.5)
    k = l2norm(k.reshape(B, S, DN_HEADS, DN_HEAD_DIM))
    v = v.reshape(B, S, DN_HEADS, DN_HEAD_DIM)
    beta = jax.nn.sigmoid(dn_b.astype(jnp.float32))
    g = -jnp.exp(a_log.astype(jnp.float32)) * jax.nn.softplus(
        dn_a.astype(jnp.float32) + dt_bias.astype(jnp.float32))
    o_a = gated_delta_rule(q, k, v, g, beta).astype(u.dtype)
    o_a = rmsnorm(o_a, dn_norm) * jax.nn.silu(dn_z.reshape(B, S, DN_HEADS, DN_HEAD_DIM))
    y_a = o_a.reshape(B, S, DN_WIDTH) @ w_a

    qd = da_q.reshape(B, S, DA_HEADS, DA_HEAD_DIM)
    kd = da_k.reshape(B, S, DA_HEADS, DA_HEAD_DIM)
    vd = da_v.reshape(B, S, DA_HEADS, DA_HEAD_DIM)
    slopes = 2.0 ** (-ALIBI_MAX_EXP * jnp.arange(1, DA_HEADS + 1, dtype=jnp.float32) / DA_HEADS)
    outs, lses = [], []
    for window, dilation in DA_PATTERNS:
        o_p, lse_p = dilated_window_branch(qd, kd, vd, slopes, window, dilation)
        outs.append(o_p)
        lses.append(lse_p)
    wts = jax.nn.softmax(jnp.stack(lses, axis=0), axis=0)
    o_b = jnp.sum(wts[..., None] * jnp.stack(outs, axis=0), axis=0).astype(u.dtype)
    y_b = o_b.reshape(B, S, DA_WIDTH) @ w_b

    merged = jax.nn.sigmoid(gate_a) * y_a + jax.nn.sigmoid(gate_b) * y_b
    return merged @ w_o

def second_inputs(seed: int = 0) -> dict:
    key = jax.random.key(seed)
    ks = jax.random.split(key, 24)
    f32 = jnp.float32
    D = D_MODEL

    def nrm(k, shape, scale):
        return jax.random.normal(k, shape, f32) * scale

    x = nrm(ks[0], (BATCH, SEQ, D), 1.0)
    c = nrm(ks[1], (BATCH, D), 1.0)
    ada_w = nrm(ks[2], (DEPTH, D, N_ADA * D), 0.5 * D ** -0.5)
    ada_b = nrm(ks[3], (DEPTH, N_ADA * D), 0.02)
    ln_ffn1 = 1.0 + nrm(ks[4], (DEPTH, D), 0.02)
    ln_mix = 1.0 + nrm(ks[5], (DEPTH, D), 0.02)
    ln_ffn2 = 1.0 + nrm(ks[6], (DEPTH, D), 0.02)
    ffn1_wg = nrm(ks[7], (DEPTH, D, D_FF_2), D ** -0.5)
    ffn1_wu = nrm(ks[8], (DEPTH, D, D_FF_2), D ** -0.5)
    ffn1_wd = nrm(ks[9], (DEPTH, D_FF_2, D), D_FF_2 ** -0.5)
    w_in = nrm(ks[10], (DEPTH, D, IN_COLS), D ** -0.5)
    conv_w = nrm(ks[11], (DEPTH, DN_CONV, 3 * DN_WIDTH), DN_CONV ** -0.5)
    a_log = jnp.log(jax.random.uniform(ks[12], (DEPTH, DN_HEADS), f32, 1.0, 16.0))
    dt = jnp.exp(jax.random.uniform(ks[13], (DEPTH, DN_HEADS), f32,
                                    math.log(1e-3), math.log(1e-1)))
    dt_bias = dt + jnp.log(-jnp.expm1(-dt))
    dn_norm = 1.0 + nrm(ks[14], (DEPTH, DN_HEAD_DIM), 0.02)
    w_a = nrm(ks[15], (DEPTH, DN_WIDTH, D), DN_WIDTH ** -0.5)
    w_b = nrm(ks[16], (DEPTH, DA_WIDTH, D), DA_WIDTH ** -0.5)
    w_o = nrm(ks[17], (DEPTH, D, D), D ** -0.5)
    ffn2_wg = nrm(ks[18], (DEPTH, D, D_FF_2), D ** -0.5)
    ffn2_wu = nrm(ks[19], (DEPTH, D, D_FF_2), D ** -0.5)
    ffn2_wd = nrm(ks[20], (DEPTH, D_FF_2, D), D_FF_2 ** -0.5)
    final_norm = 1.0 + nrm(ks[21], (D,), 0.02)
    return {"x": x, "c": c, "ada_w": ada_w, "ada_b": ada_b,
            "ln_ffn1": ln_ffn1, "ln_mix": ln_mix, "ln_ffn2": ln_ffn2,
            "ffn1_wg": ffn1_wg, "ffn1_wu": ffn1_wu, "ffn1_wd": ffn1_wd,
            "w_in": w_in, "conv_w": conv_w, "a_log": a_log, "dt_bias": dt_bias,
            "dn_norm": dn_norm, "w_a": w_a, "w_b": w_b, "w_o": w_o,
            "ffn2_wg": ffn2_wg, "ffn2_wu": ffn2_wu, "ffn2_wd": ffn2_wd,
            "final_norm": final_norm}

def second_block(x, c, ada_w, ada_b, ln_ffn1, ln_mix, ln_ffn2, ffn1_wg, ffn1_wu, ffn1_wd,
              w_in, conv_w, a_log, dt_bias, dn_norm, w_a, w_b, w_o,
              ffn2_wg, ffn2_wu, ffn2_wd, final_norm):
    h = x
    c_act = jax.nn.silu(c)
    for l in range(DEPTH):
        mod = c_act @ ada_w[l] + ada_b[l]
        (sh1, sc1, gt1, sh2, sc2, gt2, sh3, sc3, gt3) = jnp.split(mod, N_ADA, axis=-1)
        f = swiglu_2(modulate_2(rmsnorm(h, ln_ffn1[l]), sh1, sc1), ffn1_wg[l], ffn1_wu[l], ffn1_wd[l])
        h = h + MACARON_WEIGHT * gt1[:, None, :] * f
        u = modulate_2(rmsnorm(h, ln_mix[l]), sh2, sc2)
        m = hybrid_mixer(u, w_in[l], conv_w[l], a_log[l], dt_bias[l], dn_norm[l],
                         w_a[l], w_b[l], w_o[l])
        h = h + gt2[:, None, :] * m
        f = swiglu_2(modulate_2(rmsnorm(h, ln_ffn2[l]), sh3, sc3), ffn2_wg[l], ffn2_wu[l], ffn2_wd[l])
        h = h + MACARON_WEIGHT * gt3[:, None, :] * f
    return rmsnorm(h, final_norm)


def setup_inputs(seed=0):
    out = dict(first_inputs(seed))
    for name, value in second_inputs(seed + 1).items():
        if name != "x":
            out[name + "_2"] = value
    return out


def reference(
    x, c, ctx, c_ctx, ada_w, ada_b, ln_g, ln_b, ffn_w13, ffn_w2, ret_w_in, ret_decay, ret_w_out,
    na_w_qkv, na_rpb, na_w_out, mla_w_down, mla_q_norm, mla_kv_norm, mla_w_uq, mla_w_ukv,
    mla_w_out, hg_w_in, hg_lower_bounds, hg_norm_g, hg_w_out, c_2, ada_w_2, ada_b_2, ln_ffn1_2,
    ln_mix_2, ln_ffn2_2, ffn1_wg_2, ffn1_wu_2, ffn1_wd_2, w_in_2, conv_w_2, a_log_2, dt_bias_2,
    dn_norm_2, w_a_2, w_b_2, w_o_2, ffn2_wg_2, ffn2_wu_2, ffn2_wd_2, final_norm_2,
):
    x = first_block(
        x, c, ctx, c_ctx, ada_w, ada_b, ln_g, ln_b, ffn_w13, ffn_w2, ret_w_in, ret_decay,
        ret_w_out, na_w_qkv, na_rpb, na_w_out, mla_w_down, mla_q_norm, mla_kv_norm, mla_w_uq,
        mla_w_ukv, mla_w_out, hg_w_in, hg_lower_bounds, hg_norm_g, hg_w_out,
    )
    return second_block(
        x, c_2, ada_w_2, ada_b_2, ln_ffn1_2, ln_mix_2, ln_ffn2_2, ffn1_wg_2, ffn1_wu_2,
        ffn1_wd_2, w_in_2, conv_w_2, a_log_2, dt_bias_2, dn_norm_2, w_a_2, w_b_2, w_o_2,
        ffn2_wg_2, ffn2_wu_2, ffn2_wd_2, final_norm_2,
    )


_drawn_inputs = setup_inputs


def setup_inputs(seed=0):
    import zlib

    import numpy as np

    out = dict(_drawn_inputs(seed))
    spreads = {}
    factors = {'ada_b': 5.332,
     'ln_g': 2.697,
     'na_rpb': 8.0,
     'ln_ffn1_2': 8.0,
     'ln_mix_2': 8.0,
     'ln_ffn2_2': 8.0,
     'a_log_2': 2.702,
     'dn_norm_2': 8.0,
     'final_norm_2': 2.832}
    for name, (base, spread) in spreads.items():
        noise = np.random.default_rng([zlib.crc32(name.encode()), seed]).standard_normal(out[name].shape)
        drawn = base * np.exp(spread * noise) if base else spread * noise
        out[name] = __import__('jax').numpy.asarray(drawn.astype(out[name].dtype))
    for name, factor in factors.items():
        out[name] = (out[name] * factor).astype(out[name].dtype)
    return out
```

```python
from contextlib import ExitStack, contextmanager

import numpy as np

import concourse.bass as bass
from concourse import mybir

F32 = mybir.dt.float32
F32R = mybir.dt.float32r
ALU = mybir.AluOpType
ACT = mybir.ActivationFunctionType
AX = mybir.AxisListType

P = 128
T = 256
D = 1024
KD = D // P
FF = 2816
KF = FF // P
ALPHA = float(4 ** 0.25)
LN_EPS = 1e-5
RMS_EPS = 1e-6
RING = 4
SLOT = 2048
RET_H, RET_DK, RET_DV = 4, 256, 512
NA_H, NA_COLS, GRID = 16, 31, 64
DN_H = 8
DA_H, DA_DH = 12, 64
DA_W = DA_H * DA_DH
NLEV = 7
TRI = 3 * P

IN_Z, IN_BA = 3 * D, 4 * D
IN_DA = IN_BA + 2 * DN_H
IN_GATE = IN_DA + 3 * DA_W


def shape_tables():
    p = np.arange(P)
    t = np.arange(T)
    ident = np.eye(P)
    ones = np.ones((P, P))
    nf = RET_DK // 4
    inv = 10000.0 ** (-np.arange(nf, dtype=np.float32) / np.float32(nf))
    inv = inv.astype(np.float32)
    rows, cols = (t // GRID).astype(np.float32), (t % GRID).astype(np.float32)
    ang = np.concatenate([rows[:, None] * inv, cols[:, None] * inv], -1).astype(np.float32)
    cos, sin = np.cos(ang).T, np.sin(ang).T
    dist = np.concatenate([t[None, :] - (p[:, None] + P * i) + T for i in range(2)], 1)
    qc, kc = (p % GRID)[:, None], np.arange(GRID)[None, :]
    w0 = np.clip(qc - 8, 0, GRID - 16)
    win = np.where((kc >= w0) & (kc < w0 + 16), 0.0, -1e30)
    first = np.concatenate([ident, ones], 1)
    block1 = np.concatenate([cos, sin, dist, win], 1)

    d0 = p[:, None] - p[None, :]
    d1 = p[:, None] + P - np.arange(T)[None, :]
    dd = np.concatenate([d0, d1], 1)
    count = sum(((dd >= 0) & (dd % r == 0) & (dd // r <= P)).astype(float) for r in (1, 4, 16))
    lnc = np.where(count > 0, np.log(np.maximum(count, 1.0)), -1e30)
    dd = np.maximum(dd, 0)
    gt = (p[:, None] > p[None, :]).astype(float)
    le = (p[:, None] <= t[None, :]).astype(float)
    incl = np.concatenate([(p[:, None] <= t[None, :]), (p[:, None] <= p[None, :])], 1).astype(float)
    strict = np.concatenate([(p[:, None] < t[None, :]), (p[:, None] < p[None, :])], 1).astype(float)
    lev = []
    for j in range(NLEV):
        b = 2 ** j
        s_, t_ = p[:, None], p[None, :]
        lev.append(((s_ // (2 * b) == t_ // (2 * b)) & ((t_ // b) % 2 == 1) & ((s_ // b) % 2 == 0)).astype(float))
    slope = np.broadcast_to(-(2.0 ** (-8.0 * np.arange(1, DA_H + 1) / DA_H))[None, :], (P, DA_H))
    block2 = np.concatenate([dd, lnc, gt, le, incl, strict] + lev + [slope], 1)
    return [np.ascontiguousarray(x, dtype=np.float32) for x in (first, block1, block2)]


class Program:

    def __init__(self, nc, counted):
        self.nc = nc
        self.counted = counted
        self.base = {}
        self.sems = {}
        self.owner = {}
        self.last = {}
        self.loops = []
        self.n_loops = 0
        self.eng = {"pe": nc.tensor, "dve": nc.vector, "act": nc.scalar, "pool": nc.gpsimd, "sp": nc.sync}
        for engine in ("pe", "dve", "act", "pool"):
            self.sem("done_" + engine, engine)
            self.last[engine] = ("done_" + engine,)
            self.sem("settled_" + engine)
        self.sem("settled_sp")

    def sem(self, name, owner=None):
        self.sems[name] = self.nc.alloc_semaphore(name)
        self.base[name] = 0
        self.owner[name] = owner
        return name

    def at(self, name):
        v = self.base[name]
        for label, var in self.loops:
            k = self.counted.get((label, name), 0)
            if k:
                v = var * k + v
        return (name, v)

    def now(self, engine):
        return [self.at(name) for name in self.last[engine]]

    def wait(self, engine, *values):
        for v in values:
            if v is not None and not (isinstance(v[1], int) and v[1] <= 0):
                self.eng[engine].wait_ge(self.sems[v[0]], v[1])

    def up(self, ins, name, n=1):
        ins.then_inc(self.sems[name], n)
        self.base[name] += n
        if self.owner[name]:
            self.last[self.owner[name]] = (name,)
        return self.at(name)

    def settle(self, engine):
        self.eng[engine].sem_inc(self.sems["settled_" + engine], 1)

    def do(self, engine, issue, *args, after=(), also=None, settled=False, **kw):
        self.wait(engine, *after)
        if settled:
            self.settle(engine)
        return self.up(issue(*args, **kw), also or "done_" + engine)

    def fence(self):
        now = {e: self.now(e) for e in self.last}
        for e in now:
            self.wait(e, *[v for o in now for v in now[o]])

    @contextmanager
    def loop(self, n):
        label = self.n_loops
        self.n_loops += 1
        before = dict(self.base)
        if self.loops:
            for e in self.eng:
                self.settle(e)
        for e, names in self.last.items():
            self.last[e] = tuple(dict.fromkeys(names + self.counted.get((label, "last", e), ())))
        with self.nc.Fori(0, n) as var:
            self.loops.append((label, var))
            yield var
            self.loops.pop()
        for e, names in self.last.items():
            self.counted[(label, "last", e)] = names
        for name in self.base:
            k = self.base[name] - before.get(name, 0)
            self.counted[(label, name)] = k
            self.base[name] = before.get(name, 0) + k * n


def build(nc, a, out, slopes, upto=99):
    p = Program(nc, slopes)
    V, S, G, TE, SY = nc.vector, nc.scalar, nc.gpsimd, nc.tensor, nc.sync
    fixed = ExitStack()

    def sb(stack, name, shape, dt=F32):
        return stack.enter_context(nc.sbuf_tensor(name, shape, dt))

    dve = lambda issue, *x, **k: p.do("dve", issue, *x, **k)
    act = lambda *x, **k: p.do("act", S.activation, *x, **k)
    pool = lambda issue, *x, **k: p.do("pool", issue, *x, **k)

    raw = [sb(fixed, f"weights_raw{i}", [P, SLOT]) for i in range(RING)]
    w_hi = [sb(fixed, f"weights_hi{i}", [P, SLOT], F32R) for i in range(2)]
    w_lo = [sb(fixed, f"weights_lo{i}", [P, SLOT], F32R) for i in range(2)]
    h = sb(fixed, "hidden", [P, KD, T])[:, :, :]
    sq = sb(fixed, "squares", [P, KD, T])
    table0 = sb(fixed, "ident_ones", [P, 2 * P])
    ident, ones = table0[:, 0:P], table0[:, P:2 * P]
    par = sb(fixed, "vectors", [P, 6, P])
    cact = sb(fixed, "silu_c", [P, 3 * KD])
    mods = sb(fixed, "modulation", [P, 9 * KD, 2])
    cur = sb(fixed, "modulation_now", [P, 9 * KD])
    stat = [sb(fixed, f"stat{i}", [P, 2 * T]) for i in range(3)]
    small = sb(fixed, "small", [P, 64])
    ret_dec = sb(fixed, "ret_decay", [P, 2 * RET_H])
    alog = sb(fixed, "a_log", [P, 2, DN_H])
    dtb = sb(fixed, "dt_bias", [P, 2, DN_H])

    banks = [nc.alloc_psum_tensor(f"bank{i}", [P, 512], F32) for i in range(8)]
    GB = [[banks[0], banks[1]], [banks[2], banks[3]]]
    AB = banks[4:8]

    arrived = [p.sem(f"weights_arrived{i}") for i in range(RING)]
    slot_read = [p.sem(f"slot_read{i}", "dve") for i in range(RING)]
    used = [p.sem(f"weights_used{i}", "pe") for i in range(2)]
    evac = [p.sem(f"evacuated{i}", "dve") for i in range(2)]
    vecs = p.sem("vectors_arrived")
    st = {"slot": 0, "pair": 0, "set": 0, "staged": []}

    def load(parts):
        s = st["slot"]
        st["slot"] = (s + 1) % RING
        p.wait("sp", p.at(slot_read[s]))
        off = 0
        for ap in parts:
            kc, c = ap.shape[1], ap.shape[2]
            tot = sum(x.shape[2] for x in parts)
            dst = raw[s][:, 0:kc * tot].rearrange("p (k c) -> p k c", k=kc)[:, :, off:off + c]
            p.up(SY.dma_start(dst, ap), arrived[s], 16)
            off += c
        return s, parts[0].shape[1] * off

    def stage(parts):
        s, n = load(parts)
        b = st["pair"]
        st["pair"] = 1 - b
        hi, lo, src = w_hi[b][:, 0:n], w_lo[b][:, 0:n], raw[s][:, 0:n]
        t = act(hi, src, ACT.Copy, after=[p.at(arrived[s]), p.at(used[b])])
        dve(V.tensor_tensor, lo, src, hi.bitcast(F32), ALU.subtract, after=[t], also=slot_read[s])
        st["staged"].append((s, b, parts[0].shape[1]))

    def slab(compute, evacuate, keep_set=False):
        s, b, kc = st["staged"].pop(0)
        i = st["set"]
        p.wait("pe", p.at(slot_read[s]), p.at(evac[i]))
        w = [x[b][:, :].rearrange("p (k c) -> p k c", k=kc) if kc * (SLOT // kc) == SLOT
             else x[b][:, 0:kc * (SLOT // kc)].rearrange("p (k c) -> p k c", k=kc) for x in (w_hi, w_lo)]
        last = compute(w, GB[i], b)
        t = p.up(last, used[b])
        if not keep_set:
            st["set"] = 1 - i
            evacuate(GB[i], t, evac[i])
        return t

    def wview(b, kc, c):
        return [x[b][:, 0:kc * c].rearrange("p (k c) -> p k c", k=kc) for x in (w_hi, w_lo)]

    def passes(out_, l, r, first, last):
        TE.matmul(out_, l[0], r[0], start=first, stop=False)
        TE.matmul(out_, l[0], r[1], start=False, stop=False)
        return TE.matmul(out_, l[1], r[0], start=False, stop=last)

    def feature_major(out_, w, c0, act_, toks, kc=KD, k0=0, first=True, last=True):
        for k in range(kc):
            m = passes(out_, [x[:, k, c0:c0 + P] for x in w], [x[:, k0 + k, toks] for x in act_],
                       first and k == 0, last and k == kc - 1)
        return m

    def token_major(out_, w, c0, c1, act_, tok0, kc=KD):
        for k in range(kc):
            m = passes(out_, [x[:, k, tok0:tok0 + P] for x in act_], [x[:, k, c0:c1] for x in w],
                       k == 0, k == kc - 1)
        return m

    def stream(n, parts, one, m=RING):
        turns = (n - 1) // m
        stage(parts(0))
        if turns >= 2:
            with p.loop(turns) as i:
                for j in range(m):
                    stage(parts(i * m + (j + 1)))
                    one(i * m + j)
            rest = range(turns * m, n)
        else:
            rest = range(n)
        for i in rest:
            if i + 1 < n:
                stage(parts(i + 1))
            one(i)

    def wv(ap):
        return ap.rearrange("(k p) n -> p k n", p=P)

    def cols(v, c0, n):
        return v[:, :, bass.ds(c0, n)]

    def vector_load(dst, src):
        return p.up(G.dma_start(dst, src), vecs, 16)

    rows = sb(fixed, "vector_rows", [P, P])
    groups = [
        [a["c"].rearrange("o (k p) -> (o k) p", p=P), a["c_ctx"].rearrange("(k p) -> k p", p=P),
         a["c_2"].rearrange("o (k p) -> (o k) p", p=P), a["ln_g"].rearrange("l j (k p) -> (l j k) p", p=P),
         a["ln_b"].rearrange("l j (k p) -> (l j k) p", p=P), a["final_norm_2"].rearrange("(k p) -> k p", p=P),
         a["dn_norm_2"]],
        [a["ada_b"].rearrange("l (k p) -> (l k) p", p=P)],
        [a["ada_b_2"][0:1].rearrange("l (k p) -> (l k) p", p=P), a["ln_ffn1_2"].rearrange("l (k p) -> (l k) p", p=P),
         a["ln_mix_2"].rearrange("l (k p) -> (l k) p", p=P), a["ln_ffn2_2"].rearrange("l (k p) -> (l k) p", p=P)],
        [a["ada_b_2"][1:2].rearrange("l (k p) -> (l k) p", p=P)] ,
        [a["conv_w_2"][0].rearrange("j (k p) -> (j k) p", p=P)],
        [a["conv_w_2"][1].rearrange("j (k p) -> (j k) p", p=P)],
    ]
    C_LNG, C_LNB, C_FIN, C_DNN = 24, 56, 88, 96
    vector_load(table0[:, :], a["table0"])
    vector_load(ret_dec[:, :], a["ret_decay"].rearrange("d h -> (d h)").partition_broadcast(P))
    vector_load(alog[:, :, :].rearrange("p l h -> p (l h)"), a["a_log_2"].rearrange("l h -> (l h)").partition_broadcast(P))
    vector_load(dtb[:, :, :].rearrange("p l h -> p (l h)"), a["dt_bias_2"].rearrange("l h -> (l h)").partition_broadcast(P))
    for g, srcs in enumerate(groups):
        r0 = 0
        p.wait("pool", *p.now("pe"))
        for s_ in srcs:
            n = s_.shape[0]
            t = vector_load(rows[r0:r0 + n, :], s_)
            r0 += n
        p.wait("pe", t, *p.now("dve"))
        t = p.do("pe", TE.transpose, AB[0][:, 0:r0], rows[0:r0, :], ident[0:r0, 0:r0])
        dve(V.tensor_copy, par[:, g, 0:r0], AB[0][:, 0:r0], after=[t])
    act(cact[:, :], par[:, 0, 0:3 * KD], ACT.Silu, after=[*p.now("dve")])
    p.fence()

    def ada(w, n_vec, c0, n_chunks, bias):
        wk = w
        def one(n):
            s, _ = load([cols(wk, n * T, T)])
            i = st["set"]
            st["set"] = 1 - i
            ws = raw[s][:, :].rearrange("p (k c) -> p k c", k=KD)
            p.wait("pe", p.at(arrived[s]), p.at(evac[i]))
            for cb in range(2):
                for k in range(KD):
                    rhs = cact[:, c0 + k:c0 + k + (n_vec - 1) * KD + 1:KD]
                    m = TE.matmul(GB[i][0][:, cb * 2:cb * 2 + n_vec], ws[:, k, cb * P:(cb + 1) * P], rhs,
                                  start=k == 0, stop=k == KD - 1)
            t = p.up(m, "done_pe")
            for cb, raised in enumerate((slot_read[s], evac[i])):
                dve(V.tensor_copy, mods[:, bass.ds(n * 2 + cb, 1), 0:n_vec].rearrange("p c v -> p (c v)"),
                    GB[i][0][:, 2 * cb:2 * cb + n_vec], after=[t], also=raised)
        with p.loop(n_chunks // 2 // RING) as i:
            for j in range(RING):
                one(i * RING + j)
        for v in range(n_vec):
            dve(V.tensor_tensor, mods[:, 0:n_chunks, v], mods[:, 0:n_chunks, v], bias, ALU.add,
                after=[*p.now("dve")])

    def column_sums(bank, src, n, width):
        for k in range(n):
            m = TE.matmul(bank, ones, src(k), start=k == 0, stop=k == n - 1)
        return p.up(m, "done_pe")

    def rsqrt(dst, src, scale, eps, after):
        t = dve(V.tensor_scalar, dst, src, scale, eps, ALU.mult, ALU.add, after=after)
        t = act(dst, dst, ACT.Sqrt, after=[t])
        return dve(V.reciprocal, dst, dst, after=[t])

    def bc(x, n):
        return x.unsqueeze(1).broadcast_to([P, n, x.shape[1]])

    def layer_norm(hx, gcol, bcol):
        p.wait("pe", *p.now("dve"))
        t = column_sums(AB[0][:, 0:T], lambda k: hx[:, k, :], KD, T)
        t = dve(V.tensor_scalar, stat[0][:, 0:T], AB[0][:, 0:T], 1.0 / D, None, ALU.mult, after=[t])
        for q in range(2):
            x = hx[:, 4 * q:4 * q + 4, :]
            t = dve(V.tensor_tensor, x, x, bc(stat[0][:, 0:T], 4), ALU.subtract, after=[t])
            t2 = act(sq[:, 4 * q:4 * q + 4, :], x, ACT.Square, after=[t], settled=True)
        p.wait("pe", t2)
        t = column_sums(AB[1][:, 0:T], lambda k: sq[:, k, :], KD, T)
        t = rsqrt(stat[1][:, 0:T], AB[1][:, 0:T], 1.0 / D, LN_EPS, [t])
        for q in range(2):
            x = hx[:, 4 * q:4 * q + 4, :]
            t2 = dve(V.tensor_tensor, x, x, bc(stat[1][:, 0:T], 4), ALU.mult, after=[t])
        for k in range(KD):
            t = dve(V.tensor_scalar, hx[:, k, :], hx[:, k, :], gcol[:, k:k + 1], bcol[:, k:k + 1],
                    ALU.mult, ALU.add, after=[t2])
        return t

    def split_affine(x, scale, shift, hi, lo, tmp, after):
        th = act(hi, x, ACT.Identity, scale=scale, bias=shift, after=after, settled=True)
        t = dve(V.tensor_scalar, tmp, x, scale, shift, ALU.mult, ALU.add, after=after)
        return dve(V.tensor_tensor, lo, tmp, hi.bitcast(F32), ALU.subtract, after=[t, th])

    def split(x, hi, lo, after, settled=False):
        th = act(hi, x, ACT.Copy, after=after, settled=settled)
        return dve(V.tensor_tensor, lo, x, hi.bitcast(F32), ALU.subtract, after=[th])

    def feed_forward(gate_up, w_down, act_, out_one):
        with ExitStack() as f:
            mid = [sb(f, p_ + nm(), [P, KF, T], F32R) for p_ in ("ffn_hi", "ffn_lo")]
            gate = [sb(f, nm(), [P, T]) for _ in range(2)]
            prod = [sb(f, nm(), [P, T]) for _ in range(2)]

            def up_one(i):
                q = st["set"]
                b = st["staged"][0][1]
                w = wview(b, KD, T)

                def compute(_, bank, __):
                    for c in range(2):
                        m = feature_major(bank[0][:, c * T:(c + 1) * T], w, c * P, act_, slice(0, T))
                    return m

                def evacuate(bank, t, raised):
                    t1 = act(gate[q][:, :], bank[0][:, 0:T], ACT.Silu, after=[t])
                    t2 = dve(V.tensor_tensor, prod[q][:, :], gate[q][:, :], bank[0][:, T:2 * T], ALU.mult,
                             after=[t1], also=raised)
                    hi, lo = (x[:, bass.ds(i, 1), :].rearrange("p a t -> p (a t)") for x in mid)
                    split(prod[q][:, :], hi, lo, [t2], settled=True)
                slab(compute, evacuate)
            stream(KF, lambda i: [cols(g_, i * P, P) for g_ in gate_up], up_one)
            HK = KF // 2
            wd = [w_down[:, 0:HK, :], w_down[:, HK:KF, :]]
            p.wait("pe", *p.now("dve"))

            def parts(i, j):
                return [cols(wd[j % 2], i * 2 * P + (j // 2) * P, P)]

            def four(i, nxt):
                for j in range(4):
                    if j < 3:
                        stage(parts(i, j + 1))
                    elif nxt is not None:
                        stage(parts(nxt, 0))
                    w = wview(st["staged"][0][1], HK, P)

                    def compute(_, bank, __):
                        return feature_major(bank[0][:, (j // 2) * T:(j // 2 + 1) * T], w, 0, mid, slice(0, T),
                                             kc=HK, k0=(j % 2) * HK, first=j % 2 == 0, last=j % 2 == 1)

                    def evacuate(bank, t, raised):
                        out_one(i * 2, bank[0][:, 0:T], t, None)
                        out_one(i * 2 + 1, bank[0][:, T:2 * T], t, raised)
                    if j == 3:
                        slab(compute, evacuate)
                    else:
                        slab(compute, None, keep_set=True)
            stage(parts(0, 0))
            with p.loop(KD // 2 - 1) as i:
                four(i, i + 1)
            four(KD // 2 - 1, None)

    names = [0]

    def nm():
        names[0] += 1
        return f"tmp{names[0]}"

    b1 = ExitStack()
    hb = sb(b1, "hidden_both", [P, 2, KD, T])
    t1tab = sb(b1, "table1", [P, 2 * T + 2 * T + GRID])
    cosT, sinT, dist, colwin = t1tab[:, 0:T], t1tab[:, T:2 * T], t1tab[:, 2 * T:4 * T], t1tab[:, 4 * T:4 * T + GRID]
    tab_t = vector_load(t1tab[:, :], a["table1"])

    pad_d = nc.dram_tensor("rpb_padded", [NA_H, 7, 2 * GRID], F32)
    exp_d = nc.dram_tensor("rpb_expanded", [GRID, NA_H * 7, GRID], F32)
    bias_sem = p.sem("bias_tables")
    with ExitStack() as f:
        pad = sb(f, "rpb_rows", [NA_H * 7, 2 * GRID])
        t = pool(G.memset, pad[:, :], 0.0)
        p.wait("pool", t)
        for hh in range(NA_H):
            t = p.up(G.dma_start(pad[hh * 7:hh * 7 + 7, GRID - 16:GRID - 16 + NA_COLS], a["na_rpb"][hh, 4:11, :]),
                     bias_sem, 16)
        p.wait("pool", t)
        t = p.up(G.dma_start(pad_d[:, :, :].rearrange("h j c -> (h j) c"), pad[:, :]), bias_sem, 16)
        p.wait("pool", t)
        with p.loop(GRID) as c:
            p.up(G.dma_start(exp_d[bass.ds(c, 1), :, :].rearrange("o r c -> (o r) c"),
                             pad_d[:, :, bass.ds(GRID - 1 - c, GRID)].rearrange("h j c -> (h j) c")), bias_sem, 16)
        bias_t = p.at(bias_sem)
        tok = sb(f, "tokens", [P, D])
        for half, src in enumerate((a["x"], a["ctx"])):
            for tt in range(2):
                p.wait("pool", *p.now("pe"))
                ti = vector_load(tok[:, :], src[0, tt * P:(tt + 1) * P, :])
                for q in range(2):
                    p.wait("pe", ti, *p.now("dve"))
                    for k in range(4):
                        m = TE.transpose(AB[q][:, k * P:(k + 1) * P], tok[:, (4 * q + k) * P:(4 * q + k + 1) * P], ident)
                    t = p.up(m, "done_pe")
                    dve(V.tensor_copy, hb[:, half, 4 * q:4 * q + 4, tt * P:(tt + 1) * P],
                        AB[q][:, :].rearrange("p (k t) -> p k t", k=4), after=[t])
        p.fence()

    def tail(layer, half, w13, w2):
        hx = sb_half(half)
        gb = lambda c, j: par[:, 0, c + (layer * 2 + j) * KD:c + (layer * 2 + j + 1) * KD]
        t = layer_norm(hx, gb(C_LNG, 0), gb(C_LNB, 0))
        with ExitStack() as f:
            af = [sb(f, nm(), [P, KD, T], F32R) for _ in range(2)]
            tmp = [sb(f, nm(), [P, T]) for _ in range(2)]
            for k in range(KD):
                t = split_affine(hx[:, k, :], cur[:, 4 * KD + k:4 * KD + k + 1], cur[:, 3 * KD + k:3 * KD + k + 1],
                                 af[0][:, k, :], af[1][:, k, :], tmp[k % 2][:, :], [*p.now("dve")])
            p.wait("pe", t)

            def out_one(c, psum, t, raised):
                hc = hx[:, bass.ds(c, 1), :].rearrange("p a t -> p (a t)")
                g_ = small[:, 0:1]
                t0 = dve(V.tensor_copy, g_, cur[:, bass.ds(c + 5 * KD, 1)], after=[*p.now("dve")])
                t0 = dve(V.tensor_scalar, hc, hc, ALPHA, None, ALU.mult)
                dve(V.scalar_tensor_tensor, hc, psum, g_, hc, ALU.mult, ALU.add, after=[t, t0], also=raised)
            w13v = wv(w13)
            feed_forward([w13v[:, :, 0:FF], w13v[:, :, FF:2 * FF]], wv(w2), af, out_one)
        layer_norm(hx, gb(C_LNG, 1), gb(C_LNB, 1))
        p.fence()

    half_var = [None]

    def sb_half(half):
        return hb[:, bass.ds(half, 1), :, :].rearrange("p a k t -> p (a k) t")

    def modulation_of(vec):
        t = dve(V.tensor_copy, cur[:, :], mods[:, :, bass.ds(vec, 1)].rearrange("p c v -> p (c v)"),
                after=[*p.now("dve")])
        for c in (1, 4):
            t = dve(V.tensor_scalar, cur[:, c * KD:(c + 1) * KD], cur[:, c * KD:(c + 1) * KD], 1.0, None, ALU.add,
                    after=[t])
        return t

    t_mod0 = dve(V.memset, mods[:, :, :], 0.0)
    p.wait("dve", t_mod0)

    def both_modulated(am, tmp):
        for half in range(2):
            t = modulation_of(half)
            p.wait("act", t)
            for k in range(KD):
                sl = slice(half * T, (half + 1) * T)
                split_affine(hb[:, half, k, :], cur[:, KD + k:KD + k + 1], cur[:, k:k + 1],
                             am[0][:, k, sl], am[1][:, k, sl], tmp[k % 2][:, :], [t])
            p.fence()

    ada(wv(a["ada_w"][0]), 2, 0, 6 * KD, par[:, 1, 0:6 * KD])
    with ExitStack() as f:
        am = [sb(f, nm(), [P, KD, 2 * T], F32R) for _ in range(2)]
        y = sb(f, "mixer_out", [P, KD, 2 * T])
        tmp = [sb(f, nm(), [P, 2 * T]) for _ in range(2)]
        both_modulated(am, [x[:, 0:T] for x in tmp])
        dve(V.memset, y[:, :, :], 0.0)
        lg = small[:, 8:16]
        t = act(lg, ret_dec[:, :], ACT.Exp, after=[p.at(vecs)])
        dve(V.tensor_scalar, lg, lg, -1.0, None, ALU.mult, after=[t])
        Pm = sb(f, "ret_probs", [P, 4, T])
        Pc = sb(f, "ret_probs_ctx", [P, 2, T])
        Dm = sb(f, "ret_decays", [P, 4, T])
        o = sb(f, "ret_out", [P, 4, 2 * T])
        p.fence()
        wi = wv(a["ret_w_in"])
        with p.loop(RET_H) as hd:
            with ExitStack() as g1:
                q = sb(g1, nm(), [P, 2, 2 * T])
                k_ = sb(g1, nm(), [P, 2, 2 * T])
                v = sb(g1, nm(), [P, 4, RET_DV])
                stage([cols(wi, hd * RET_DK, RET_DK)])
                for which, dst in enumerate((q, k_)):
                    nxt = [cols(wi, hd * RET_DK + D, RET_DK)] if which == 0 else \
                          [cols(wi, hd * RET_DV + 2 * D, T)]
                    stage(nxt)
                    w = wview(st["staged"][0][1], KD, T)

                    def compute(_, bank, __):
                        for c in range(2):
                            m = feature_major(bank[c][:, :], w, c * P, am, slice(0, 2 * T))
                        return m

                    def evacuate(bank, t, raised):
                        for c in range(2):
                            act(dst[:, c, T:2 * T], bank[c][:, T:2 * T], ACT.Copy, after=[t])
                        x1, x2 = bank[0][:, 0:T], bank[1][:, 0:T]
                        A, B = tmp[0], tmp[1]
                        t1 = dve(V.tensor_tensor, A[:, 0:T], x1, cosT, ALU.mult, after=[t, tab_t, *p.now("dve"), *p.now("act")])
                        t1 = dve(V.tensor_tensor, A[:, T:2 * T], x2, sinT, ALU.mult)
                        t1 = dve(V.tensor_tensor, B[:, 0:T], x1, sinT, ALU.mult)
                        t1 = dve(V.tensor_tensor, B[:, T:2 * T], x2, cosT, ALU.mult)
                        dve(V.tensor_tensor, dst[:, 0, 0:T], A[:, 0:T], A[:, T:2 * T], ALU.subtract, after=[t1])
                        dve(V.tensor_tensor, dst[:, 1, 0:T], B[:, 0:T], B[:, T:2 * T], ALU.add,
                            after=[*p.now("act")], also=raised)
                    slab(compute, evacuate)
                for j in range(2):
                    if j == 0:
                        stage([cols(wi, hd * RET_DV + (2 * D + T), T)])
                    else:
                        stage([cols(wi, hd * RET_DV + 4 * D, T)])
                    w = wview(st["staged"][0][1], KD, T)

                    def compute(_, bank, __):
                        for tt in range(4):
                            m = token_major(bank[tt // 2][:, (tt % 2) * T:(tt % 2 + 1) * T], w, 0, T, am, tt * P)
                        return m

                    def evacuate(bank, t, raised):
                        for c in range(2):
                            dve(V.tensor_copy, v[:, 2 * c:2 * c + 2, j * T:(j + 1) * T],
                                bank[c][:, :].rearrange("p (a n) -> p a n", a=2), after=[t],
                                also=raised if c else None)
                    slab(compute, evacuate)
                lf = small[:, 16:17]
                lb = small[:, 17:18]
                t = dve(V.tensor_copy, lf, lg[:, bass.ds(hd, 1)], after=[*p.now("dve")])
                t = dve(V.tensor_scalar, lb, lg[:, bass.ds(hd + RET_H, 1)], -1.0, None, ALU.mult)
                A, B = tmp[0][:, :], tmp[1][:, :]
                d2 = dist
                self_ = Dm[:, 0:2, :].rearrange("p a t -> p (a t)")
                cross = Dm[:, 2:4, :].rearrange("p a t -> p (a t)")
                t = dve(V.tensor_scalar, A, d2, -float(T), 0.0, ALU.add, ALU.max, after=[t])
                ta = act(A, A, ACT.Exp, scale=lf, after=[t])
                t = dve(V.tensor_scalar, B, d2, -float(T), 0.0, ALU.add, ALU.min)
                tb = act(B, B, ACT.Exp, scale=lb, after=[t])
                t = dve(V.scalar_tensor_tensor, A, d2, float(T), A, ALU.is_ge, ALU.mult, after=[ta])
                t = dve(V.scalar_tensor_tensor, B, d2, float(T), B, ALU.is_le, ALU.mult, after=[tb])
                t = dve(V.tensor_tensor, self_, A, B, ALU.add, after=[t])
                ta = act(A, d2, ACT.Exp, scale=lf, after=[t])
                t = dve(V.tensor_scalar, B, d2, -2.0 * T, None, ALU.add, after=[t])
                tb = act(B, B, ACT.Exp, scale=lb, after=[t])
                t = dve(V.tensor_tensor, cross, A, B, ALU.add, after=[ta, tb])
                p.wait("pe", *p.now("dve"), *p.now("act"))
                for i in range(4):
                    for c in range(2):
                        m = TE.matmul(AB[i // 2][:, (i % 2) * T:(i % 2 + 1) * T], k_[:, c, i * P:(i + 1) * P],
                                      q[:, c, 0:T], start=c == 0, stop=c == 1)
                for i in range(2):
                    for c in range(2):
                        m = TE.matmul(AB[2][:, i * T:(i + 1) * T], k_[:, c, T + i * P:T + (i + 1) * P],
                                      q[:, c, T:2 * T], start=c == 0, stop=c == 1)
                t = p.up(m, "done_pe")
                fl = lambda x: x.rearrange("p a t -> p (a t)")
                for i in range(2):
                    dve(V.scalar_tensor_tensor, fl(Pm[:, 2 * i:2 * i + 2, :]), AB[i][:, :], RET_DK ** -0.5,
                        fl(Dm[:, 2 * i:2 * i + 2, :]), ALU.mult, ALU.mult, after=[t])
                t = dve(V.scalar_tensor_tensor, fl(Pc[:, :, :]), AB[2][:, :], RET_DK ** -0.5, self_,
                        ALU.mult, ALU.mult)
                p.wait("pe", t)
                for c in range(4):
                    for i in range(4):
                        TE.matmul(AB[c][:, 0:T], v[:, i, c * P:(c + 1) * P], Pm[:, i, :], start=i == 0, stop=i == 3)
                    for i in range(2):
                        m = TE.matmul(AB[c][:, T:2 * T], v[:, 2 + i, c * P:(c + 1) * P], Pc[:, i, :],
                                      start=i == 0, stop=i == 1)
                    t = p.up(m, "done_pe")
                    t1 = dve(V.tensor_copy, o[:, c, :], AB[c][:, :], after=[t])
                    t2 = act(sq[:, 2 * c:2 * c + 2, :].rearrange("p a t -> p (a t)"), o[:, c, :], ACT.Square, after=[t1])
                p.wait("pe", t2)
                t = column_sums(AB[0][:, :], lambda k: sq[:, 2 * k:2 * k + 2, :].rearrange("p a t -> p (a t)"), 4, 512)
                t = rsqrt(stat[0][:, :], AB[0][:, :], 1.0 / RET_DV, RMS_EPS, [t])
                t = dve(V.tensor_tensor, o[:, :, :], o[:, :, :], bc(stat[0][:, :], 4), ALU.mult, after=[t])
            with ExitStack() as g2:
                z = [sb(g2, nm(), [P, 4, 2 * T], F32R) for _ in range(2)]
                wo = a["ret_w_out"].rearrange("(g k p) n -> g p k n", p=P, k=4)
                wo_h = wo[bass.ds(hd, 1), :, :, :].rearrange("g p k n -> p (g k) n")
                for j in range(2):
                    stage([cols(wi, hd * RET_DV + (4 * D + T), T)] if j == 0 else [cols(wo_h, 0, T)])
                    w = wview(st["staged"][0][1], KD, T)

                    def compute(_, bank, __):
                        for c in range(2):
                            m = feature_major(bank[c][:, :], w, c * P, am, slice(0, 2 * T))
                        return m

                    def evacuate(bank, t, raised):
                        for c in range(2):
                            A = tmp[c][:, :]
                            n = 2 * j + c
                            t1 = act(A, bank[c][:, :], ACT.Silu, after=[t, *p.now("dve")])
                            t1 = dve(V.tensor_tensor, A, A, o[:, n, :], ALU.mult, after=[t1],
                                     also=raised if c else None)
                            split(A, z[0][:, n, :], z[1][:, n, :], [t1])
                    slab(compute, evacuate)
                for j in range(4):
                    if j < 3:
                        stage([cols(wo_h, (j + 1) * T, T)])
                    w = wview(st["staged"][0][1], 4, T)
                    p.wait("pe", *p.now("dve")) if j == 0 else None

                    def compute(_, bank, __):
                        for c in range(2):
                            m = feature_major(bank[c][:, :], w, c * P, z, slice(0, 2 * T), kc=4)
                        return m

                    def evacuate(bank, t, raised):
                        for c in range(2):
                            yc = y[:, 2 * j + c, :]
                            dve(V.tensor_tensor, yc, yc, bank[c][:, :], ALU.add, after=[t],
                                also=raised if c else None)
                    slab(compute, evacuate)
            p.fence()
        for half in range(2):
            hx = hb[:, half, :, :]
            t = dve(V.tensor_scalar, hx, hx, ALPHA, None, ALU.mult, after=[*p.now("dve")])
            for k in range(KD):
                dve(V.scalar_tensor_tensor, hx[:, k, :], y[:, k, half * T:(half + 1) * T],
                    mods[:, 2 * KD + k, half:half + 1], hx[:, k, :], ALU.mult, ALU.add, after=[t])
        p.fence()

    def dump(src):
        with ExitStack() as f:
            rows_out = [sb(f, nm(), [P, D]) for _ in range(2)]
            for tt in range(2):
                for q in range(2):
                    p.wait("pe", *p.now("dve"))
                    for k in range(4):
                        m = TE.transpose(AB[2 * tt + q][:, k * P:(k + 1) * P], src[:, 4 * q + k, tt * P:(tt + 1) * P], ident)
                    t = p.up(m, "done_pe")
                    t = dve(V.tensor_copy, rows_out[tt][:, q * 512:(q + 1) * 512], AB[2 * tt + q][:, :], after=[t])
                p.wait("sp", t)
                p.up(SY.dma_start(out[0, tt * P:(tt + 1) * P, :], rows_out[tt][:, :]), stored, 16)
            p.wait("sp", p.at(stored))
            p.wait("pool", p.at(bias_sem))
    stored = p.sem("stored")

    if upto == 1:
        dump(hb[:, 0, :, :]); return
    with p.loop(2) as half:
        modulation_of(half)
        tail(0, half, a["ffn_w13"][0], a["ffn_w2"][0])
    if upto == 2:
        dump(hb[:, 0, :, :]); return

    ada(wv(a["ada_w"][1]), 2, 0, 6 * KD, par[:, 1, 6 * KD:12 * KD])
    with ExitStack() as f:
        am = [sb(f, nm(), [P, KD, 2 * T], F32R) for _ in range(2)]
        tmp = [sb(f, nm(), [P, T]) for _ in range(2)]
        both_modulated(am, [x[:, :] for x in tmp])
        oc = [sb(f, nm(), [P, KD, T], F32R) for _ in range(2)]
        q = sb(f, nm(), [P, T])
        k_ = sb(f, nm(), [P, 2 * T])
        v = sb(f, nm(), [P, 4, P])
        U = sb(f, "na_bias", [P, 2, 6, GRID])
        pr = [sb(f, nm(), [P, 2 * T]) for _ in range(4)]
        PT = sb(f, "na_probs_t", [P, 2, 4, T])
        ob = sb(f, nm(), [P, T])
        u_sem = p.sem("na_bias_arrived")
        p.wait("pool", bias_t)
        ex = exp_d[:, :, :].rearrange("c (g e j) k -> g c e j k", g=NA_H // 2, e=2)
        wq = wv(a["na_w_qkv"])
        with p.loop(NA_H // 2) as hp:
            for half in range(2):
                for e in range(2):
                    src = ex[bass.ds(hp, 1), :, e, 1 - half:7 - half, :].rearrange("g c j k -> c (g j) k")
                    p.up(G.dma_start(U[half * GRID:(half + 1) * GRID, e, :, :], src), u_sem, 16)
            tu = pool(G.tensor_tensor, out=U[:, :, :, :].rearrange("p e j k -> p (e j) k"),
                      in0=U[:, :, :, :].rearrange("p e j k -> p (e j) k"), in1=bc(colwin, 12), op=ALU.add,
                      after=[p.at(u_sem), tab_t])
            stage([cols(wq, hp * P, P), cols(wq, hp * P + D, P)])
            stage([cols(wq, hp * P + 2 * D, P)])
            w = wview(st["staged"][0][1], KD, T)

            def compute(_, bank, __):
                feature_major(bank[0][:, 0:T], w, 0, am, slice(0, T))
                return feature_major(bank[1][:, :], w, P, am, slice(0, 2 * T))

            def evacuate(bank, t, raised):
                t1 = act(k_[:, :], bank[1][:, :], ACT.Copy, after=[t])
                dve(V.tensor_scalar, q[:, :], bank[0][:, 0:T], (D // NA_H) ** -0.5, None, ALU.mult, after=[t, t1],
                    also=raised)
            slab(compute, evacuate)
            w2_ = wview(st["staged"][0][1], KD, P)

            def compute(_, bank, __):
                for tt in range(4):
                    m = token_major(bank[0][:, tt * P:(tt + 1) * P], w2_, 0, P, am, tt * P)
                return m

            def evacuate(bank, t, raised):
                dve(V.tensor_copy, v[:, :, :].rearrange("p a n -> p (a n)"), bank[0][:, :], after=[t], also=raised)
            slab(compute, evacuate)
            p.wait("pe", *p.now("dve"), *p.now("act"), tu)
            tS = []
            for e in range(2):
                r_ = slice(e * GRID, e * GRID + GRID)
                for tt in range(2):
                    bank = AB[2 * e + tt]
                    TE.matmul(bank[:, :], q[r_, tt * P:(tt + 1) * P], k_[r_, :], start=True, stop=False)
                    jj = 2 - 2 * tt
                    m = TE.matmul(bank[:, 0:T], ident, U[:, e, jj:jj + 4, :].rearrange("p j k -> p (j k)"),
                                  start=False, stop=True)
                    tS.append(p.up(m, "done_pe"))
            for i in range(4):
                bank, nmx, sm = AB[i], small[:, 20 + i:21 + i], small[:, 24 + i:25 + i]
                t = dve(V.tensor_reduce, nmx, bank[:, :], axis=AX.X, op=ALU.max, negate=True, after=[tS[i]])
                t = act(pr[i][:, :], bank[:, :], ACT.Exp, bias=nmx, accum_out=sm, after=[t])
                t = dve(V.reciprocal, sm, sm, after=[t])
                t = dve(V.tensor_scalar, pr[i][:, :], pr[i][:, :], sm, None, ALU.mult, after=[t])
                p.wait("pe", t)
                for s_ in range(4):
                    m = TE.transpose(bank[:, s_ * P:(s_ + 1) * P], pr[i][:, s_ * P:(s_ + 1) * P], ident)
                t = p.up(m, "done_pe")
                e, tt = i // 2, i % 2
                dve(V.tensor_copy, PT[:, e, :, tt * P:(tt + 1) * P], bank[:, :].rearrange("p (s t) -> p s t", s=4),
                    after=[t])
            p.wait("pe", *p.now("dve"))
            for e in range(2):
                r_ = slice(e * GRID, e * GRID + GRID)
                for s_ in range(4):
                    m = TE.matmul(AB[0][r_, 0:T], v[:, s_, r_], PT[:, e, s_, :], start=s_ == 0, stop=s_ == 3)
            t = p.up(m, "done_pe")
            t = dve(V.tensor_copy, ob[:, :], AB[0][:, 0:T], after=[t])
            hi, lo = (x[:, bass.ds(hp, 1), :].rearrange("p a t -> p (a t)") for x in oc)
            split(ob[:, :], hi, lo, [t], settled=True)
            p.fence()
        hx = hb[:, 0, :, :]
        modulation_of(0)
        dve(V.tensor_scalar, hx, hx, ALPHA, None, ALU.mult, after=[*p.now("dve")])
        p.wait("dve", *p.now("dve"))
        p.wait("pe", *p.now("dve"))
        def residual(src, wvw, kc, hx, gate_cols, scale=None):
            def one(i):
                w = wview(st["staged"][0][1], kc, T)

                def compute(_, bank, __):
                    for c in range(2):
                        m = feature_major(bank[0][:, c * T:(c + 1) * T], w, c * P, src, slice(0, T), kc=kc)
                    return m

                def evacuate(bank, t, raised):
                    for c in range(2):
                        n = i * 2 + c
                        dve(V.scalar_tensor_tensor, hx[:, n, :], bank[0][:, c * T:(c + 1) * T],
                            gate_cols[:, n:n + 1], hx[:, n, :], ALU.mult, ALU.add, after=[t],
                            also=raised if c else None)
                slab(compute, evacuate)
            stream(4, lambda i: [cols(wvw, i * T, T)], one)
        residual(oc, wv(a["na_w_out"]), KD, hx, cur[:, 2 * KD:3 * KD])
        p.fence()
    if upto == 3:
        dump(hb[:, 0, :, :]); return
    tail(1, 0, a["ffn_w13"][1], a["ffn_w2"][1])
    dve(V.tensor_copy, h[:, :, :], hb[:, 0, :, :], after=[*p.now("dve")])
    p.fence()
    b1.close()
    if upto == 4:
        dump(h); return

    b2 = ExitStack()
    NT2 = TRI * 2 + P + T + TRI * 2 + NLEV * P + DA_H
    t2tab = sb(b2, "table2", [P, NT2])
    tab2 = vector_load(t2tab[:, :], a["table2"])
    off = [0]

    def take(n):
        x = t2tab[:, off[0]:off[0] + n]
        off[0] += n
        return x
    da_dist, da_lnc, gt_m, le_m, incl, strict = (take(n) for n in (TRI, TRI, P, T, TRI, TRI))
    lev = [take(P) for _ in range(NLEV)]
    slope = take(DA_H)
    for e in ("dve", "act", "pool", "pe"):
        p.wait(e, tab2)
    adab = sb(b2, "ada_bias", [P, 2, 9 * KD])
    lng = sb(b2, "norm_gains", [P, 2, 3, KD])
    convw = sb(b2, "conv_taps", [P, 2, 4, 3, DN_H])
    for l in range(2):
        dve(V.tensor_copy, adab[:, l, :], par[:, 2 + l, 0:9 * KD])
        dve(V.tensor_copy, lng[:, l, :, :], par[:, 2, 9 * KD:15 * KD].rearrange("p (j l k) -> p l j k", j=3, l=2)[:, l])
        dve(V.tensor_copy, convw[:, l, :, :, :].rearrange("p j x h -> p (j x h)"), par[:, 4 + l, 0:96])
    dnn = par[:, 0, C_DNN:C_DNN + 2]
    gl = sb(b2, "gains_now", [P, 3, KD])
    bias_now = sb(b2, "ada_bias_now", [P, 9 * KD])
    dnn_now = sb(b2, "dn_norm_now", [P, 1])
    cw_l = sb(b2, "conv_now", [P, 4, 3, DN_H])
    p.fence()

    def rms_scale(hx, dst):
        for q in range(2):
            t = act(sq[:, 4 * q:4 * q + 4, :], hx[:, 4 * q:4 * q + 4, :], ACT.Square, after=[*p.now("dve")])
        p.wait("pe", t)
        t = column_sums(AB[0][:, 0:T], lambda k: sq[:, k, :], KD, T)
        return rsqrt(dst, AB[0][:, 0:T], 1.0 / D, RMS_EPS, [t])

    def normed(hx, j, am, tmp):
        t = rms_scale(hx, stat[0][:, 0:T])
        t = dve(V.tensor_tensor, sq[:, :, :], hx, bc(stat[0][:, 0:T], KD), ALU.mult, after=[t, *p.now("pe")])
        for k in range(KD):
            sh, sc = cur[:, 3 * j * KD + k:3 * j * KD + k + 1], cur[:, (3 * j + 1) * KD + k:(3 * j + 1) * KD + k + 1]
            split_affine(sq[:, k, :], sc, sh, am[0][:, k, :], am[1][:, k, :], tmp[k % 2][:, :], [t])
        p.wait("pe", *p.now("dve"))

    def lv(ap, l, pat="l (k p) n -> l p k n"):
        return ap.rearrange(pat, p=P)[bass.ds(l, 1)].rearrange("l p k n -> p (l k) n")

    def macaron(l, j, wg, wu, wd):
        with ExitStack() as f:
            am = [sb(f, nm(), [P, KD, T], F32R) for _ in range(2)]
            tmp = [sb(f, nm(), [P, T]) for _ in range(2)]
            normed(h, j, am, tmp)

            def out_one(c, psum, t, raised):
                hc = h[:, bass.ds(c, 1), :].rearrange("p a t -> p (a t)")
                g_ = small[:, 0:1]
                t0 = dve(V.tensor_copy, g_, cur[:, bass.ds(c + (3 * j + 2) * KD, 1)], after=[*p.now("dve")])
                dve(V.scalar_tensor_tensor, hc, psum, g_, hc, ALU.mult, ALU.add, after=[t, t0], also=raised)
            feed_forward([lv(wg, l), lv(wu, l)], lv(wd, l), am, out_one)
            p.fence()

    def mixer(l):
        with ExitStack() as f:
            u = [sb(f, nm(), [P, KD, T], F32R) for _ in range(2)]
            tmp = [sb(f, nm(), [P, T]) for _ in range(2)]
            ya = sb(f, "branch_a", [P, KD, T])
            zo = sb(f, "dn_gate_out", [P, DN_H, T])
            beta = sb(f, "beta", [P, 2, DN_H])
            gdec = sb(f, "log_decay", [P, 2, DN_H])
            rk = sb(f, "key_scale", [P, 2, 2, DN_H])
            rqb = sb(f, "query_scale_beta", [P, 2, 2, DN_H])
            normed(h, 1, u, tmp)
            wi = lv(a["w_in_2"], l)
            stage([cols(wi, IN_BA, 2 * DN_H)])
            wba = wview(st["staged"][0][1], KD, 2 * DN_H)
            ba = sb(f, "beta_decay_in", [P, 2, 2 * DN_H])

            def compute(_, bank, __):
                for tt in range(2):
                    m = token_major(bank[0][:, tt * 16:(tt + 1) * 16], wba, 0, 16, u, tt * P)
                return m

            def evacuate(bank, t, raised):
                dve(V.tensor_copy, ba[:, :, :].rearrange("p a n -> p (a n)"), bank[0][:, 0:32], after=[t], also=raised)
            slab(compute, evacuate)
            act(beta[:, :, :], ba[:, :, 0:DN_H], ACT.Sigmoid, after=[*p.now("dve")])
            s0, s1, s2, s3, s4 = (small[:, 0:16], small[:, 16:32], small[:, 32:48], small[:, 48:64], stat[1][:, 0:16])
            r3 = lambda x: x.rearrange("p (a n) -> p a n", a=2)
            t = dve(V.tensor_tensor, r3(s0), ba[:, :, DN_H:2 * DN_H],
                    dtb[:, bass.ds(l, 1), :].broadcast_to([P, 2, DN_H]), ALU.add, after=[*p.now("dve")])
            chain = lambda op, *x, **k_: dve(op, *x, after=[*p.now("dve"), *p.now("act")], **k_)
            t = act(s1, s0, ACT.Abs, after=[*p.now("dve")])
            act(s1, s1, ACT.Exp, scale=-1.0, after=[t])
            chain(V.tensor_scalar, s2, s1, 2.0, None, ALU.add)
            chain(V.reciprocal, s2, s2)
            chain(V.tensor_tensor, s2, s2, s1, ALU.mult)
            chain(V.tensor_tensor, s3, s2, s2, ALU.mult)
            chain(V.tensor_scalar, s4, s3, 1.0 / 15, None, ALU.mult)
            for n in (13, 11, 9, 7, 5, 3):
                chain(V.scalar_tensor_tensor, s4, s4, 1.0 / n, s3, ALU.add, ALU.mult)
            chain(V.scalar_tensor_tensor, s4, s4, 1.0, s2, ALU.add, ALU.mult)
            chain(V.tensor_scalar, s0, s0, 0.0, None, ALU.max)
            chain(V.scalar_tensor_tensor, s4, s4, 2.0, s0, ALU.mult, ALU.add)
            act(s1[:, 0:DN_H], alog[:, bass.ds(l, 1), :].rearrange("p a n -> p (a n)"), ACT.Exp, after=[*p.now("dve")], settled=True)
            chain(V.scalar_tensor_tensor, gdec[:, :, :], r3(s4), -1.0, bc(s1[:, 0:DN_H], 2), ALU.mult, ALU.mult)
            p.fence()

            with ExitStack() as f2:
                vb = sb(f2, "dn_v_beta", [P, DN_H, 2, P])
                MT = sb(f2, "dn_m_t", [P, DN_H, TRI])
                Aqk = sb(f2, "dn_qk", [P, DN_H, TRI])
                with ExitStack() as f3:
                    qa = sb(f3, "dn_q", [P, DN_H, T])
                    ka = sb(f3, "dn_k", [P, DN_H, T])
                    with ExitStack() as f4:
                        cin = sb(f4, "conv_in", [P, 3, T + 3])
                        cy = sb(f4, "conv_out", [P, 3, T])
                        vf = sb(f4, "dn_v", [P, T])
                        cw = sb(f4, "taps", [P, 4, 3])
                        dve(V.memset, cin[:, :, 0:3], 0.0)
                        p.fence()
                        with p.loop(DN_H) as hd:
                            stage([cols(wi, hd * P, P), cols(wi, hd * P + D, P)])
                            stage([cols(wi, hd * P + 2 * D, P), cols(wi, hd * P + IN_Z, P)])
                            dve(V.tensor_copy, cw[:, :, :], cw_l[:, :, :, bass.ds(hd, 1)].rearrange("p j x h -> p j (x h)"))
                            for j in range(2):
                                w = wview(st["staged"][0][1], KD, T)

                                def compute(_, bank, __):
                                    for c in range(2):
                                        m = feature_major(bank[0][:, c * T:(c + 1) * T], w, c * P, u, slice(0, T))
                                    return m

                                def evacuate(bank, t, raised):
                                    if j == 0:
                                        dve(V.tensor_copy, cin[:, 0:2, 3:], bank[0][:, :].rearrange("p (a t) -> p a t", a=2),
                                            after=[t], also=raised)
                                    else:
                                        t1 = act(zo[:, bass.ds(hd, 1), :].rearrange("p a t -> p (a t)"),
                                                 bank[0][:, T:2 * T], ACT.Silu, after=[t], settled=True)
                                        dve(V.tensor_copy, cin[:, 2, 3:], bank[0][:, 0:T], after=[t, t1], also=raised)
                                slab(compute, evacuate)
                                for x in ((0, 1) if j == 0 else (2,)):
                                    t = dve(V.tensor_scalar, cy[:, x, :], cin[:, x, 0:T], cw[:, 0, x:x + 1], None, ALU.mult,
                                            after=[*p.now("dve")])
                                    for jj in range(1, 4):
                                        t = dve(V.scalar_tensor_tensor, cy[:, x, :], cin[:, x, jj:jj + T],
                                                cw[:, jj, x:x + 1], cy[:, x, :], ALU.mult, ALU.add, after=[t])
                            act(qa[:, bass.ds(hd, 1), :].rearrange("p a t -> p (a t)"), cy[:, 0, :], ACT.Silu, after=[t], settled=True)
                            act(ka[:, bass.ds(hd, 1), :].rearrange("p a t -> p (a t)"), cy[:, 1, :], ACT.Silu)
                            t = act(vf[:, :], cy[:, 2, :], ACT.Silu)
                            p.wait("pe", t)
                            for tt in range(2):
                                m = TE.transpose(AB[0][:, tt * P:(tt + 1) * P], vf[:, tt * P:(tt + 1) * P], ident)
                            t = p.up(m, "done_pe")
                            t = dve(V.tensor_copy, vb[:, bass.ds(hd, 1), :, :].rearrange("p a b n -> p (a b) n"),
                                    AB[0][:, 0:T].rearrange("p (a n) -> p a n", a=2), after=[t])
                            p.fence()
                    for tt in range(2):
                        x = vb[:, :, tt, :]
                        t = dve(V.tensor_tensor, x, x, beta[:, tt, :].unsqueeze(2).broadcast_to([P, DN_H, P]), ALU.mult)
                    for n, src in enumerate((qa, ka)):
                        t = act(sq[:, :, :], src[:, :, :], ACT.Square, after=[*p.now("pe")])
                        p.wait("pe", t)
                        for tt in range(2):
                            for hh in range(DN_H):
                                c = (n * 2 + tt) * DN_H + hh
                                m = TE.matmul(AB[0][:, c:c + 1], sq[:, hh, tt * P:(tt + 1) * P], ones[:, 0:1],
                                              start=True, stop=True)
                        t = p.up(m, "done_pe")
                    fl4 = lambda x: x.rearrange("p a b n -> p (a b n)")
                    t = rsqrt(fl4(rk[:, :, :, :]), AB[0][:, 0:4 * DN_H], 1.0, RMS_EPS, [t])
                    dve(V.tensor_scalar, rqb[:, 0, :, :], rk[:, 0, :, :], P ** -0.5, None, ALU.mult, after=[t])
                    dve(V.tensor_tensor, rqb[:, 1, :, :], rk[:, 1, :, :], beta[:, :, :], ALU.mult, after=[t])
                    p.fence()
                    with ExitStack() as f4:
                        G0 = sb(f4, "decay_steps", [P, TRI])
                        E = sb(f4, "decay_exp", [P, TRI])
                        Eb = [sb(f4, nm(), [P, TRI]) for _ in range(2)]
                        sc = sb(f4, "head_scalars", [P, 2, 4])
                        qh = sb(f4, nm(), [P, 2, T])
                        with p.loop(DN_H) as hd:
                            one_h = bass.ds(hd, 1)
                            dve(V.tensor_copy, sc[:, :, 0:1], gdec[:, :, one_h])
                            dve(V.tensor_copy, sc[:, :, 1:2], rk[:, 1, :, one_h])
                            dve(V.tensor_copy, sc[:, :, 2:3], rqb[:, 0, :, one_h])
                            t = dve(V.tensor_copy, sc[:, :, 3:4], rqb[:, 1, :, one_h])
                            act(qh[:, 0, :], qa[:, one_h, :].rearrange("p a t -> p (a t)"), ACT.Copy, settled=True)
                            act(qh[:, 1, :], ka[:, one_h, :].rearrange("p a t -> p (a t)"), ACT.Copy)
                            dve(V.tensor_scalar, G0[:, 0:T], le_m, sc[:, 0, 0:1], None, ALU.mult, after=[t])
                            t = dve(V.tensor_scalar, G0[:, T:TRI], le_m[:, 0:P], sc[:, 1, 0:1], None, ALU.mult)
                            p.wait("pe", t)
                            TE.matmul(AB[0][:, 0:T], gt_m, G0[:, 0:T], start=True, stop=False)
                            TE.matmul(AB[0][:, P:T], ones, G0[:, T:TRI], start=False, stop=True)
                            m = TE.matmul(AB[0][:, T:TRI], gt_m, G0[:, T:TRI], start=True, stop=True)
                            tD = p.up(m, "done_pe")
                            for n in range(2):
                                for tt in range(2):
                                    m = TE.matmul(AB[1][:, (2 * n + tt) * P:(2 * n + tt + 1) * P],
                                                  sc[:, tt, 2 + n:3 + n].broadcast_to([P, P]), ident, start=True, stop=True)
                            p.wait("pe", *p.now("act"))
                            kk = qh[:, 1, :]
                            for n, bank in ((0, AB[2]), (1, AB[3])):
                                TE.matmul(bank[:, 0:T], kk[:, 0:P], qh[:, n, :], start=True, stop=True)
                                m = TE.matmul(bank[:, T:TRI], kk[:, P:T], qh[:, n, P:T], start=True, stop=True)
                            tK = p.up(m, "done_pe")
                            t = act(E[:, :], AB[0][:, 0:TRI], ACT.Exp, after=[tD])
                            for n, mask in ((0, incl), (1, strict)):
                                dst = Aqk if n == 0 else MT
                                t1 = pool(G.tensor_tensor, out=Eb[n][:, :], in0=E[:, :], in1=mask, op=ALU.mult, after=[t])
                                fac = AB[1][:, n * T:(n + 1) * T]
                                t2 = dve(V.tensor_tensor, Eb[n][:, 0:T], Eb[n][:, 0:T], fac, ALU.mult, after=[t1, tK])
                                t2 = dve(V.tensor_tensor, Eb[n][:, T:TRI], Eb[n][:, T:TRI], fac[:, P:T], ALU.mult)
                                for tt, s_ in ((0, slice(0, T)), (1, slice(T, TRI))):
                                    dve(V.scalar_tensor_tensor, dst[:, one_h, s_].rearrange("p a t -> p (a t)"),
                                        AB[2 + n][:, s_], sc[:, tt, 1:2], Eb[n][:, s_], ALU.mult, ALU.mult, after=[t2])
                            p.fence()
                with ExitStack() as f3:
                    X = sb(f3, "inv", [P, 2, DN_H, P])
                    XT = sb(f3, "inv_t", [P, 2, DN_H, P])
                    ML = [sb(f3, nm(), [P, 4, P]) for _ in range(2)]
                    Y = [sb(f3, nm(), [P, 4, P]) for _ in range(2)]
                    fl = lambda x: x.rearrange("p a t -> p (a t)")

                    def mt(tt, hh):
                        return MT[:, hh, 0:P] if tt == 0 else MT[:, hh, T:TRI]
                    for gi in range(4):
                        tt, h0 = gi // 2, (gi % 2) * 4
                        m4 = MT[:, h0:h0 + 4, 0:P] if tt == 0 else MT[:, h0:h0 + 4, T:TRI]
                        xt = XT[:, tt, h0:h0 + 4, :]
                        t = dve(V.tensor_tensor, xt, m4, bc(lev[0], 4), ALU.mult)
                        t = dve(V.tensor_tensor, xt, bc(ident, 4), xt, ALU.subtract, after=[t])
                        p.wait("pe", t)
                        for i in range(4):
                            m = TE.transpose(AB[gi][:, i * P:(i + 1) * P], XT[:, tt, h0 + i, :], ident)
                        t = p.up(m, "done_pe")
                        act(fl(X[:, tt, h0:h0 + 4, :]), AB[gi][:, :], ACT.Copy, after=[t])
                    p.fence()
                    for j in range(1, NLEV):
                        for gi in range(4):
                            tt, h0 = gi // 2, (gi % 2) * 4
                            b = gi % 2
                            m4 = MT[:, h0:h0 + 4, 0:P] if tt == 0 else MT[:, h0:h0 + 4, T:TRI]
                            x4, xt4 = fl(X[:, tt, h0:h0 + 4, :]), fl(XT[:, tt, h0:h0 + 4, :])
                            bk = [AB[0], AB[1], banks[0]] if b == 0 else [AB[2], AB[3], banks[2]]
                            t = pool(G.tensor_tensor, out=ML[b][:, :, :], in0=m4, in1=bc(lev[j], 4), op=ALU.mult,
                                     after=[*p.now("pe")])
                            p.wait("pe", t, *p.now("dve"))
                            for i in range(4):
                                m = TE.matmul(bk[0][:, i * P:(i + 1) * P], ML[b][:, i, :], X[:, tt, h0 + i, :],
                                              start=True, stop=True)
                            t = p.up(m, "done_pe")
                            t = act(fl(Y[b][:, :, :]), bk[0][:, :], ACT.Copy, after=[t])
                            p.wait("pe", t)
                            for i in range(4):
                                m = TE.matmul(bk[1][:, i * P:(i + 1) * P], XT[:, tt, h0 + i, :], Y[b][:, i, :],
                                              start=True, stop=True)
                            t1 = p.up(m, "done_pe")
                            for i in range(4):
                                m = TE.matmul(bk[2][:, i * P:(i + 1) * P], Y[b][:, i, :], XT[:, tt, h0 + i, :],
                                              start=True, stop=True)
                            t2 = p.up(m, "done_pe")
                            dve(V.tensor_tensor, x4, x4, bk[1][:, :], ALU.subtract, after=[t2])
                            dve(V.tensor_tensor, xt4, xt4, bk[2][:, :], ALU.subtract, after=[t2])
                        p.fence()
                    vn = [sb(f3, nm(), [P, 4, P]) for _ in range(2)]
                    for gi in range(2):
                        h0 = 4 * gi
                        for i in range(4):
                            m = TE.matmul(AB[0][:, i * P:(i + 1) * P], XT[:, 0, h0 + i, :], vb[:, h0 + i, 0, :],
                                          start=True, stop=True)
                        t = p.up(m, "done_pe")
                        t = act(fl(vn[0][:, :, :]), AB[0][:, :], ACT.Copy, after=[t])
                        p.wait("pe", t)
                        for i in range(4):
                            m = TE.matmul(AB[1][:, i * P:(i + 1) * P], MT[:, h0 + i, P:T], vn[0][:, i, :],
                                          start=True, stop=True)
                        t = p.up(m, "done_pe")
                        x = vb[:, h0:h0 + 4, 1, :]
                        t = dve(V.tensor_tensor, x, x, AB[1][:, :].rearrange("p (a n) -> p a n", a=4), ALU.subtract, after=[t])
                        p.wait("pe", t)
                        for i in range(4):
                            m = TE.matmul(AB[0][:, i * P:(i + 1) * P], XT[:, 1, h0 + i, :], vb[:, h0 + i, 1, :],
                                          start=True, stop=True)
                        t = p.up(m, "done_pe")
                        t = act(fl(vn[1][:, :, :]), AB[0][:, :], ACT.Copy, after=[t])
                        p.wait("pe", t)
                        for i in range(4):
                            bank = AB[2 + i // 2][:, (i % 2) * T:(i % 2 + 1) * T]
                            TE.matmul(bank, vn[0][:, i, :], Aqk[:, h0 + i, 0:T], start=True, stop=False)
                            m = TE.matmul(bank[:, P:T], vn[1][:, i, :], Aqk[:, h0 + i, T:TRI], start=False, stop=True)
                        t = p.up(m, "done_pe")
                        for i in range(2):
                            s2_ = sq[:, 2 * i:2 * i + 2, :].rearrange("p a t -> p (a t)")
                            t1 = act(s2_, AB[2 + i][:, :], ACT.Square, after=[t])
                            p.wait("pe", t1)
                            m = TE.matmul(AB[i][:, :], ones, s2_, start=True, stop=True)
                            t1 = p.up(m, "done_pe")
                            t1 = rsqrt(stat[i][:, :], AB[i][:, :], 1.0 / P, RMS_EPS, [t1])
                            t1 = dve(V.scalar_tensor_tensor, stat[i][:, :], AB[2 + i][:, :], dnn_now[:, 0:1], stat[i][:, :],
                                     ALU.mult, ALU.mult, after=[t1])
                            zz = fl(zo[:, h0 + 2 * i:h0 + 2 * i + 2, :])
                            dve(V.tensor_tensor, zz, zz, stat[i][:, :], ALU.mult, after=[t1])
                        p.fence()

            def project(src, wvw, kc, dst):
                def one(i):
                    w = wview(st["staged"][0][1], kc, T)

                    def compute(_, bank, __):
                        for c in range(2):
                            m = feature_major(bank[0][:, c * T:(c + 1) * T], w, c * P, src, slice(0, T), kc=kc)
                        return m

                    def evacuate(bank, t, raised):
                        dve(V.tensor_copy, dst[:, 2 * i:2 * i + 2, :].rearrange("p a t -> p (a t)"), bank[0][:, :],
                            after=[t], also=raised)
                    slab(compute, evacuate)
                stream(4, lambda i: [cols(wvw, i * T, T)], one)

            with ExitStack() as f2:
                os_ = [sb(f2, nm(), [P, KD, T], F32R) for _ in range(2)]
                for k in range(KD):
                    t = split(zo[:, k, :], os_[0][:, k, :], os_[1][:, k, :], [*p.now("dve")])
                p.wait("pe", t)
                project(os_, lv(a["w_a_2"], l), KD, ya)
                p.fence()
            yb = zo
            with ExitStack() as f2:
                KB = DA_W // P
                ob = [sb(f2, nm(), [P, KB, T], F32R) for _ in range(2)]
                v = sb(f2, "da_v", [P, 2, DA_W])
                qk = sb(f2, "da_qk", [P, 2, T])
                bias = sb(f2, "da_bias", [P, 2, TRI])
                pr = [sb(f2, nm(), [P, T]) for _ in range(4)]
                PT = sb(f2, "da_probs_t", [P, 2, TRI])
                of = sb(f2, nm(), [P, T])
                sl = sb(f2, "slopes_now", [P, 2])

                def one(i):
                    w = wview(st["staged"][0][1], KD, T)

                    def compute(_, bank, __):
                        for tt in range(2):
                            m = token_major(bank[0][:, tt * T:(tt + 1) * T], w, 0, T, u, tt * P)
                        return m

                    def evacuate(bank, t, raised):
                        dve(V.tensor_copy, v[:, :, i * T:(i + 1) * T], bank[0][:, :].rearrange("p (a n) -> p a n", a=2),
                            after=[t], also=raised)
                    slab(compute, evacuate)
                stream(3, lambda i: [cols(wi, i * T + (IN_DA + 2 * DA_W), T)], one)
                p.fence()
                with p.loop(KB) as hp:
                    stage([cols(wi, hp * P + IN_DA, P), cols(wi, hp * P + (IN_DA + DA_W), P)])
                    w = wview(st["staged"][0][1], KD, T)

                    def compute(_, bank, __):
                        for c in range(2):
                            m = feature_major(bank[0][:, c * T:(c + 1) * T], w, c * P, u, slice(0, T))
                        return m

                    def evacuate(bank, t, raised):
                        dve(V.tensor_scalar, qk[:, 0, :], bank[0][:, 0:T], DA_DH ** -0.5, None, ALU.mult, after=[t])
                        dve(V.tensor_copy, qk[:, 1, :], bank[0][:, T:2 * T], also=raised)
                    slab(compute, evacuate)
                    t = dve(V.tensor_copy, sl[:, :], slope[:, bass.ds(hp * 2, 2)])
                    for e in range(2):
                        t1 = dve(V.scalar_tensor_tensor, bias[:, e, :], da_dist, sl[:, e:e + 1], da_lnc, ALU.mult, ALU.add,
                                 after=[t])
                    p.wait("pe", t1)
                    vp = sq[:, 0:1, :].rearrange("p a t -> p (a t)").rearrange("p (a n) -> p a n", a=2)
                    t = dve(V.tensor_copy, vp, v[:, :, bass.ds(hp * P, P)], after=[*p.now("pe")])
                    tS = []
                    for e in range(2):
                        r_ = slice(e * DA_DH, (e + 1) * DA_DH)
                        for tt in range(2):
                            bank, n = AB[2 * e + tt], (tt + 1) * P
                            TE.matmul(bank[:, 0:n], qk[r_, 0, tt * P:(tt + 1) * P], qk[r_, 1, 0:n], start=True, stop=False)
                            m = TE.matmul(bank[:, 0:n], ident, bias[:, e, tt * P:tt * P + n], start=False, stop=True)
                            tS.append(p.up(m, "done_pe"))
                    for i in range(4):
                        e, tt = i // 2, i % 2
                        n = (tt + 1) * P
                        bank, nmx, sm = AB[i], small[:, 20 + i:21 + i], small[:, 24 + i:25 + i]
                        t = dve(V.tensor_reduce, nmx, bank[:, 0:n], axis=AX.X, op=ALU.max, negate=True, after=[tS[i]])
                        t = act(pr[i][:, 0:n], bank[:, 0:n], ACT.Exp, bias=nmx, accum_out=sm, after=[t])
                        t = dve(V.reciprocal, sm, sm, after=[t])
                        t = dve(V.tensor_scalar, pr[i][:, 0:n], pr[i][:, 0:n], sm, None, ALU.mult, after=[t])
                        p.wait("pe", t)
                        for s_ in range(tt + 1):
                            m = TE.transpose(bank[:, s_ * P:(s_ + 1) * P], pr[i][:, s_ * P:(s_ + 1) * P], ident)
                        t = p.up(m, "done_pe")
                        if tt == 0:
                            dve(V.tensor_copy, PT[:, e, 0:P], bank[:, 0:P], after=[t])
                        else:
                            dve(V.tensor_copy, PT[:, e, P:TRI], bank[:, 0:T], after=[t])
                    p.wait("pe", *p.now("dve"))
                    for e in range(2):
                        r_ = slice(e * DA_DH, (e + 1) * DA_DH)
                        TE.matmul(AB[0][r_, 0:T], vp[:, 0, r_], PT[:, e, 0:T], start=True, stop=False)
                        m = TE.matmul(AB[0][r_, P:T], vp[:, 1, r_], PT[:, e, T:TRI], start=False, stop=True)
                    t = p.up(m, "done_pe")
                    t = dve(V.tensor_copy, of[:, :], AB[0][:, 0:T], after=[t])
                    hi, lo = (x[:, bass.ds(hp, 1), :].rearrange("p a t -> p (a t)") for x in ob)
                    split(of[:, :], hi, lo, [t], settled=True)
                    p.fence()
                project(ob, lv(a["w_b_2"], l), KB, yb)
                p.fence()
            with ExitStack() as f2:
                mg = [sb(f2, nm(), [P, KD, T], F32R) for _ in range(2)]
                sg = [sb(f2, nm(), [P, 2 * T]) for _ in range(2)]
                mt_ = [sb(f2, nm(), [P, T]) for _ in range(2)]

                def one(i):
                    q_ = st["set"]
                    w = wview(st["staged"][0][1], KD, T)

                    def compute(_, bank, __):
                        for c in range(2):
                            m = feature_major(bank[0][:, c * T:(c + 1) * T], w, c * P, u, slice(0, T))
                        return m

                    def evacuate(bank, t, raised):
                        s_ = sg[q_]
                        t1 = act(s_[:, :], bank[0][:, :], ACT.Sigmoid, after=[t])
                        dve(V.tensor_tensor, mt_[q_][:, :], s_[:, 0:T], ya[:, i, :], ALU.mult, after=[t1], also=raised)
                        t1 = dve(V.tensor_tensor, s_[:, T:2 * T], s_[:, T:2 * T], yb[:, i, :], ALU.mult)
                        t1 = dve(V.tensor_tensor, mt_[q_][:, :], mt_[q_][:, :], s_[:, T:2 * T], ALU.add, after=[t1])
                        split(mt_[q_][:, :], mg[0][:, i, :], mg[1][:, i, :], [t1])
                    slab(compute, evacuate)
                stream(KD, lambda i: [cols(wi, i * P + IN_GATE, P), cols(wi, i * P + (IN_GATE + D), P)], one)
                p.wait("pe", *p.now("dve"))
                wo = lv(a["w_o_2"], l)

                def two(i):
                    w = wview(st["staged"][0][1], KD, T)

                    def compute(_, bank, __):
                        for c in range(2):
                            m = feature_major(bank[0][:, c * T:(c + 1) * T], w, c * P, mg, slice(0, T))
                        return m

                    def evacuate(bank, t, raised):
                        for c in range(2):
                            n = 2 * i + c
                            dve(V.scalar_tensor_tensor, h[:, n, :], bank[0][:, c * T:(c + 1) * T],
                                cur[:, 5 * KD + n:5 * KD + n + 1], h[:, n, :], ALU.mult, ALU.add, after=[t],
                                also=raised if c else None)
                    slab(compute, evacuate)
                stream(4, lambda i: [cols(wo, i * T, T)], two)
                p.fence()

    n_layers = 2
    with p.loop(n_layers) as l:
        one_l = bass.ds(l, 1)
        dve(V.tensor_copy, bias_now[:, :], adab[:, one_l, :].rearrange("p a n -> p (a n)"))
        dve(V.tensor_copy, gl[:, :, :], lng[:, one_l, :, :].rearrange("p a j k -> p (a j) k"))
        dve(V.tensor_copy, cw_l[:, :, :, :].rearrange("p j x h -> p (j x h)"),
            convw[:, one_l, :, :, :].rearrange("p a j x h -> p (a j x h)"))
        t = dve(V.tensor_copy, dnn_now[:, :], dnn[:, one_l])
        p.wait("dve", t)
        ada(lv(a["ada_w_2"], l), 1, 2 * KD, 9 * KD, bias_now[:, :])
        t = dve(V.tensor_copy, cur[:, :], mods[:, :, 0], after=[*p.now("dve")])
        for j in range(3):
            sc_, gt_ = cur[:, (3 * j + 1) * KD:(3 * j + 2) * KD], cur[:, (3 * j + 2) * KD:(3 * j + 3) * KD]
            dve(V.scalar_tensor_tensor, sc_, sc_, 1.0, gl[:, j, :], ALU.add, ALU.mult, after=[t])
            if j != 1:
                dve(V.tensor_scalar, gt_, gt_, 0.5, None, ALU.mult, after=[t])
        p.fence()
        macaron(l, 0, a["ffn1_wg_2"], a["ffn1_wu_2"], a["ffn1_wd_2"])
        if upto != 5:
            mixer(l)
            macaron(l, 2, a["ffn2_wg_2"], a["ffn2_wu_2"], a["ffn2_wd_2"])
    if upto < 99:
        dump(h); return
    t = rms_scale(h, stat[0][:, 0:T])
    for k in range(KD):
        dve(V.scalar_tensor_tensor, h[:, k, :], h[:, k, :], par[:, 0, C_FIN + k:C_FIN + k + 1], stat[0][:, 0:T],
            ALU.mult, ALU.mult, after=[t])
    dump(h)
    b2.close()


USED = ["x", "c", "ctx", "c_ctx", "ada_w", "ada_b", "ln_g", "ln_b", "ffn_w13", "ffn_w2", "ret_w_in", "ret_decay",
        "ret_w_out", "na_w_qkv", "na_rpb", "na_w_out", "c_2", "ada_w_2", "ada_b_2", "ln_ffn1_2", "ln_mix_2",
        "ln_ffn2_2", "ffn1_wg_2", "ffn1_wu_2", "ffn1_wd_2", "w_in_2", "conv_w_2", "a_log_2", "dt_bias_2",
        "dn_norm_2", "w_a_2", "w_b_2", "w_o_2", "ffn2_wg_2", "ffn2_wu_2", "ffn2_wd_2", "final_norm_2"]


def program(nc, arrays, counted, upto=99):
    aps = {n: nc.dram_tensor("in_" + n, list(v.shape), F32, kind="ExternalInput").ap() for n, v in arrays.items()}
    out = nc.dram_tensor("hidden_out", [1, T, D], F32, kind="ExternalOutput").ap()
    build(nc, aps, out, counted, upto)


def kernel(**inputs):
    import concourse.bacc as _bacc
    from concourse.bass_utils import run_bass_kernel_spmd as _run

    arrays = {n: np.ascontiguousarray(inputs[n]) for n in USED}
    for n, t in enumerate(shape_tables()):
        arrays[f"table{n}"] = t
    counted = {}
    for _ in range(2):
        nc = _bacc.Bacc("TRN2", target_bir_lowering=False, num_devices=1)
        program(nc, arrays, counted)
    r = _run(nc, [{"in_" + n: v for n, v in arrays.items()}], core_ids=[0])
    return r.results[0]["hidden_out"]
```

```python
from contextlib import ExitStack, contextmanager

import numpy as np

import concourse.bass as bass
from concourse import mybir

F32 = mybir.dt.float32
F32R = mybir.dt.float32r
ALU = mybir.AluOpType
ACT = mybir.ActivationFunctionType
AX = mybir.AxisListType

P = 128
T = 256
D = 1024
KD = D // P
FF = 2816
KF = FF // P
ALPHA = float(4 ** 0.25)
LN_EPS = 1e-5
RMS_EPS = 1e-6
RING = 4
SIDE1 = 768
SIDE2 = 1152
SLOT = 2048
RET_H, RET_DK, RET_DV = 4, 256, 512
NA_H, NA_COLS, GRID = 16, 31, 64
DN_H = 8
DA_H, DA_DH = 12, 64
DA_W = DA_H * DA_DH
HALF = P // 2
NLEV = 7
TRI = 3 * P

IN_Z, IN_BA = 3 * D, 4 * D
IN_DA = IN_BA + 2 * DN_H
IN_GATE = IN_DA + 3 * DA_W


def shape_tables():
    p = np.arange(P)
    t = np.arange(T)
    ident = np.eye(P)
    ones = np.ones((P, P))
    nf = RET_DK // 4
    inv = 10000.0 ** (-np.arange(nf, dtype=np.float32) / np.float32(nf))
    inv = inv.astype(np.float32)
    rows, cols = (t // GRID).astype(np.float32), (t % GRID).astype(np.float32)
    ang = np.concatenate([rows[:, None] * inv, cols[:, None] * inv], -1).astype(np.float32)
    cos, sin = np.cos(ang).T, np.sin(ang).T
    dist = np.concatenate([t[None, :] - (p[:, None] + P * i) + T for i in range(2)], 1)
    qc, kc = (p % GRID)[:, None], np.arange(GRID)[None, :]
    w0 = np.clip(qc - 8, 0, GRID - 16)
    win = np.where((kc >= w0) & (kc < w0 + 16), 0.0, -1e30)
    first = np.concatenate([ident, ones], 1)
    block1 = np.concatenate([cos, sin, dist, win], 1)

    d0 = p[:, None] - p[None, :]
    d1 = p[:, None] + P - np.arange(T)[None, :]
    dd = np.concatenate([d0, d1], 1)
    count = sum(((dd >= 0) & (dd % r == 0) & (dd // r <= P)).astype(float) for r in (1, 4, 16))
    lnc = np.where(count > 0, np.log(np.maximum(count, 1.0)), -1e30)
    dd = np.maximum(dd, 0)
    gt = (p[:, None] > p[None, :]).astype(float)
    le = (p[:, None] <= t[None, :]).astype(float)
    incl = np.concatenate([(p[:, None] <= t[None, :]), (p[:, None] <= p[None, :])], 1).astype(float)
    strict = np.concatenate([(p[:, None] < t[None, :]), (p[:, None] < p[None, :])], 1).astype(float)
    lev = []
    for j in range(NLEV - 1):
        row, col = (p % HALF)[:, None] >> j, np.arange(HALF)[None, :] >> j
        low = (row // 2 == col // 2) & (row % 2 == 1) & (col % 2 == 0)
        up_ = (row // 2 == col // 2) & (row % 2 == 0) & (col % 2 == 1)
        lev.append((low if j else up_).astype(float))
    slope = np.broadcast_to(-(2.0 ** (-8.0 * np.arange(1, DA_H + 1) / DA_H))[None, :], (P, DA_H))
    block2 = np.concatenate([dd, lnc, gt, le, incl, strict] + lev + [slope], 1)
    return [np.ascontiguousarray(x, dtype=np.float32) for x in (first, block1, block2)]


class Program:

    def __init__(self, nc, counted):
        self.nc = nc
        self.counted = counted
        self.base = {}
        self.sems = {}
        self.owner = {}
        self.last = {}
        self.loops = []
        self.n_loops = 0
        self.eng = {"pe": nc.tensor, "dve": nc.vector, "act": nc.scalar, "pool": nc.gpsimd, "sp": nc.sync}
        for engine in ("pe", "dve", "act", "pool"):
            self.sem("done_" + engine, engine)
            self.last[engine] = ("done_" + engine,)
            self.sem("settled_" + engine)
        self.sem("settled_sp")

    def sem(self, name, owner=None):
        self.sems[name] = self.nc.alloc_semaphore(name)
        self.base[name] = 0
        self.owner[name] = owner
        return name

    def at(self, name):
        v = self.base[name]
        for label, var in self.loops:
            k = self.counted.get((label, name), 0)
            if k:
                v = var * k + v
        return (name, v)

    def now(self, engine):
        return [self.at(name) for name in self.last[engine]]

    def wait(self, engine, *values):
        for v in values:
            if v is not None and not (isinstance(v[1], int) and v[1] <= 0):
                self.eng[engine].wait_ge(self.sems[v[0]], v[1])

    def up(self, ins, name, n=1):
        ins.then_inc(self.sems[name], n)
        self.base[name] += n
        if self.owner[name]:
            self.last[self.owner[name]] = (name,)
        return self.at(name)

    def settle(self, engine):
        self.eng[engine].sem_inc(self.sems["settled_" + engine], 1)

    def do(self, engine, issue, *args, after=(), also=None, settled=False, **kw):
        self.wait(engine, *after)
        if settled:
            self.settle(engine)
        return self.up(issue(*args, **kw), also or "done_" + engine)

    def fence(self):
        now = {e: self.now(e) for e in self.last}
        for e in now:
            self.wait(e, *[v for o in now for v in now[o]])

    @contextmanager
    def loop(self, n):
        label = self.n_loops
        self.n_loops += 1
        before = dict(self.base)
        if self.loops:
            for e in self.eng:
                self.settle(e)
        for e, names in self.last.items():
            self.last[e] = tuple(dict.fromkeys(names + self.counted.get((label, "last", e), ())))
        with self.nc.Fori(0, n) as var:
            self.loops.append((label, var))
            yield var
            self.loops.pop()
        for e, names in self.last.items():
            self.counted[(label, "last", e)] = names
        for name in self.base:
            k = self.base[name] - before.get(name, 0)
            self.counted[(label, name)] = k
            self.base[name] = before.get(name, 0) + k * n


def build(nc, a, out, slopes, upto=99):
    p = Program(nc, slopes)
    V, S, G, TE, SY = nc.vector, nc.scalar, nc.gpsimd, nc.tensor, nc.sync
    fixed = ExitStack()

    def sb(stack, name, shape, dt=F32):
        return stack.enter_context(nc.sbuf_tensor(name, shape, dt))

    dve = lambda issue, *x, **k: p.do("dve", issue, *x, **k)
    act = lambda *x, **k: p.do("act", S.activation, *x, **k)
    pool = lambda issue, *x, **k: p.do("pool", issue, *x, **k)

    raw = [sb(fixed, f"weights_raw{i}", [P, SLOT]) for i in range(RING)]
    w_hi = [sb(fixed, f"weights_hi{i}", [P, SLOT], F32R) for i in range(2)]
    w_lo = [sb(fixed, f"weights_lo{i}", [P, SLOT], F32R) for i in range(2)]
    h = sb(fixed, "hidden", [P, KD, T])[:, :, :]
    sq = sb(fixed, "squares", [P, KD, T])
    table0 = sb(fixed, "ident_ones", [P, 2 * P])
    ident, ones = table0[:, 0:P], table0[:, P:2 * P]
    par = sb(fixed, "vectors", [P, 6, P])
    cact = sb(fixed, "silu_c", [P, 3 * KD])
    mods1 = sb(fixed, "modulation_1", [P, 2, 6 * KD, 2])
    mods2 = sb(fixed, "modulation_2", [P, 2, 9 * KD])
    cur = sb(fixed, "modulation_now", [P, 9 * KD])
    stat = [sb(fixed, f"stat{i}", [P, 2 * T]) for i in range(3)]
    small = sb(fixed, "small", [P, 64])
    ret_dec = sb(fixed, "ret_decay", [P, 2 * RET_H])
    alog = sb(fixed, "a_log", [P, 2, DN_H])
    dtb = sb(fixed, "dt_bias", [P, 2, DN_H])

    banks = [nc.alloc_psum_tensor(f"bank{i}", [P, 512], F32) for i in range(8)]
    GB = [[banks[0], banks[1]], [banks[2], banks[3]]]
    AB = banks[4:8]

    arrived = [p.sem(f"weights_arrived{i}") for i in range(RING)]
    slot_read = [p.sem(f"slot_read{i}", "dve") for i in range(RING)]
    used = [p.sem(f"weights_used{i}", "pe") for i in range(2)]
    evac = [p.sem(f"evacuated{i}", "dve") for i in range(2)]
    vecs = p.sem("vectors_arrived")
    st = {"slot": 0, "pair": 0, "set": 0, "staged": [], "side": []}

    def load(parts):
        s = st["slot"]
        st["slot"] = (s + 1) % RING
        p.wait("sp", p.at(slot_read[s]))
        if p.loops:
            p.settle("sp")
        off = 0
        for ap in parts:
            kc, c = ap.shape[1], ap.shape[2]
            tot = sum(x.shape[2] for x in parts)
            dst = raw[s][:, 0:kc * tot].rearrange("p (k c) -> p k c", k=kc)[:, :, off:off + c]
            p.up(SY.dma_start(dst, ap), arrived[s], 16)
            off += c
        return s, parts[0].shape[1] * off

    def stage(parts):
        s, n = load(parts)
        b = st["pair"]
        st["pair"] = 1 - b
        hi, lo, src = w_hi[b][:, 0:n], w_lo[b][:, 0:n], raw[s][:, 0:n]
        t = act(hi, src, ACT.Copy, after=[p.at(arrived[s]), p.at(used[b])])
        dve(V.tensor_tensor, lo, src, hi.bitcast(F32), ALU.subtract, after=[t], also=slot_read[s])
        st["staged"].append((s, b, parts[0].shape[1]))

    def slab(compute, evacuate, keep_set=False):
        if st["side"]:
            st["side"].pop(0)()
        s, b, kc = st["staged"].pop(0)
        i = st["set"]
        p.wait("pe", p.at(slot_read[s]), p.at(evac[i]))
        w = [x[b][:, :].rearrange("p (k c) -> p k c", k=kc) if kc * (SLOT // kc) == SLOT
             else x[b][:, 0:kc * (SLOT // kc)].rearrange("p (k c) -> p k c", k=kc) for x in (w_hi, w_lo)]
        last = compute(w, GB[i], b)
        t = p.up(last, used[b])
        if not keep_set:
            st["set"] = 1 - i
            evacuate(GB[i], t, evac[i])
        return t

    def wview(b, kc, c):
        return [x[b][:, 0:kc * c].rearrange("p (k c) -> p k c", k=kc) for x in (w_hi, w_lo)]

    def passes(out_, l, r, first, last):
        TE.matmul(out_, l[0], r[0], start=first, stop=False)
        TE.matmul(out_, l[0], r[1], start=False, stop=False)
        return TE.matmul(out_, l[1], r[0], start=False, stop=last)

    def feature_major(out_, w, c0, act_, toks, kc=KD, k0=0, first=True, last=True):
        for k in range(kc):
            m = passes(out_, [x[:, k, c0:c0 + P] for x in w], [x[:, k0 + k, toks] for x in act_],
                       first and k == 0, last and k == kc - 1)
        return m

    def token_major(out_, w, c0, c1, act_, tok0, kc=KD):
        for k in range(kc):
            m = passes(out_, [x[:, k, tok0:tok0 + P] for x in act_], [x[:, k, c0:c1] for x in w],
                       k == 0, k == kc - 1)
        return m

    def stream(n, parts, one, m=RING, side=None):
        turns = (n - 1) // m
        stage(parts(0))
        if turns >= 2:
            with p.loop(turns) as i:
                finish = side(i) if side else None
                for j in range(m):
                    stage(parts(i * m + (j + 1)))
                    one(i * m + j)
                if finish:
                    finish()
            rest = range(turns * m, n)
        else:
            rest = range(n)
        for i in rest:
            if i + 1 < n:
                stage(parts(i + 1))
            one(i)

    def wv(ap):
        return ap.rearrange("(k p) n -> p k n", p=P)

    def cols(v, c0, n):
        return v[:, :, bass.ds(c0, n)]

    def vector_load(dst, src):
        return p.up(SY.dma_start(dst, src), vecs, 16)

    b1 = ExitStack()
    hb = sb(b1, "hidden_both", [P, 2, KD, T])
    t1tab = sb(b1, "table1", [P, 2 * T + 2 * T + GRID])
    pad = sb(b1, "rpb_rows", [NA_H * 7, 2 * GRID])
    side_w = [sb(b1, f"side_weights{i}", [P, SIDE2]) for i in range(2)]
    side_acc = sb(b1, "side_sums", [P, 2 * SIDE1])

    f0 = ExitStack()
    rows = sb(f0, "vector_rows", [P, 6, P])
    groups = [
        [a["c"].rearrange("o (k p) -> (o k) p", p=P), a["c_ctx"].rearrange("(k p) -> k p", p=P),
         a["c_2"].rearrange("o (k p) -> (o k) p", p=P), a["ln_g"].rearrange("l j (k p) -> (l j k) p", p=P),
         a["ln_b"].rearrange("l j (k p) -> (l j k) p", p=P), a["final_norm_2"].rearrange("(k p) -> k p", p=P),
         a["dn_norm_2"]],
        [a["ada_b"].rearrange("l (k p) -> (l k) p", p=P)],
        [a["ada_b_2"][0:1].rearrange("l (k p) -> (l k) p", p=P), a["ln_ffn1_2"].rearrange("l (k p) -> (l k) p", p=P),
         a["ln_mix_2"].rearrange("l (k p) -> (l k) p", p=P), a["ln_ffn2_2"].rearrange("l (k p) -> (l k) p", p=P)],
        [a["ada_b_2"][1:2].rearrange("l (k p) -> (l k) p", p=P)] ,
        [a["conv_w_2"][0].rearrange("j (k p) -> (j k) p", p=P)],
        [a["conv_w_2"][1].rearrange("j (k p) -> (j k) p", p=P)],
    ]
    C_LNG, C_LNB, C_FIN, C_DNN = 24, 56, 88, 96
    vector_load(table0[:, :], a["table0"])
    vector_load(ret_dec[:, :], a["ret_decay"].rearrange("d h -> (d h)").partition_broadcast(P))
    vector_load(alog[:, :, :].rearrange("p l h -> p (l h)"), a["a_log_2"].rearrange("l h -> (l h)").partition_broadcast(P))
    vector_load(dtb[:, :, :].rearrange("p l h -> p (l h)"), a["dt_bias_2"].rearrange("l h -> (l h)").partition_broadcast(P))
    tok = sb(f0, "tokens", [P, 2, 2, D])
    x_in = p.sem("tokens_arrived")
    for g, srcs in enumerate(groups):
        r0 = 0
        for s_ in srcs:
            vector_load(rows[r0:r0 + s_.shape[0], g, :], s_)
            r0 += s_.shape[0]
    for half, src in enumerate((a["x"], a["ctx"])):
        p.up(SY.dma_start(tok[:, half, :, :], src[0].rearrange("(a p) n -> p a n", p=P)), x_in, 16)
    p.wait("pe", p.at(vecs))
    for g, srcs in enumerate(groups):
        r0 = sum(s_.shape[0] for s_ in srcs)
        t = p.do("pe", TE.transpose, AB[g % 4][:, 0:r0], rows[0:r0, g, :], ident[0:r0, 0:r0],
                 after=[*p.now("dve")] if g >= 4 else [])
        dve(V.tensor_copy, par[:, g, 0:r0], AB[g % 4][:, 0:r0], after=[t])
        if g == 0:
            act(cact[:, :], par[:, 0, 0:3 * KD], ACT.Silu, after=[*p.now("dve")])
    for e in ("dve", "act"):
        p.wait(e, p.at(vecs))

    def ada_first(wk, dst, bias):
        with ExitStack() as f:
            row = sb(f, "modulation_rows", [2, 6 * D])

            def one(n):
                s, _ = load([cols(wk, n * T, T)])
                i = st["set"]
                st["set"] = 1 - i
                ws = raw[s][:, :].rearrange("p (k c) -> p k c", k=KD)
                p.wait("pe", p.at(arrived[s]), p.at(slot_read[(s - 2) % RING]))
                for k in range(KD):
                    m = TE.matmul(GB[i][0][0:2, 0:T], cact[:, k:k + KD + 1:KD], ws[:, k, :], start=k == 0,
                                  stop=k == KD - 1)
                t = p.up(m, "done_pe")
                dve(V.tensor_copy, row[:, bass.ds(n * T, T)], GB[i][0][0:2, 0:T], after=[t], also=slot_read[s])
            p.wait("pe", *p.now("act"))
            with p.loop(6 * KD // 2 // RING) as i:
                for j in range(RING):
                    one(i * RING + j)
            p.wait("pe", *p.now("dve"))
            for n in range(6 * KD):
                m = TE.transpose(AB[0][:, 2 * n:2 * n + 2], row[:, n * P:(n + 1) * P], ident[0:2, 0:2])
            t = p.up(m, "done_pe")
            dve(V.tensor_tensor, dst, AB[0][:, 0:12 * KD].rearrange("p (n v) -> p n v", v=2),
                bias.unsqueeze(2).broadcast_to([P, 6 * KD, 2]), ALU.add, after=[t])
            p.fence()

    side_in = [p.sem(f"side_arrived{i}") for i in range(2)]
    side_read = [p.sem(f"side_read{i}", "dve") for i in range(2)]

    def side_steps(wk, c0, width, vec_cols):
        def step(k):
            i = k % 2
            buf = side_w[i][:, 0:width]
            p.wait("sp", p.at(side_read[i]))
            p.up(SY.dma_start(buf, wk[:, k, bass.ds(c0, width)]), side_in[i], 16)
            p.wait("dve", p.at(side_in[i]), *p.now("dve"), *p.now("pe") if k == 0 else [])
            for n, v in enumerate(vec_cols):
                acc, c = side_acc[:, n * width:(n + 1) * width], cact[:, v + k:v + k + 1]
                also = side_read[i] if n == len(vec_cols) - 1 else None
                if k == 0:
                    dve(V.tensor_scalar, acc, buf, c, None, ALU.mult, also=also)
                else:
                    dve(V.scalar_tensor_tensor, acc, buf, c, acc, ALU.mult, ALU.add, also=also)
        return [lambda k=k: step(k) for k in range(KD)]

    def side_finish(width, dst, bias):
        n = width // P
        bank, raised = GB[st["set"]][0], evac[st["set"]]
        p.wait("pe", *p.now("dve"))
        for v in range(len(dst)):
            for c in range(n):
                m = TE.matmul(bank[:, v * n + c:v * n + c + 1], side_acc[:, v * width + c * P:v * width + (c + 1) * P], ones[:, 0:1],
                              start=True, stop=True)
        t = p.up(m, "done_pe")
        for v, d_ in enumerate(dst):
            dve(V.tensor_tensor, d_, bank[:, v * n:(v + 1) * n], bias, ALU.add, after=[t], also=raised)

    def column_sums(bank, src, n, width):
        for k in range(n):
            m = TE.matmul(bank, ones, src(k), start=k == 0, stop=k == n - 1)
        return p.up(m, "done_pe")

    def rsqrt(dst, src, scale, eps, after):
        t = dve(V.tensor_scalar, dst, src, scale, eps, ALU.mult, ALU.add, after=after)
        t = act(dst, dst, ACT.Sqrt, after=[t])
        return dve(V.reciprocal, dst, dst, after=[t])

    def bc(x, n):
        return x.unsqueeze(1).broadcast_to([P, n, x.shape[1]])

    def layer_norm(hx, gcol, bcol):
        p.wait("pe", *p.now("dve"))
        t = column_sums(AB[0][:, 0:T], lambda k: hx[:, k, :], KD, T)
        t = dve(V.tensor_scalar, stat[0][:, 0:T], AB[0][:, 0:T], 1.0 / D, None, ALU.mult, after=[t])
        for q in range(2):
            x = hx[:, 4 * q:4 * q + 4, :]
            t = dve(V.tensor_tensor, x, x, bc(stat[0][:, 0:T], 4), ALU.subtract, after=[t])
            t2 = act(sq[:, 4 * q:4 * q + 4, :], x, ACT.Square, after=[t], settled=True)
        p.wait("pe", t2)
        t = column_sums(AB[1][:, 0:T], lambda k: sq[:, k, :], KD, T)
        t = rsqrt(stat[1][:, 0:T], AB[1][:, 0:T], 1.0 / D, LN_EPS, [t])
        for q in range(2):
            x = hx[:, 4 * q:4 * q + 4, :]
            t2 = dve(V.tensor_tensor, x, x, bc(stat[1][:, 0:T], 4), ALU.mult, after=[t])
        for k in range(KD):
            t = dve(V.tensor_scalar, hx[:, k, :], hx[:, k, :], gcol[:, k:k + 1], bcol[:, k:k + 1],
                    ALU.mult, ALU.add, after=[t2])
        return t

    def split_affine(x, scale, shift, hi, lo, tmp, after):
        th = act(hi, x, ACT.Identity, scale=scale, bias=shift, after=after, settled=True)
        t = dve(V.tensor_scalar, tmp, x, scale, shift, ALU.mult, ALU.add, after=after)
        return dve(V.tensor_tensor, lo, tmp, hi.bitcast(F32), ALU.subtract, after=[t, th])

    def split(x, hi, lo, after, settled=False):
        th = act(hi, x, ACT.Copy, after=after, settled=settled)
        return dve(V.tensor_tensor, lo, x, hi.bitcast(F32), ALU.subtract, after=[th])

    def feed_forward(gate_up, w_down, act_, out_one, side=None):
        with ExitStack() as f:
            mid = [sb(f, p_ + nm(), [P, KF, T], F32R) for p_ in ("ffn_hi", "ffn_lo")]
            gate = [sb(f, nm(), [P, T]) for _ in range(2)]
            prod = [sb(f, nm(), [P, T]) for _ in range(2)]

            def up_one(i):
                q = st["set"]
                b = st["staged"][0][1]
                w = wview(b, KD, T)

                def compute(_, bank, __):
                    for c in range(2):
                        m = feature_major(bank[0][:, c * T:(c + 1) * T], w, c * P, act_, slice(0, T))
                    return m

                def evacuate(bank, t, raised):
                    t1 = act(gate[q][:, :], bank[0][:, 0:T], ACT.Silu, after=[t])
                    t2 = dve(V.tensor_tensor, prod[q][:, :], gate[q][:, :], bank[0][:, T:2 * T], ALU.mult,
                             after=[t1], also=raised)
                    hi, lo = (x[:, bass.ds(i, 1), :].rearrange("p a t -> p (a t)") for x in mid)
                    split(prod[q][:, :], hi, lo, [t2], settled=True)
                slab(compute, evacuate)
            stream(KF, lambda i: [cols(g_, i * P, P) for g_ in gate_up], up_one, m=2 * RING if side else RING,
                   side=side)
            HK = KF // 2
            wd = [w_down[:, 0:HK, :], w_down[:, HK:KF, :]]
            p.wait("pe", *p.now("dve"))

            def parts(i, j):
                return [cols(wd[j % 2], i * 2 * P + (j // 2) * P, P)]

            def four(i, nxt):
                for j in range(4):
                    if j < 3:
                        stage(parts(i, j + 1))
                    elif nxt is not None:
                        stage(parts(nxt, 0))
                    w = wview(st["staged"][0][1], HK, P)

                    def compute(_, bank, __):
                        return feature_major(bank[0][:, (j // 2) * T:(j // 2 + 1) * T], w, 0, mid, slice(0, T),
                                             kc=HK, k0=(j % 2) * HK, first=j % 2 == 0, last=j % 2 == 1)

                    def evacuate(bank, t, raised):
                        out_one(i * 2, bank[0][:, 0:T], t, None)
                        out_one(i * 2 + 1, bank[0][:, T:2 * T], t, raised)
                    if j == 3:
                        slab(compute, evacuate)
                    else:
                        slab(compute, None, keep_set=True)
            stage(parts(0, 0))
            if side:
                for i in range(KD // 2):
                    if i % 2 == 0:
                        finish = side(2 + i // 2)
                    four(i, i + 1 if i < KD // 2 - 1 else None)
                    if i % 2:
                        finish()
            else:
                with p.loop(KD // 2 - 1) as i:
                    four(i, i + 1)
                four(KD // 2 - 1, None)

    names = [0]

    def nm():
        names[0] += 1
        return f"tmp{names[0]}"

    cosT, sinT, dist, colwin = t1tab[:, 0:T], t1tab[:, T:2 * T], t1tab[:, 2 * T:4 * T], t1tab[:, 4 * T:4 * T + GRID]
    tab_t = p.up(SY.dma_start(t1tab[:, :], a["table1"]), p.sem("table1_arrived"), 16)

    pad_d = nc.dram_tensor("rpb_padded", [NA_H, 7, 2 * GRID], F32)
    exp_d = nc.dram_tensor("rpb_expanded", [GRID, NA_H * 7, GRID], F32)
    bias_sem = p.sem("bias_tables")
    t = pool(G.memset, pad[:, :], 0.0)
    p.wait("pool", t)
    for hh in range(NA_H):
        t = p.up(G.dma_start(pad[hh * 7:hh * 7 + 7, GRID - 16:GRID - 16 + NA_COLS], a["na_rpb"][hh, 4:11, :]),
                 bias_sem, 16)
    p.wait("pool", t)
    t = p.up(G.dma_start(pad_d[:, :, :].rearrange("h j c -> (h j) c"), pad[:, :]), bias_sem, 16)
    p.wait("pool", t)
    with p.loop(GRID) as c:
        p.up(G.dma_start(exp_d[bass.ds(c, 1), :, :].rearrange("o r c -> (o r) c"),
                         pad_d[:, :, bass.ds(GRID - 1 - c, GRID)].rearrange("h j c -> (h j) c")), bias_sem, 16)
    bias_t = p.at(bias_sem)
    p.wait("pe", p.at(x_in))
    for half in range(2):
        for tt in range(2):
            for q in range(2):
                bank = AB[2 * tt + q]
                p.wait("pe", *p.now("dve"))
                for k in range(4):
                    m = TE.transpose(bank[:, k * P:(k + 1) * P], tok[:, half, tt, (4 * q + k) * P:(4 * q + k + 1) * P],
                                     ident)
                t = p.up(m, "done_pe")
                dve(V.tensor_copy, hb[:, half, 4 * q:4 * q + 4, tt * P:(tt + 1) * P],
                    bank[:, :].rearrange("p (k t) -> p k t", k=4), after=[t])
    p.fence()
    f0.close()

    def tail(layer, half, w13, w2, side=None):
        hx = sb_half(half)
        gb = lambda c, j: par[:, 0, c + (layer * 2 + j) * KD:c + (layer * 2 + j + 1) * KD]
        t = layer_norm(hx, gb(C_LNG, 0), gb(C_LNB, 0))
        with ExitStack() as f:
            af = [sb(f, nm(), [P, KD, T], F32R) for _ in range(2)]
            tmp = [sb(f, nm(), [P, T]) for _ in range(2)]
            for k in range(KD):
                t = split_affine(hx[:, k, :], cur[:, 4 * KD + k:4 * KD + k + 1], cur[:, 3 * KD + k:3 * KD + k + 1],
                                 af[0][:, k, :], af[1][:, k, :], tmp[k % 2][:, :], [*p.now("dve")])
            p.wait("pe", t)

            def out_one(c, psum, t, raised):
                hc = hx[:, bass.ds(c, 1), :].rearrange("p a t -> p (a t)")
                g_ = small[:, 0:1]
                t0 = dve(V.tensor_copy, g_, cur[:, bass.ds(c + 5 * KD, 1)], after=[*p.now("dve")])
                t0 = dve(V.tensor_scalar, hc, hc, ALPHA, None, ALU.mult)
                dve(V.scalar_tensor_tensor, hc, psum, g_, hc, ALU.mult, ALU.add, after=[t, t0], also=raised)
            w13v = wv(w13)
            feed_forward([w13v[:, :, 0:FF], w13v[:, :, FF:2 * FF]], wv(w2), af, out_one, side)
        layer_norm(hx, gb(C_LNG, 1), gb(C_LNB, 1))
        p.fence()

    def sb_half(half):
        return hb[:, bass.ds(half, 1), :, :].rearrange("p a k t -> p (a k) t")

    def modulation_of(layer, vec):
        t = dve(V.tensor_copy, cur[:, 0:6 * KD], mods1[:, layer, :, bass.ds(vec, 1)].rearrange("p c v -> p (c v)"),
                after=[*p.now("dve")])
        for c in (1, 4):
            t = dve(V.tensor_scalar, cur[:, c * KD:(c + 1) * KD], cur[:, c * KD:(c + 1) * KD], 1.0, None, ALU.add,
                    after=[t])
        return t

    def both_modulated(layer, am, tmp):
        for half in range(2):
            t = modulation_of(layer, half)
            p.wait("act", t)
            for k in range(KD):
                sl = slice(half * T, (half + 1) * T)
                split_affine(hb[:, half, k, :], cur[:, KD + k:KD + k + 1], cur[:, k:k + 1],
                             am[0][:, k, sl], am[1][:, k, sl], tmp[k % 2][:, :], [t])
            p.fence()

    ada_first(wv(a["ada_w"][0]), mods1[:, 0, :, :], par[:, 1, 0:6 * KD])
    with ExitStack() as f:
        am = [sb(f, nm(), [P, KD, 2 * T], F32R) for _ in range(2)]
        y = sb(f, "mixer_out", [P, KD, 2 * T])
        tmp = stat[1:3]
        both_modulated(0, am, [x[:, 0:T] for x in tmp])
        dve(V.memset, y[:, :, :], 0.0)
        lg = small[:, 8:16]
        t = act(lg, ret_dec[:, :], ACT.Exp, after=[p.at(vecs)])
        dve(V.tensor_scalar, lg, lg, -1.0, None, ALU.mult, after=[t])
        Pc = sb(f, "ret_probs_ctx", [P, 2, T])
        Pm = sb(f, "ret_probs", [P, 4, T])
        o = sb(f, "ret_out", [P, 4, 2 * T])
        p.fence()
        wi = wv(a["ret_w_in"])
        with p.loop(RET_H) as hd:
            nq = SIDE1 // P
            for g_ in range(2):
                s_ = side_steps(wv(a["ada_w"][1]), (hd * 2 + g_) * SIDE1, SIDE1, (0, KD))
                st["side"] += [lambda x=x, y=y: (x(), y()) for x, y in zip(s_[::2], s_[1::2])]
                end = lambda g_=g_: side_finish(
                    SIDE1, [mods1[:, 1, bass.ds((hd * 2 + g_) * nq, nq), v_:v_ + 1].rearrange("p n v -> p (n v)")
                            for v_ in range(2)], par[:, 1, bass.ds((hd * 2 + g_) * nq + 6 * KD, nq)])
                if g_ == 0:
                    st["side"].append(end)
            with ExitStack() as g1:
                q, k_ = (h[:, 4 * i:4 * i + 4, :].rearrange("p (c a) t -> p c (a t)", a=2) for i in range(2))
                v = sb(g1, nm(), [P, 4, RET_DV])
                stage([cols(wi, hd * RET_DK, RET_DK)])
                for which, dst in enumerate((q, k_)):
                    nxt = [cols(wi, hd * RET_DK + D, RET_DK)] if which == 0 else \
                          [cols(wi, hd * RET_DV + 2 * D, T)]
                    stage(nxt)
                    w = wview(st["staged"][0][1], KD, T)

                    def compute(_, bank, __):
                        for c in range(2):
                            m = feature_major(bank[c][:, :], w, c * P, am, slice(0, 2 * T))
                        return m

                    def evacuate(bank, t, raised):
                        for c in range(2):
                            act(dst[:, c, T:2 * T], bank[c][:, T:2 * T], ACT.Copy, after=[t])
                        x1, x2 = bank[0][:, 0:T], bank[1][:, 0:T]
                        A, B = tmp[0], tmp[1]
                        t1 = dve(V.tensor_tensor, A[:, 0:T], x1, cosT, ALU.mult, after=[t, tab_t, *p.now("dve"), *p.now("act")])
                        t1 = dve(V.tensor_tensor, A[:, T:2 * T], x2, sinT, ALU.mult)
                        t1 = dve(V.tensor_tensor, B[:, 0:T], x1, sinT, ALU.mult)
                        t1 = dve(V.tensor_tensor, B[:, T:2 * T], x2, cosT, ALU.mult)
                        dve(V.tensor_tensor, dst[:, 0, 0:T], A[:, 0:T], A[:, T:2 * T], ALU.subtract, after=[t1])
                        dve(V.tensor_tensor, dst[:, 1, 0:T], B[:, 0:T], B[:, T:2 * T], ALU.add,
                            after=[*p.now("act")], also=raised)
                    slab(compute, evacuate)
                for j in range(2):
                    if j == 0:
                        stage([cols(wi, hd * RET_DV + (2 * D + T), T)])
                    else:
                        stage([cols(wi, hd * RET_DV + 4 * D, T)])
                    w = wview(st["staged"][0][1], KD, T)

                    def compute(_, bank, __):
                        for tt in range(4):
                            m = token_major(bank[tt // 2][:, (tt % 2) * T:(tt % 2 + 1) * T], w, 0, T, am, tt * P)
                        return m

                    def evacuate(bank, t, raised):
                        for c in range(2):
                            dve(V.tensor_copy, v[:, 2 * c:2 * c + 2, j * T:(j + 1) * T],
                                bank[c][:, :].rearrange("p (a n) -> p a n", a=2), after=[t],
                                also=raised if c else None)
                    slab(compute, evacuate)
                lf = small[:, 16:17]
                lb = small[:, 17:18]
                t = dve(V.tensor_copy, lf, lg[:, bass.ds(hd, 1)], after=[*p.now("dve")])
                t = dve(V.tensor_scalar, lb, lg[:, bass.ds(hd + RET_H, 1)], -1.0, None, ALU.mult)
                A, B = tmp[0][:, :], tmp[1][:, :]
                d2 = dist
                self_ = Pm[:, 0:2, :].rearrange("p a t -> p (a t)")
                cross = Pm[:, 2:4, :].rearrange("p a t -> p (a t)")
                t = dve(V.tensor_scalar, A, d2, -float(T), 0.0, ALU.add, ALU.max, after=[t])
                ta = act(A, A, ACT.Exp, scale=lf, after=[t])
                t = dve(V.tensor_scalar, B, d2, -float(T), 0.0, ALU.add, ALU.min)
                tb = act(B, B, ACT.Exp, scale=lb, after=[t])
                t = dve(V.scalar_tensor_tensor, A, d2, float(T), A, ALU.is_ge, ALU.mult, after=[ta])
                t = dve(V.scalar_tensor_tensor, B, d2, float(T), B, ALU.is_le, ALU.mult, after=[tb])
                t = dve(V.tensor_tensor, self_, A, B, ALU.add, after=[t])
                ta = act(A, d2, ACT.Exp, scale=lf, after=[t])
                t = dve(V.tensor_scalar, B, d2, -2.0 * T, None, ALU.add, after=[t])
                tb = act(B, B, ACT.Exp, scale=lb, after=[t])
                t = dve(V.tensor_tensor, cross, A, B, ALU.add, after=[ta, tb])
                p.wait("pe", *p.now("dve"), *p.now("act"))
                for i in range(4):
                    for c in range(2):
                        m = TE.matmul(AB[i // 2][:, (i % 2) * T:(i % 2 + 1) * T], k_[:, c, i * P:(i + 1) * P],
                                      q[:, c, 0:T], start=c == 0, stop=c == 1)
                for i in range(2):
                    for c in range(2):
                        m = TE.matmul(AB[2][:, i * T:(i + 1) * T], k_[:, c, T + i * P:T + (i + 1) * P],
                                      q[:, c, T:2 * T], start=c == 0, stop=c == 1)
                t = p.up(m, "done_pe")
                fl = lambda x: x.rearrange("p a t -> p (a t)")
                dve(V.scalar_tensor_tensor, fl(Pc[:, :, :]), AB[2][:, :], RET_DK ** -0.5, self_, ALU.mult, ALU.mult,
                    after=[t])
                for i in range(2):
                    t = dve(V.scalar_tensor_tensor, fl(Pm[:, 2 * i:2 * i + 2, :]), AB[i][:, :], RET_DK ** -0.5,
                            fl(Pm[:, 2 * i:2 * i + 2, :]), ALU.mult, ALU.mult)
                p.wait("pe", t)
                for c in range(4):
                    for i in range(4):
                        TE.matmul(AB[c][:, 0:T], v[:, i, c * P:(c + 1) * P], Pm[:, i, :], start=i == 0, stop=i == 3)
                    for i in range(2):
                        m = TE.matmul(AB[c][:, T:2 * T], v[:, 2 + i, c * P:(c + 1) * P], Pc[:, i, :],
                                      start=i == 0, stop=i == 1)
                    t = p.up(m, "done_pe")
                    t1 = dve(V.tensor_copy, o[:, c, :], AB[c][:, :], after=[t])
                    t2 = act(sq[:, 2 * c:2 * c + 2, :].rearrange("p a t -> p (a t)"), o[:, c, :], ACT.Square, after=[t1])
                p.wait("pe", t2)
                t = column_sums(AB[0][:, :], lambda k: sq[:, 2 * k:2 * k + 2, :].rearrange("p a t -> p (a t)"), 4, 512)
                t = rsqrt(stat[0][:, :], AB[0][:, :], 1.0 / RET_DV, RMS_EPS, [t])
                t = dve(V.tensor_tensor, o[:, :, :], o[:, :, :], bc(stat[0][:, :], 4), ALU.mult, after=[t])
            with ExitStack() as g2:
                z = [sb(g2, nm(), [P, 4, 2 * T], F32R) for _ in range(2)]
                wo = a["ret_w_out"].rearrange("(g k p) n -> g p k n", p=P, k=4)
                wo_h = wo[bass.ds(hd, 1), :, :, :].rearrange("g p k n -> p (g k) n")
                for j in range(2):
                    stage([cols(wi, hd * RET_DV + (4 * D + T), T)] if j == 0 else [cols(wo_h, 0, T)])
                    w = wview(st["staged"][0][1], KD, T)

                    def compute(_, bank, __):
                        for c in range(2):
                            m = feature_major(bank[c][:, :], w, c * P, am, slice(0, 2 * T))
                        return m

                    def evacuate(bank, t, raised):
                        for c in range(2):
                            A = tmp[c][:, :]
                            n = 2 * j + c
                            t1 = act(A, bank[c][:, :], ACT.Silu, after=[t, *p.now("dve")])
                            t1 = dve(V.tensor_tensor, A, A, o[:, n, :], ALU.mult, after=[t1],
                                     also=raised if c else None)
                            split(A, z[0][:, n, :], z[1][:, n, :], [t1])
                    slab(compute, evacuate)
                for j in range(4):
                    if j < 3:
                        stage([cols(wo_h, (j + 1) * T, T)])
                    w = wview(st["staged"][0][1], 4, T)
                    p.wait("pe", *p.now("dve")) if j == 0 else None

                    def compute(_, bank, __):
                        for c in range(2):
                            m = feature_major(bank[c][:, :], w, c * P, z, slice(0, 2 * T), kc=4)
                        return m

                    def evacuate(bank, t, raised):
                        for c in range(2):
                            yc = y[:, 2 * j + c, :]
                            dve(V.tensor_tensor, yc, yc, bank[c][:, :], ALU.add, after=[t],
                                also=raised if c else None)
                    slab(compute, evacuate)
            assert not st["side"]
            end()
            p.fence()
        for half in range(2):
            hx = hb[:, half, :, :]
            t = dve(V.tensor_scalar, hx, hx, ALPHA, None, ALU.mult, after=[*p.now("dve")])
            for k in range(KD):
                dve(V.scalar_tensor_tensor, hx[:, k, :], y[:, k, half * T:(half + 1) * T],
                    mods1[:, 0, 2 * KD + k, half:half + 1], hx[:, k, :], ALU.mult, ALU.add, after=[t])
        p.fence()

    def dump(src):
        with ExitStack() as f:
            rows_out = [sb(f, nm(), [P, D]) for _ in range(2)]
            for tt in range(2):
                for q in range(2):
                    p.wait("pe", *p.now("dve"))
                    for k in range(4):
                        m = TE.transpose(AB[2 * tt + q][:, k * P:(k + 1) * P], src[:, 4 * q + k, tt * P:(tt + 1) * P], ident)
                    t = p.up(m, "done_pe")
                    t = dve(V.tensor_copy, rows_out[tt][:, q * 512:(q + 1) * 512], AB[2 * tt + q][:, :], after=[t])
                p.wait("sp", t)
                p.up(SY.dma_start(out[0, tt * P:(tt + 1) * P, :], rows_out[tt][:, :]), stored, 16)
            p.wait("sp", p.at(stored))
            p.wait("pool", p.at(bias_sem))
    stored = p.sem("stored")

    if upto == 1:
        dump(hb[:, 0, :, :]); return
    SW = 9 * D // 8

    def side2(layer, block):
        assert not st["side"]
        st["side"] = side_steps(wv(a["ada_w_2"][layer]), block * SW, SW, (2 * KD,))
        n = SW // P

        def finish():
            assert not st["side"]
            side_finish(SW, [mods2[:, layer, bass.ds(block * n, n)]], par[:, 2 + layer, bass.ds(block * n, n)])
        return finish

    def side2_of(layer):
        return lambda block: side2(layer, block)

    def attention(pairs, parts, project, bias_of, bias_done, scores, chunks, probs, transposed, value_pair, values, dst,
                  side=None):
        def one_pair(n, even, ahead, further):
            if even:
                st["slot"] = slot0
            finish = side(n) if side else None
            p.wait("pe", p.at(evac[st["set"] ^ 1]), p.at(bias_done))
            tS = [p.up(scores(AB[i], i // 2, i % 2), "done_pe") for i in range(4)]
            if ahead:
                bias_of(n + 1, [tS[3]])
            if further:
                stage(parts(n + 2))
            dst_v, src_v = value_pair(n)
            dve(V.tensor_copy, dst_v, src_v, after=[tS[0]])
            sums = lambda i: small[:, 24 + i:25 + i]
            tE = []
            for i in range(4):
                w_ = chunks(i % 2) * P
                nmx = small[:, 20 + i:21 + i]
                t = dve(V.tensor_reduce, nmx, AB[i][:, 0:w_], axis=AX.X, op=ALU.max, negate=True, after=[tS[i]])
                tE.append(act(probs[i][:, 0:w_], AB[i][:, 0:w_], ACT.Exp, bias=nmx, accum_out=sums(i), after=[t]))
                if i and st["side"]:
                    st["side"].pop(0)()
            tN = []
            for i in range(4):
                w_ = chunks(i % 2) * P
                t = dve(V.reciprocal, sums(i), sums(i), after=[tE[i]])
                tN.append(dve(V.tensor_scalar, probs[i][:, 0:w_], probs[i][:, 0:w_], sums(i), None, ALU.mult, after=[t]))
            if ahead:
                project(n + 1)
            tT = []
            for i in range(4):
                p.wait("pe", tN[i])
                for s_ in range(chunks(i % 2)):
                    m = TE.transpose(AB[i][:, s_ * P:(s_ + 1) * P], probs[i][:, s_ * P:(s_ + 1) * P], ident)
                t = p.up(m, "done_pe")
                d_, s_ = transposed(i // 2, i % 2, AB[i])
                tT.append(act(d_, s_, ACT.Copy, after=[t]) if i % 2 else dve(V.tensor_copy, d_, s_, after=[t]))
                if st["side"]:
                    st["side"].pop(0)()
            bank, raised = GB[st["set"]][0][:, 0:T], evac[st["set"]]
            for e in range(2):
                p.wait("pe", *tT[2 * e:2 * e + 2], p.at(raised))
                m = values(bank, e)
            t = p.up(m, "done_pe")
            ob = stat[0][:, 0:T]
            t = dve(V.tensor_copy, ob, bank, after=[t, *p.now("act")], also=raised)
            hi, lo = (x[:, bass.ds(n, 1), :].rearrange("p a t -> p (a t)") for x in dst)
            split(ob, hi, lo, [t], settled=True)
            if finish:
                while st["side"]:
                    st["side"].pop(0)()
                finish()
        bias_of(0, p.now("pe"))
        slot0 = st["slot"]
        stage(parts(0))
        stage(parts(1))
        project(0)
        turns = pairs // 2 - 1
        with p.loop(turns) as i:
            for e in range(2):
                one_pair(i * 2 + e, e == 0, True, True)
        for e in range(2):
            one_pair(2 * turns + e, e == 0, e == 0, False)

    with p.loop(2) as half:
        modulation_of(0, half)
        tail(0, half, a["ffn_w13"][0], a["ffn_w2"][0], lambda q: side2(0, half * 4 + q))
    if upto == 2:
        dump(hb[:, 0, :, :]); return

    with ExitStack() as f:
        am = [sb(f, nm(), [P, KD, 2 * T], F32R) for _ in range(2)]
        tmp = [sb(f, nm(), [P, T]) for _ in range(2)]
        both_modulated(1, am, [x[:, :] for x in tmp])
        oc = [sb(f, nm(), [P, KD, T], F32R) for _ in range(2)]
        q = sb(f, nm(), [P, T])
        k_ = sb(f, nm(), [P, 2 * T])
        v = sb(f, "na_v", [P, 4, D])
        vp = sb(f, "na_v_pair", [P, 4, P])
        U = sb(f, "na_bias", [P, 2, 6, GRID])
        probs = [sq[:, 2 * i:2 * i + 2, :].rearrange("p a t -> p (a t)") for i in range(4)]
        PT = h.rearrange("p (e s) t -> p e s t", e=2)
        wq = wv(a["na_w_qkv"])

        def values(i):
            w = wview(st["staged"][0][1], KD, T)

            def compute(_, bank, __):
                for tt in range(4):
                    m = token_major(bank[tt // 2][:, (tt % 2) * T:(tt % 2 + 1) * T], w, 0, T, am, tt * P)
                return m

            def evacuate(bank, t, raised):
                for c in range(2):
                    dve(V.tensor_copy, v[:, 2 * c:2 * c + 2, bass.ds(i * T, T)],
                        bank[c][:, :].rearrange("p (a n) -> p a n", a=2), after=[t], also=raised if c else None)
            slab(compute, evacuate)
        stream(4, lambda i: [cols(wq, i * T + 2 * D, T)], values)

        u_sem = p.sem("na_bias_arrived")
        u_done = p.sem("na_bias_ready", "pool")
        p.wait("pool", bias_t)
        ex = exp_d[:, :, :].rearrange("c (g e j) k -> g c e j k", g=NA_H // 2, e=2)

        def na_bias(n, free):
            p.wait("pool", *free)
            for half in range(2):
                for e in range(2):
                    src = ex[bass.ds(n, 1), :, e, 1 - half:7 - half, :].rearrange("g c j k -> c (g j) k")
                    p.up(G.dma_start(U[half * GRID:(half + 1) * GRID, e, :, :], src), u_sem, 16)
            u = U[:, :, :, :].rearrange("p e j k -> p (e j) k")
            pool(G.tensor_tensor, out=u, in0=u, in1=bc(colwin, 12), op=ALU.add, after=[p.at(u_sem), tab_t], also=u_done)

        def na_project(n):
            w = wview(st["staged"][0][1], KD, T)

            def compute(_, bank, __):
                feature_major(bank[0][:, 0:T], w, 0, am, slice(0, T))
                return feature_major(bank[1][:, :], w, P, am, slice(0, 2 * T))

            def evacuate(bank, t, raised):
                t1 = act(k_[:, :], bank[1][:, :], ACT.Copy, after=[t])
                dve(V.tensor_scalar, q[:, :], bank[0][:, 0:T], (D // NA_H) ** -0.5, None, ALU.mult, after=[t, t1],
                    also=raised)
            slab(compute, evacuate)

        def na_scores(bank, e, tt):
            r_, jj = slice(e * GRID, e * GRID + GRID), 2 - 2 * tt
            TE.matmul(bank[:, :], q[r_, tt * P:(tt + 1) * P], k_[r_, :], start=True, stop=False)
            return TE.matmul(bank[:, 0:T], ident, U[:, e, jj:jj + 4, :].rearrange("p j k -> p (j k)"),
                             start=False, stop=True)

        def na_transposed(e, tt, bank):
            return PT[:, e, :, tt * P:(tt + 1) * P], bank[:, :].rearrange("p (s t) -> p s t", s=4)

        def na_values(bank, e):
            r_ = slice(e * GRID, e * GRID + GRID)
            for s_ in range(4):
                m = TE.matmul(bank[r_, 0:T], vp[:, s_, r_], PT[:, e, s_, :], start=s_ == 0, stop=s_ == 3)
            return m
        attention(NA_H // 2, lambda n: [cols(wq, n * P, P), cols(wq, n * P + D, P)], na_project, na_bias, u_done,
                  na_scores, lambda tt: 4, probs, na_transposed,
                  lambda n: (vp[:, :, :], v[:, :, bass.ds(n * P, P)]), na_values, oc, side2_of(1))
        hx = hb[:, 0, :, :]
        modulation_of(1, 0)
        dve(V.tensor_scalar, hx, hx, ALPHA, None, ALU.mult, after=[*p.now("dve")])
        p.wait("dve", *p.now("dve"))
        p.wait("pe", *p.now("dve"))
        def residual(src, wvw, kc, hx, gate_cols, scale=None):
            def one(i):
                w = wview(st["staged"][0][1], kc, T)

                def compute(_, bank, __):
                    for c in range(2):
                        m = feature_major(bank[0][:, c * T:(c + 1) * T], w, c * P, src, slice(0, T), kc=kc)
                    return m

                def evacuate(bank, t, raised):
                    for c in range(2):
                        n = i * 2 + c
                        dve(V.scalar_tensor_tensor, hx[:, n, :], bank[0][:, c * T:(c + 1) * T],
                            gate_cols[:, n:n + 1], hx[:, n, :], ALU.mult, ALU.add, after=[t],
                            also=raised if c else None)
                slab(compute, evacuate)
            stream(4, lambda i: [cols(wvw, i * T, T)], one)
        residual(oc, wv(a["na_w_out"]), KD, hx, cur[:, 2 * KD:3 * KD])
        p.fence()
    if upto == 3:
        dump(hb[:, 0, :, :]); return
    tail(1, 0, a["ffn_w13"][1], a["ffn_w2"][1])
    dve(V.tensor_copy, h[:, :, :], hb[:, 0, :, :], after=[*p.now("dve")])
    p.fence()
    b1.close()
    if upto == 4:
        dump(h); return

    b2 = ExitStack()
    NT2 = TRI * 2 + P + T + TRI * 2 + (NLEV - 1) * HALF + DA_H
    t2tab = sb(b2, "table2", [P, NT2])
    p.wait("sp", *[v for e in p.last for v in p.now(e)])
    tab2 = p.up(SY.dma_start(t2tab[:, :], a["table2"]), p.sem("table2_arrived"), 16)
    off = [0]

    def take(n):
        x = t2tab[:, off[0]:off[0] + n]
        off[0] += n
        return x
    da_dist, da_lnc, gt_m, le_m, incl, strict = (take(n) for n in (TRI, TRI, P, T, TRI, TRI))
    lev = [take(HALF) for _ in range(NLEV - 1)]
    slope = take(DA_H)
    for e in ("dve", "act", "pool", "pe"):
        p.wait(e, tab2)
    lng = sb(b2, "norm_gains", [P, 2, 3, KD])
    convw = sb(b2, "conv_taps", [P, 2, 4, 3, DN_H])
    for l in range(2):
        dve(V.tensor_copy, lng[:, l, :, :], par[:, 2, 9 * KD:15 * KD].rearrange("p (j l k) -> p l j k", j=3, l=2)[:, l])
        dve(V.tensor_copy, convw[:, l, :, :, :].rearrange("p j x h -> p (j x h)"), par[:, 4 + l, 0:96])
    dnn = par[:, 0, C_DNN:C_DNN + 2]
    gl = sb(b2, "gains_now", [P, 3, KD])
    dnn_now = sb(b2, "dn_norm_now", [P, 1])
    cw_l = sb(b2, "conv_now", [P, 4, 3, DN_H])
    p.fence()

    def rms_scale(hx, dst):
        for q in range(2):
            t = act(sq[:, 4 * q:4 * q + 4, :], hx[:, 4 * q:4 * q + 4, :], ACT.Square, after=[*p.now("dve")])
        p.wait("pe", t)
        t = column_sums(AB[0][:, 0:T], lambda k: sq[:, k, :], KD, T)
        return rsqrt(dst, AB[0][:, 0:T], 1.0 / D, RMS_EPS, [t])

    def normed(hx, j, am, tmp):
        t = rms_scale(hx, stat[0][:, 0:T])
        t = dve(V.tensor_tensor, sq[:, :, :], hx, bc(stat[0][:, 0:T], KD), ALU.mult, after=[t, *p.now("pe")])
        for k in range(KD):
            sh, sc = cur[:, 3 * j * KD + k:3 * j * KD + k + 1], cur[:, (3 * j + 1) * KD + k:(3 * j + 1) * KD + k + 1]
            split_affine(sq[:, k, :], sc, sh, am[0][:, k, :], am[1][:, k, :], tmp[k % 2][:, :], [t])
        p.wait("pe", *p.now("dve"))

    def lv(ap, l, pat="l (k p) n -> l p k n"):
        return ap.rearrange(pat, p=P)[bass.ds(l, 1)].rearrange("l p k n -> p (l k) n")

    def macaron(l, j, wg, wu, wd):
        with ExitStack() as f:
            am = [sb(f, nm(), [P, KD, T], F32R) for _ in range(2)]
            tmp = [sb(f, nm(), [P, T]) for _ in range(2)]
            normed(h, j, am, tmp)

            def out_one(c, psum, t, raised):
                hc = h[:, bass.ds(c, 1), :].rearrange("p a t -> p (a t)")
                g_ = small[:, 0:1]
                t0 = dve(V.tensor_copy, g_, cur[:, bass.ds(c + (3 * j + 2) * KD, 1)], after=[*p.now("dve")])
                dve(V.scalar_tensor_tensor, hc, psum, g_, hc, ALU.mult, ALU.add, after=[t, t0], also=raised)
            feed_forward([lv(wg, l), lv(wu, l)], lv(wd, l), am, out_one)
            p.fence()

    KB = DA_W // P
    conv_read = [p.sem(n, "act") for n in ("conv_qk_read", "conv_v_read")]
    prep_a, prep_d = p.sem("head_qk_ready", "act"), p.sem("head_steps_ready", "dve")
    head_done = [p.sem(f"head_done{b}", "dve") for b in range(2)]
    da_done = p.sem("da_bias_ready", "dve")

    def mixer(l):
        with ExitStack() as f:
            u = [sb(f, nm(), [P, KD, T], F32R) for _ in range(2)]
            tmp = [sb(f, nm(), [P, T]) for _ in range(2)]
            ya = sb(f, "branch_a", [P, KD, T])
            zo = sb(f, "dn_gate_out", [P, DN_H, T])
            beta = sb(f, "beta", [P, 2, DN_H])
            gdec = sb(f, "log_decay", [P, 2, DN_H])
            rk = sb(f, "key_scale", [P, 2, 2, DN_H])
            rqb = sb(f, "query_scale_beta", [P, 2, 2, DN_H])
            normed(h, 1, u, tmp)
            wi = lv(a["w_in_2"], l)
            stage([cols(wi, IN_BA, 2 * DN_H)])
            wba = wview(st["staged"][0][1], KD, 2 * DN_H)
            ba = sb(f, "beta_decay_in", [P, 2, 2 * DN_H])

            def compute(_, bank, __):
                for tt in range(2):
                    m = token_major(bank[0][:, tt * 16:(tt + 1) * 16], wba, 0, 16, u, tt * P)
                return m

            def evacuate(bank, t, raised):
                dve(V.tensor_copy, ba[:, :, :].rearrange("p a n -> p (a n)"), bank[0][:, 0:32], after=[t], also=raised)
            slab(compute, evacuate)
            act(beta[:, :, :], ba[:, :, 0:DN_H], ACT.Sigmoid, after=[*p.now("dve")])
            s0, s1, s2, s3, s4 = (small[:, 0:16], small[:, 16:32], small[:, 32:48], small[:, 48:64], stat[1][:, 0:16])
            r3 = lambda x: x.rearrange("p (a n) -> p a n", a=2)
            t = dve(V.tensor_tensor, r3(s0), ba[:, :, DN_H:2 * DN_H],
                    dtb[:, bass.ds(l, 1), :].broadcast_to([P, 2, DN_H]), ALU.add, after=[*p.now("dve")])
            chain = lambda op, *x, **k_: dve(op, *x, after=[*p.now("dve"), *p.now("act")], **k_)
            t = act(s1, s0, ACT.Abs, after=[*p.now("dve")])
            act(s1, s1, ACT.Exp, scale=-1.0, after=[t])
            chain(V.tensor_scalar, s2, s1, 2.0, None, ALU.add)
            chain(V.reciprocal, s2, s2)
            chain(V.tensor_tensor, s2, s2, s1, ALU.mult)
            chain(V.tensor_tensor, s3, s2, s2, ALU.mult)
            chain(V.tensor_scalar, s4, s3, 1.0 / 15, None, ALU.mult)
            for n in (13, 11, 9, 7, 5, 3):
                chain(V.scalar_tensor_tensor, s4, s4, 1.0 / n, s3, ALU.add, ALU.mult)
            chain(V.scalar_tensor_tensor, s4, s4, 1.0, s2, ALU.add, ALU.mult)
            chain(V.tensor_scalar, s0, s0, 0.0, None, ALU.max)
            chain(V.scalar_tensor_tensor, s4, s4, 2.0, s0, ALU.mult, ALU.add)
            act(s1[:, 0:DN_H], alog[:, bass.ds(l, 1), :].rearrange("p a n -> p (a n)"), ACT.Exp, after=[*p.now("dve")], settled=True)
            chain(V.scalar_tensor_tensor, gdec[:, :, :], r3(s4), -1.0, bc(s1[:, 0:DN_H], 2), ALU.mult, ALU.mult)
            p.fence()

            with ExitStack() as f2:
                vb = sb(f2, "dn_v_beta", [P, DN_H, 2, P])
                MT = sb(f2, "dn_m_t", [P, DN_H, TRI])
                Aqk = sb(f2, "dn_qk", [P, DN_H, TRI])
                with ExitStack() as f3:
                    qa = sb(f3, "dn_q", [P, DN_H, T])
                    ka = sb(f3, "dn_k", [P, DN_H, T])
                    with ExitStack() as f4:
                        cin = sb(f4, "conv_in", [P, 3, T + 3])
                        cy = sb(f4, "conv_out", [P, 3, T])
                        cw = sb(f4, "taps", [P, 4, 3])
                        dve(V.memset, cin[:, :, 0:3], 0.0)
                        p.fence()
                        row = lambda x, hd: x[:, bass.ds(hd, 1), 0:T].rearrange("p a t -> p (a t)")

                        def parts(hd, j):
                            c = (2 * D, IN_Z) if j else (0, D)
                            return [cols(wi, hd * P + c[0], P), cols(wi, hd * P + c[1], P)]

                        def convolve(xs, t, reader, raised=None):
                            for jj in range(4):
                                for x in xs:
                                    src, tap = cin[:, x, jj:jj + T], cw[:, jj, x:x + 1]
                                    if jj == 0:
                                        t1 = dve(V.tensor_scalar, cy[:, x, :], src, tap, None, ALU.mult, after=[*t, reader],
                                                 also=raised)
                                    else:
                                        t1 = dve(V.scalar_tensor_tensor, cy[:, x, :], src, tap, cy[:, x, :], ALU.mult,
                                                 ALU.add, after=[tt_[x]])
                                    tt_[x] = t1
                        tt_ = {}

                        def one(hd, j):
                            w = wview(st["staged"][0][1], KD, T)

                            def compute(_, bank, __):
                                for c in range(2):
                                    m = feature_major(bank[c][:, 0:T], w, c * P, u, slice(0, T))
                                return m

                            def evacuate(bank, t, raised):
                                silu = lambda dst, src, after, **k_: act(dst, src, ACT.Silu, after=after, settled=True, **k_)
                                if j == 0:
                                    t1 = dve(V.tensor_copy, cw[:, :, :],
                                             cw_l[:, :, :, bass.ds(hd, 1)].rearrange("p j x h -> p j (x h)"))
                                    dve(V.tensor_copy, cin[:, 0, 3:], bank[0][:, 0:T], after=[t])
                                    t2 = dve(V.tensor_copy, cin[:, 1, 3:], bank[1][:, 0:T], also=raised)
                                    convolve((0, 1), [t1, t2], p.at(conv_read[0]))
                                    silu(row(qa, hd), cy[:, 0, :], [tt_[1]])
                                    silu(row(ka, hd), cy[:, 1, :], [], also=conv_read[0])
                                else:
                                    t2 = dve(V.tensor_copy, cin[:, 2, 3:], bank[0][:, 0:T], after=[t])
                                    t1 = silu(row(zo, hd), bank[1][:, 0:T], [t])
                                    convolve((2,), [t1, t2], p.at(conv_read[1]), raised)
                                    silu(row(Aqk, hd), cy[:, 2, :], [tt_[2]], also=conv_read[1])
                            slab(compute, evacuate)

                        def two_heads(i, last):
                            for j in range(4):
                                if j < 3:
                                    stage(parts(i * 2 + (j + 1) // 2, (j + 1) % 2))
                                elif not last:
                                    stage(parts(i * 2 + 2, 0))
                                one(i * 2 + j // 2, j % 2)
                        stage(parts(0, 0))
                        with p.loop(DN_H // 2 - 1) as i:
                            two_heads(i, False)
                        two_heads(DN_H // 2 - 1, True)
                    p.wait("pe", *p.now("act"))
                    for n in range(4):
                        tt, h0 = n // 2, (n % 2) * 4
                        for i in range(4):
                            m = TE.transpose(AB[n][:, i * P:(i + 1) * P], Aqk[:, h0 + i, tt * P:(tt + 1) * P], ident)
                        t = p.up(m, "done_pe")
                        dve(V.tensor_tensor, vb[:, h0:h0 + 4, tt, :], AB[n][:, :].rearrange("p (a n) -> p a n", a=4),
                            beta[:, tt, h0:h0 + 4].unsqueeze(2).broadcast_to([P, 4, P]), ALU.mult, after=[t])
                    for n, src in enumerate((qa, ka)):
                        t = act(sq[:, :, :], src[:, :, :], ACT.Square, after=[*p.now("pe"), *p.now("act")])
                        p.wait("pe", t)
                        for tt in range(2):
                            for hh in range(DN_H):
                                c = (n * 2 + tt) * DN_H + hh
                                m = TE.matmul(banks[0][:, c:c + 1], sq[:, hh, tt * P:(tt + 1) * P], ones[:, 0:1],
                                              start=True, stop=True)
                        t = p.up(m, "done_pe")
                    fl4 = lambda x: x.rearrange("p a b n -> p (a b n)")
                    t = rsqrt(fl4(rk[:, :, :, :]), banks[0][:, 0:4 * DN_H], 1.0, RMS_EPS, [t])
                    dve(V.tensor_scalar, rqb[:, 0, :, :], rk[:, 0, :, :], P ** -0.5, None, ALU.mult, after=[t])
                    dve(V.tensor_tensor, rqb[:, 1, :, :], rk[:, 1, :, :], beta[:, :, :], ALU.mult, after=[t])
                    p.fence()
                    with ExitStack() as f4:
                        two_of = lambda name, shape: [sb(f4, f"{name}{b}", shape) for b in range(2)]
                        G0, E = two_of("decay_steps", [P, TRI]), two_of("decay_exp", [P, TRI])
                        Eb = [two_of(f"decay_masked{n}", [P, TRI]) for n in range(2)]
                        sc = two_of("head_scalars", [P, 2, 4])
                        qh = two_of("head_qk", [P, 2, T])
                        bank_of = [AB, banks[0:4]]

                        def prepare(hd, b):
                            one_h, free = bass.ds(hd, 1), p.at(head_done[b])
                            for n, x in enumerate((gdec[:, :, one_h], rk[:, 1, :, one_h], rqb[:, 0, :, one_h],
                                                   rqb[:, 1, :, one_h])):
                                t = dve(V.tensor_copy, sc[b][:, :, n:n + 1], x, after=[free])
                            act(qh[b][:, 0, :], qa[:, one_h, :].rearrange("p a t -> p (a t)"), ACT.Copy, after=[free],
                                settled=True)
                            act(qh[b][:, 1, :], ka[:, one_h, :].rearrange("p a t -> p (a t)"), ACT.Copy, also=prep_a)
                            dve(V.tensor_scalar, G0[b][:, 0:T], le_m, sc[b][:, 0, 0:1], None, ALU.mult, after=[t])
                            dve(V.tensor_scalar, G0[b][:, T:TRI], le_m[:, 0:P], sc[b][:, 1, 0:1], None, ALU.mult, also=prep_d)

                        def one_head(hd, b, last):
                            one_h, bank = bass.ds(hd, 1), bank_of[b]
                            p.wait("pe", p.at(prep_d), p.at(head_done[b]))
                            TE.matmul(bank[0][:, 0:T], gt_m, G0[b][:, 0:T], start=True, stop=False)
                            TE.matmul(bank[0][:, P:T], ones, G0[b][:, T:TRI], start=False, stop=True)
                            m = TE.matmul(bank[0][:, T:TRI], gt_m, G0[b][:, T:TRI], start=True, stop=True)
                            tD = p.up(m, "done_pe")
                            for n in range(2):
                                for tt in range(2):
                                    m = TE.matmul(bank[1][:, (2 * n + tt) * P:(2 * n + tt + 1) * P],
                                                  sc[b][:, tt, 2 + n:3 + n].broadcast_to([P, P]), ident, start=True, stop=True)
                            p.wait("pe", p.at(prep_a))
                            kk = qh[b][:, 1, :]
                            for n in range(2):
                                TE.matmul(bank[2 + n][:, 0:T], kk[:, 0:P], qh[b][:, n, :], start=True, stop=True)
                                m = TE.matmul(bank[2 + n][:, T:TRI], kk[:, P:T], qh[b][:, n, P:T], start=True, stop=True)
                            tK = p.up(m, "done_pe")
                            if not last:
                                prepare(hd + 1, 1 - b)
                            t = act(E[b][:, :], bank[0][:, 0:TRI], ACT.Exp, after=[tD])
                            for n, mask in ((0, incl), (1, strict)):
                                dst, Em = (Aqk, MT)[n], Eb[n][b]
                                t1 = pool(G.tensor_tensor, out=Em[:, :], in0=E[b][:, :], in1=mask, op=ALU.mult, after=[t])
                                fac = bank[1][:, n * T:(n + 1) * T]
                                dve(V.tensor_tensor, Em[:, 0:T], Em[:, 0:T], fac, ALU.mult, after=[t1, tK])
                                t2 = dve(V.tensor_tensor, Em[:, T:TRI], Em[:, T:TRI], fac[:, P:T], ALU.mult)
                                for tt, s_ in ((0, slice(0, T)), (1, slice(T, TRI))):
                                    dve(V.scalar_tensor_tensor, dst[:, one_h, s_].rearrange("p a t -> p (a t)"),
                                        bank[2 + n][:, s_], sc[b][:, tt, 1:2], Em[:, s_], ALU.mult, ALU.mult, after=[t2],
                                        also=head_done[b] if n and tt else None)
                        prepare(0, 0)
                        with p.loop(DN_H // 2 - 1) as i:
                            for b in range(2):
                                one_head(i * 2 + b, b, False)
                        for b in range(2):
                            one_head(DN_H - 2 + b, b, b == 1)
                        p.fence()
                with ExitStack() as f3:
                    XT = sb(f3, "inv_t", [P, 2, DN_H, P])
                    Xc = sb(f3, "inv_tiles", [P, 2, DN_H, HALF])
                    XTc = sb(f3, "inv_tiles_t", [P, 2, DN_H, HALF])
                    Y = [sb(f3, nm(), [P, DN_H, HALF]) for _ in range(2)]
                    fl = lambda x: x.rearrange("p a t -> p (a t)")
                    rows_of = [slice(0, HALF), slice(HALF, P)]
                    blk = [slice(i * HALF, (i + 1) * HALF) for i in range(DN_H)]

                    def each_tile(bank, lhs, rhs):
                        p.settle("pe")
                        for r_ in rows_of:
                            for i in range(DN_H):
                                m = TE.matmul(bank[r_, blk[i]], lhs(i, r_), rhs(i, r_), start=True, stop=True)
                        return p.up(m, "done_pe")
                    joined = []
                    for tt in range(2):
                        for r_ in rows_of:
                            t = dve(V.tensor_tensor, XTc[r_, tt], MT[r_, :, tt * T + r_.start:tt * T + r_.stop],
                                    lev[0][r_, :].unsqueeze(1).broadcast_to([HALF, DN_H, HALF]), ALU.mult)
                        for r_ in rows_of:
                            t = dve(V.tensor_tensor, XTc[r_, tt], ident[r_, r_].unsqueeze(1).broadcast_to([HALF, DN_H, HALF]),
                                    XTc[r_, tt], ALU.subtract, after=[t])
                        p.wait("pe", t)
                        t = each_tile(AB[2 * tt], lambda i, r_: XTc[r_, tt, i, :], lambda i, r_: ident[r_, r_])
                        joined.append(act(fl(Xc[:, tt]), AB[2 * tt][:, :], ACT.Copy, after=[t]))
                    for j in range(1, NLEV - 1):
                        ty = []
                        for tt in range(2):
                            p.wait("pe", joined[tt])
                            t = each_tile(AB[2 * tt], lambda i, r_: MT[r_, i, tt * T + r_.start:tt * T + r_.stop],
                                          lambda i, r_: Xc[r_, tt, i, :])
                            ty.append(dve(V.tensor_tensor, Y[tt][:, :, :], AB[2 * tt][:, :].rearrange("p (a n) -> p a n", a=DN_H),
                                          bc(lev[j], DN_H), ALU.mult, after=[t]))
                        for tt in range(2):
                            p.wait("pe", ty[tt])
                            t1 = each_tile(AB[2 * tt + 1], lambda i, r_: XTc[r_, tt, i, :], lambda i, r_: Y[tt][r_, i, :])
                            t2 = each_tile(banks[2 * tt], lambda i, r_: Y[tt][r_, i, :], lambda i, r_: XTc[r_, tt, i, :])
                            x, xt = fl(Xc[:, tt]), fl(XTc[:, tt])
                            dve(V.tensor_tensor, x, x, AB[2 * tt + 1][:, :], ALU.subtract, after=[t1])
                            joined[tt] = dve(V.tensor_tensor, xt, xt, banks[2 * tt][:, :], ALU.subtract, after=[t2])
                    top, low = rows_of
                    t = pool(G.memset, XT[low, :, :, 0:HALF], 0.0, settled=True)
                    for tt in range(2):
                        p.wait("pe", joined[tt])
                        p.settle("pe")
                        for i in range(DN_H):
                            m = TE.matmul(AB[2 * tt][low, blk[i]], MT[top, i, tt * T + HALF:tt * T + P], Xc[top, tt, i, :],
                                          start=True, stop=True)
                        t = p.up(m, "done_pe")
                        ty[tt] = act(fl(Y[tt])[low, :], AB[2 * tt][low, :], ACT.Copy, after=[t])
                        for r_ in rows_of:
                            dve(V.tensor_copy, XT[r_, tt, :, r_], XTc[r_, tt], after=[joined[tt]])
                    for tt in range(2):
                        p.wait("pe", ty[tt])
                        p.settle("pe")
                        for i in range(DN_H):
                            m = TE.matmul(AB[2 * tt + 1][top, blk[i]], Y[tt][low, i, :], XTc[low, tt, i, :],
                                          start=True, stop=True)
                        t = p.up(m, "done_pe")
                        dve(V.tensor_scalar, XT[top, tt, :, low], AB[2 * tt + 1][top, :].rearrange("p (a n) -> p a n", a=DN_H),
                            -1.0, None, ALU.mult, after=[t])
                    p.fence()
                    vn = [sb(f3, nm(), [P, 4, P]) for _ in range(2)]
                    for gi in range(2):
                        h0 = 4 * gi
                        for i in range(4):
                            m = TE.matmul(AB[0][:, i * P:(i + 1) * P], XT[:, 0, h0 + i, :], vb[:, h0 + i, 0, :],
                                          start=True, stop=True)
                        t = p.up(m, "done_pe")
                        t = act(fl(vn[0][:, :, :]), AB[0][:, :], ACT.Copy, after=[t])
                        p.wait("pe", t)
                        for i in range(4):
                            m = TE.matmul(AB[1][:, i * P:(i + 1) * P], MT[:, h0 + i, P:T], vn[0][:, i, :],
                                          start=True, stop=True)
                        t = p.up(m, "done_pe")
                        x = vb[:, h0:h0 + 4, 1, :]
                        t = dve(V.tensor_tensor, x, x, AB[1][:, :].rearrange("p (a n) -> p a n", a=4), ALU.subtract, after=[t])
                        p.wait("pe", t)
                        for i in range(4):
                            m = TE.matmul(AB[0][:, i * P:(i + 1) * P], XT[:, 1, h0 + i, :], vb[:, h0 + i, 1, :],
                                          start=True, stop=True)
                        t = p.up(m, "done_pe")
                        t = act(fl(vn[1][:, :, :]), AB[0][:, :], ACT.Copy, after=[t])
                        p.wait("pe", t)
                        for i in range(4):
                            bank = AB[2 + i // 2][:, (i % 2) * T:(i % 2 + 1) * T]
                            TE.matmul(bank, vn[0][:, i, :], Aqk[:, h0 + i, 0:T], start=True, stop=False)
                            m = TE.matmul(bank[:, P:T], vn[1][:, i, :], Aqk[:, h0 + i, T:TRI], start=False, stop=True)
                        t = p.up(m, "done_pe")
                        for i in range(2):
                            s2_ = sq[:, 2 * i:2 * i + 2, :].rearrange("p a t -> p (a t)")
                            t1 = act(s2_, AB[2 + i][:, :], ACT.Square, after=[t])
                            p.wait("pe", t1)
                            m = TE.matmul(AB[i][:, :], ones, s2_, start=True, stop=True)
                            t1 = p.up(m, "done_pe")
                            t1 = rsqrt(stat[i][:, :], AB[i][:, :], 1.0 / P, RMS_EPS, [t1])
                            t1 = dve(V.scalar_tensor_tensor, stat[i][:, :], AB[2 + i][:, :], dnn_now[:, 0:1], stat[i][:, :],
                                     ALU.mult, ALU.mult, after=[t1])
                            zz = fl(zo[:, h0 + 2 * i:h0 + 2 * i + 2, :])
                            dve(V.tensor_tensor, zz, zz, stat[i][:, :], ALU.mult, after=[t1])
                        p.fence()

            def project(src, wvw, kc, dst):
                def one(i):
                    w = wview(st["staged"][0][1], kc, T)

                    def compute(_, bank, __):
                        for c in range(2):
                            m = feature_major(bank[0][:, c * T:(c + 1) * T], w, c * P, src, slice(0, T), kc=kc)
                        return m

                    def evacuate(bank, t, raised):
                        dve(V.tensor_copy, dst[:, 2 * i:2 * i + 2, :].rearrange("p a t -> p (a t)"), bank[0][:, :],
                            after=[t], also=raised)
                    slab(compute, evacuate)
                stream(4, lambda i: [cols(wvw, i * T, T)], one)

            with ExitStack() as f2:
                os_ = [sb(f2, nm(), [P, KD, T], F32R) for _ in range(2)]
                for k in range(KD):
                    t = split(zo[:, k, :], os_[0][:, k, :], os_[1][:, k, :], [*p.now("dve")])
                p.wait("pe", t)
                project(os_, lv(a["w_a_2"], l), KD, ya)
                p.fence()
            yb = zo
            with ExitStack() as f2:
                ob = [sb(f2, nm(), [P, KB, T], F32R) for _ in range(2)]
                v = sb(f2, "da_v", [P, 2, DA_W])
                vp = sb(f2, "da_v_pair", [P, 2, P])
                qk = sb(f2, "da_qk", [P, 2, T])
                bias = sb(f2, "da_bias", [P, 2, TRI])
                probs = [sb(f2, nm(), [P, T]) for _ in range(4)]
                PT = sb(f2, "da_probs_t", [P, 2, TRI])
                sl = sb(f2, "slopes_now", [P, 2])

                def one(i):
                    w = wview(st["staged"][0][1], KD, T)

                    def compute(_, bank, __):
                        for tt in range(2):
                            m = token_major(bank[0][:, tt * T:(tt + 1) * T], w, 0, T, u, tt * P)
                        return m

                    def evacuate(bank, t, raised):
                        dve(V.tensor_copy, v[:, :, i * T:(i + 1) * T], bank[0][:, :].rearrange("p (a n) -> p a n", a=2),
                            after=[t], also=raised)
                    slab(compute, evacuate)
                stream(3, lambda i: [cols(wi, i * T + (IN_DA + 2 * DA_W), T)], one)

                def da_bias(n, free):
                    t = dve(V.tensor_copy, sl[:, :], slope[:, bass.ds(n * 2, 2)], after=[*p.now("dve")])
                    for e in range(2):
                        dve(V.scalar_tensor_tensor, bias[:, e, :], da_dist, sl[:, e:e + 1], da_lnc, ALU.mult, ALU.add,
                            after=[t, *free], also=da_done)

                def da_project(n):
                    w = wview(st["staged"][0][1], KD, T)

                    def compute(_, bank, __):
                        for c in range(2):
                            m = feature_major(bank[c][:, 0:T], w, c * P, u, slice(0, T))
                        return m

                    def evacuate(bank, t, raised):
                        t1 = act(qk[:, 1, :], bank[1][:, 0:T], ACT.Copy, after=[t])
                        dve(V.tensor_scalar, qk[:, 0, :], bank[0][:, 0:T], DA_DH ** -0.5, None, ALU.mult, after=[t, t1],
                            also=raised)
                    slab(compute, evacuate)

                def da_scores(bank, e, tt):
                    r_, n = slice(e * DA_DH, (e + 1) * DA_DH), (tt + 1) * P
                    TE.matmul(bank[:, 0:n], qk[r_, 0, tt * P:(tt + 1) * P], qk[r_, 1, 0:n], start=True, stop=False)
                    return TE.matmul(bank[:, 0:n], ident, bias[:, e, tt * P:tt * P + n], start=False, stop=True)

                def da_transposed(e, tt, bank):
                    return (PT[:, e, P:TRI], bank[:, 0:T]) if tt else (PT[:, e, 0:P], bank[:, 0:P])

                def da_values(bank, e):
                    r_ = slice(e * DA_DH, (e + 1) * DA_DH)
                    TE.matmul(bank[r_, 0:T], vp[:, 0, r_], PT[:, e, 0:T], start=True, stop=False)
                    return TE.matmul(bank[r_, P:T], vp[:, 1, r_], PT[:, e, T:TRI], start=False, stop=True)
                attention(KB, lambda n: [cols(wi, n * P + IN_DA, P), cols(wi, n * P + (IN_DA + DA_W), P)], da_project,
                          da_bias, da_done, da_scores, lambda tt: tt + 1, probs, da_transposed,
                          lambda n: (vp[:, :, :], v[:, :, bass.ds(n * P, P)]), da_values, ob)
                p.wait("pe", *p.now("dve"))
                project(ob, lv(a["w_b_2"], l), KB, yb)
                p.fence()
            with ExitStack() as f2:
                mg = [sb(f2, nm(), [P, KD, T], F32R) for _ in range(2)]
                sg = [sb(f2, nm(), [P, 2 * T]) for _ in range(2)]
                mt_ = [sb(f2, nm(), [P, T]) for _ in range(2)]

                def one(i):
                    q_ = st["set"]
                    w = wview(st["staged"][0][1], KD, T)

                    def compute(_, bank, __):
                        for c in range(2):
                            m = feature_major(bank[0][:, c * T:(c + 1) * T], w, c * P, u, slice(0, T))
                        return m

                    def evacuate(bank, t, raised):
                        s_ = sg[q_]
                        t1 = act(s_[:, :], bank[0][:, :], ACT.Sigmoid, after=[t])
                        dve(V.tensor_tensor, mt_[q_][:, :], s_[:, 0:T], ya[:, i, :], ALU.mult, after=[t1], also=raised)
                        t1 = dve(V.tensor_tensor, s_[:, T:2 * T], s_[:, T:2 * T], yb[:, i, :], ALU.mult)
                        t1 = dve(V.tensor_tensor, mt_[q_][:, :], mt_[q_][:, :], s_[:, T:2 * T], ALU.add, after=[t1])
                        split(mt_[q_][:, :], mg[0][:, i, :], mg[1][:, i, :], [t1])
                    slab(compute, evacuate)
                stream(KD, lambda i: [cols(wi, i * P + IN_GATE, P), cols(wi, i * P + (IN_GATE + D), P)], one)
                p.wait("pe", *p.now("dve"))
                wo = lv(a["w_o_2"], l)

                def two(i):
                    w = wview(st["staged"][0][1], KD, T)

                    def compute(_, bank, __):
                        for c in range(2):
                            m = feature_major(bank[0][:, c * T:(c + 1) * T], w, c * P, mg, slice(0, T))
                        return m

                    def evacuate(bank, t, raised):
                        for c in range(2):
                            n = 2 * i + c
                            dve(V.scalar_tensor_tensor, h[:, n, :], bank[0][:, c * T:(c + 1) * T],
                                cur[:, 5 * KD + n:5 * KD + n + 1], h[:, n, :], ALU.mult, ALU.add, after=[t],
                                also=raised if c else None)
                    slab(compute, evacuate)
                stream(4, lambda i: [cols(wo, i * T, T)], two)
                p.fence()

    n_layers = 2
    with p.loop(n_layers) as l:
        one_l = bass.ds(l, 1)
        dve(V.tensor_copy, gl[:, :, :], lng[:, one_l, :, :].rearrange("p a j k -> p (a j) k"))
        dve(V.tensor_copy, cw_l[:, :, :, :].rearrange("p j x h -> p (j x h)"),
            convw[:, one_l, :, :, :].rearrange("p a j x h -> p (a j x h)"))
        t = dve(V.tensor_copy, dnn_now[:, :], dnn[:, one_l])
        p.wait("dve", t)
        t = dve(V.tensor_copy, cur[:, :], mods2[:, one_l, :].rearrange("p a n -> p (a n)"), after=[*p.now("dve")])
        for j in range(3):
            sc_, gt_ = cur[:, (3 * j + 1) * KD:(3 * j + 2) * KD], cur[:, (3 * j + 2) * KD:(3 * j + 3) * KD]
            dve(V.scalar_tensor_tensor, sc_, sc_, 1.0, gl[:, j, :], ALU.add, ALU.mult, after=[t])
            if j != 1:
                dve(V.tensor_scalar, gt_, gt_, 0.5, None, ALU.mult, after=[t])
        p.fence()
        macaron(l, 0, a["ffn1_wg_2"], a["ffn1_wu_2"], a["ffn1_wd_2"])
        if upto != 5:
            mixer(l)
            macaron(l, 2, a["ffn2_wg_2"], a["ffn2_wu_2"], a["ffn2_wd_2"])
    if upto < 99:
        dump(h); return
    t = rms_scale(h, stat[0][:, 0:T])
    for k in range(KD):
        dve(V.scalar_tensor_tensor, h[:, k, :], h[:, k, :], par[:, 0, C_FIN + k:C_FIN + k + 1], stat[0][:, 0:T],
            ALU.mult, ALU.mult, after=[t])
    dump(h)
    b2.close()


USED = ["x", "c", "ctx", "c_ctx", "ada_w", "ada_b", "ln_g", "ln_b", "ffn_w13", "ffn_w2", "ret_w_in", "ret_decay",
        "ret_w_out", "na_w_qkv", "na_rpb", "na_w_out", "c_2", "ada_w_2", "ada_b_2", "ln_ffn1_2", "ln_mix_2",
        "ln_ffn2_2", "ffn1_wg_2", "ffn1_wu_2", "ffn1_wd_2", "w_in_2", "conv_w_2", "a_log_2", "dt_bias_2",
        "dn_norm_2", "w_a_2", "w_b_2", "w_o_2", "ffn2_wg_2", "ffn2_wu_2", "ffn2_wd_2", "final_norm_2"]


def program(nc, arrays, counted, upto=99):
    aps = {n: nc.dram_tensor("in_" + n, list(v.shape), F32, kind="ExternalInput").ap() for n, v in arrays.items()}
    out = nc.dram_tensor("hidden_out", [1, T, D], F32, kind="ExternalOutput").ap()
    build(nc, aps, out, counted, upto)


def kernel(**inputs):
    import concourse.bacc as _bacc
    from concourse.bass_utils import run_bass_kernel_spmd as _run

    arrays = {n: np.ascontiguousarray(inputs[n]) for n in USED}
    for n, t in enumerate(shape_tables()):
        arrays[f"table{n}"] = t
    counted = {}
    for _ in range(2):
        nc = _bacc.Bacc("TRN2", target_bir_lowering=False, num_devices=1)
        program(nc, arrays, counted)
    r = _run(nc, [{"in_" + n: v for n, v in arrays.items()}], core_ids=[0])
    return r.results[0]["hidden_out"]
```

```python
from contextlib import ExitStack, contextmanager

import numpy as np

import concourse.bass as bass
from concourse import mybir

F32 = mybir.dt.float32
F32R = mybir.dt.float32r
ALU = mybir.AluOpType
ACT = mybir.ActivationFunctionType
AX = mybir.AxisListType

P = 128
T = 256
D = 1024
KD = D // P
FF = 2816
KF = FF // P
ALPHA = float(4 ** 0.25)
LN_EPS = 1e-5
RMS_EPS = 1e-6
RING = 4
SIDE1 = 768
SIDE2 = 1152
SIDE_W = 2 * SIDE2
SLOT = 2048
RET_H, RET_DK, RET_DV = 4, 256, 512
NA_H, NA_COLS, GRID = 16, 31, 64
DN_H = 8
DA_H, DA_DH = 12, 64
DA_W = DA_H * DA_DH
HALF = P // 2
NLEV = 7
TRI = 3 * P

IN_Z, IN_BA = 3 * D, 4 * D
IN_DA = IN_BA + 2 * DN_H
IN_GATE = IN_DA + 3 * DA_W


def shape_tables():
    p = np.arange(P)
    t = np.arange(T)
    ident = np.eye(P)
    ones = np.ones((P, P))
    nf = RET_DK // 4
    inv = 10000.0 ** (-np.arange(nf, dtype=np.float32) / np.float32(nf))
    inv = inv.astype(np.float32)
    rows, cols = (t // GRID).astype(np.float32), (t % GRID).astype(np.float32)
    ang = np.concatenate([rows[:, None] * inv, cols[:, None] * inv], -1).astype(np.float32)
    cos, sin = np.cos(ang).T, np.sin(ang).T
    dist = np.concatenate([t[None, :] - (p[:, None] + P * i) + T for i in range(2)], 1)
    qc, kc = (p % GRID)[:, None], np.arange(GRID)[None, :]
    w0 = np.clip(qc - 8, 0, GRID - 16)
    win = np.where((kc >= w0) & (kc < w0 + 16), 0.0, -1e30)
    first = np.concatenate([ident, ones], 1)
    block1 = np.concatenate([cos, sin, dist, win], 1)

    d0 = p[:, None] - p[None, :]
    d1 = p[:, None] + P - np.arange(T)[None, :]
    dd = np.concatenate([d0, d1], 1)
    count = sum(((dd >= 0) & (dd % r == 0) & (dd // r <= P)).astype(float) for r in (1, 4, 16))
    lnc = np.where(count > 0, np.log(np.maximum(count, 1.0)), -1e30)
    dd = np.maximum(dd, 0)
    gt = (p[:, None] > p[None, :]).astype(float)
    le = (p[:, None] <= t[None, :]).astype(float)
    incl = np.concatenate([(p[:, None] <= t[None, :]), (p[:, None] <= p[None, :])], 1).astype(float)
    strict = np.concatenate([(p[:, None] < t[None, :]), (p[:, None] < p[None, :])], 1).astype(float)
    lev = []
    for j in range(NLEV - 1):
        row, col = (p % HALF)[:, None] >> j, np.arange(HALF)[None, :] >> j
        low = (row // 2 == col // 2) & (row % 2 == 1) & (col % 2 == 0)
        up_ = (row // 2 == col // 2) & (row % 2 == 0) & (col % 2 == 1)
        lev.append((low if j else up_).astype(float))
    slope = np.broadcast_to(-(2.0 ** (-8.0 * np.arange(1, DA_H + 1) / DA_H))[None, :], (P, DA_H))
    block2 = np.concatenate([dd, lnc, gt, le, incl, strict] + lev + [slope], 1)
    return [np.ascontiguousarray(x, dtype=np.float32) for x in (first, block1, block2)]


class Program:

    def __init__(self, nc, counted):
        self.nc = nc
        self.counted = counted
        self.base = {}
        self.sems = {}
        self.owner = {}
        self.last = {}
        self.loops = []
        self.n_loops = 0
        self.eng = {"pe": nc.tensor, "dve": nc.vector, "act": nc.scalar, "pool": nc.gpsimd, "sp": nc.sync}
        for engine in ("pe", "dve", "act", "pool"):
            self.sem("done_" + engine, engine)
            self.last[engine] = ("done_" + engine,)
            self.sem("settled_" + engine)
        self.sem("settled_sp")

    def sem(self, name, owner=None):
        self.sems[name] = self.nc.alloc_semaphore(name)
        self.base[name] = 0
        self.owner[name] = owner
        return name

    def at(self, name):
        v = self.base[name]
        for label, var in self.loops:
            k = self.counted.get((label, name), 0)
            if k:
                v = var * k + v
        return (name, v)

    def now(self, engine):
        return [self.at(name) for name in self.last[engine]]

    def wait(self, engine, *values):
        for v in values:
            if v is not None and not (isinstance(v[1], int) and v[1] <= 0):
                self.eng[engine].wait_ge(self.sems[v[0]], v[1])

    def up(self, ins, name, n=1):
        ins.then_inc(self.sems[name], n)
        self.base[name] += n
        if self.owner[name]:
            self.last[self.owner[name]] = (name,)
        return self.at(name)

    def settle(self, engine):
        self.eng[engine].sem_inc(self.sems["settled_" + engine], 1)

    def do(self, engine, issue, *args, after=(), also=None, settled=False, **kw):
        self.wait(engine, *after)
        if settled:
            self.settle(engine)
        return self.up(issue(*args, **kw), also or "done_" + engine)

    def fence(self):
        now = {e: self.now(e) for e in self.last}
        for e in now:
            self.wait(e, *[v for o in now for v in now[o]])

    @contextmanager
    def loop(self, n):
        label = self.n_loops
        self.n_loops += 1
        before = dict(self.base)
        if self.loops:
            for e in self.eng:
                self.settle(e)
        for e, names in self.last.items():
            self.last[e] = tuple(dict.fromkeys(names + self.counted.get((label, "last", e), ())))
        with self.nc.Fori(0, n) as var:
            self.loops.append((label, var))
            yield var
            self.loops.pop()
        for e, names in self.last.items():
            self.counted[(label, "last", e)] = names
        for name in self.base:
            k = self.base[name] - before.get(name, 0)
            self.counted[(label, name)] = k
            self.base[name] = before.get(name, 0) + k * n


def build(nc, a, out, slopes, upto=99):
    p = Program(nc, slopes)
    V, S, G, TE, SY = nc.vector, nc.scalar, nc.gpsimd, nc.tensor, nc.sync
    fixed = ExitStack()

    def sb(stack, name, shape, dt=F32):
        return stack.enter_context(nc.sbuf_tensor(name, shape, dt))

    dve = lambda issue, *x, **k: p.do("dve", issue, *x, **k)
    act = lambda *x, **k: p.do("act", S.activation, *x, **k)
    pool = lambda issue, *x, **k: p.do("pool", issue, *x, **k)

    raw = [sb(fixed, f"weights_raw{i}", [P, SLOT]) for i in range(RING)]
    w_hi = [sb(fixed, f"weights_hi{i}", [P, SLOT], F32R) for i in range(2)]
    w_lo = [sb(fixed, f"weights_lo{i}", [P, SLOT], F32R) for i in range(2)]
    h = sb(fixed, "hidden", [P, KD, T])[:, :, :]
    sq = sb(fixed, "squares", [P, KD, T])
    table0 = sb(fixed, "ident_ones", [P, 2 * P])
    ident, ones = table0[:, 0:P], table0[:, P:2 * P]
    par = sb(fixed, "vectors", [P, 6, P])
    cact = sb(fixed, "silu_c", [P, 3 * KD])
    mods1 = sb(fixed, "modulation_1", [P, 2, 6 * KD, 2])
    mods2 = sb(fixed, "modulation_2", [P, 2, 9 * KD])
    cur = sb(fixed, "modulation_now", [P, 9 * KD])
    stat = [sb(fixed, f"stat{i}", [P, 2 * T]) for i in range(3)]
    small = sb(fixed, "small", [P, 64])
    ret_dec = sb(fixed, "ret_decay", [P, 2 * RET_H])
    alog = sb(fixed, "a_log", [P, 2, DN_H])
    dtb = sb(fixed, "dt_bias", [P, 2, DN_H])

    banks = [nc.alloc_psum_tensor(f"bank{i}", [P, 512], F32) for i in range(8)]
    GB = [[banks[0], banks[1]], [banks[2], banks[3]]]
    AB = banks[4:8]

    arrived = [p.sem(f"weights_arrived{i}") for i in range(RING)]
    slot_read = [p.sem(f"slot_read{i}", "dve") for i in range(RING)]
    used = [p.sem(f"weights_used{i}", "pe") for i in range(2)]
    evac = [p.sem(f"evacuated{i}", "dve") for i in range(2)]
    vecs = p.sem("vectors_arrived")
    st = {"slot": 0, "pair": 0, "set": 0, "staged": [], "side": [], "ends": []}

    def load(parts):
        s = st["slot"]
        st["slot"] = (s + 1) % RING
        p.wait("sp", p.at(slot_read[s]))
        if p.loops:
            p.settle("sp")
        off = 0
        for ap in parts:
            kc, c = ap.shape[1], ap.shape[2]
            tot = sum(x.shape[2] for x in parts)
            dst = raw[s][:, 0:kc * tot].rearrange("p (k c) -> p k c", k=kc)[:, :, off:off + c]
            p.up(SY.dma_start(dst, ap), arrived[s], 16)
            off += c
        return s, parts[0].shape[1] * off

    def stage(parts):
        s, n = load(parts)
        b = st["pair"]
        st["pair"] = 1 - b
        hi, lo, src = w_hi[b][:, 0:n], w_lo[b][:, 0:n], raw[s][:, 0:n]
        t = act(hi, src, ACT.Copy, after=[p.at(arrived[s]), p.at(used[b])])
        dve(V.tensor_tensor, lo, src, hi.bitcast(F32), ALU.subtract, after=[t], also=slot_read[s])
        st["staged"].append((s, b, parts[0].shape[1]))

    def slab(compute, evacuate, keep_set=False, also_after=False):
        side_work()
        s, b, kc = st["staged"].pop(0)
        i = st["set"]
        p.wait("pe", p.at(slot_read[s]), p.at(evac[i]))
        w = [x[b][:, :].rearrange("p (k c) -> p k c", k=kc) if kc * (SLOT // kc) == SLOT
             else x[b][:, 0:kc * (SLOT // kc)].rearrange("p (k c) -> p k c", k=kc) for x in (w_hi, w_lo)]
        last = compute(w, GB[i], b)
        t = p.up(last, used[b])
        if not keep_set:
            st["set"] = 1 - i
            if st["side"] and st["side"][0] in st["ends"]:
                st["side"].pop(0)()
            evacuate(GB[i], t, evac[i])
        if also_after:
            side_work()
        return t

    def side_work(any_=False):
        if st["side"] and (any_ or st["side"][0] not in st["ends"]):
            st["side"].pop(0)()

    def wview(b, kc, c):
        return [x[b][:, 0:kc * c].rearrange("p (k c) -> p k c", k=kc) for x in (w_hi, w_lo)]

    def passes(out_, l, r, first, last):
        TE.matmul(out_, l[0], r[0], start=first, stop=False)
        TE.matmul(out_, l[0], r[1], start=False, stop=False)
        return TE.matmul(out_, l[1], r[0], start=False, stop=last)

    def feature_major(out_, w, c0, act_, toks, kc=KD, k0=0, first=True, last=True):
        for k in range(kc):
            m = passes(out_, [x[:, k, c0:c0 + P] for x in w], [x[:, k0 + k, toks] for x in act_],
                       first and k == 0, last and k == kc - 1)
        return m

    def token_major(out_, w, c0, c1, act_, tok0, kc=KD):
        for k in range(kc):
            m = passes(out_, [x[:, k, tok0:tok0 + P] for x in act_], [x[:, k, c0:c1] for x in w],
                       k == 0, k == kc - 1)
        return m

    def stream(n, parts, one, m=RING, side=None, staged=False, then=None):
        turns = (n - 1) // m
        if not staged:
            stage(parts(0))
        if turns >= 2:
            with p.loop(turns) as i:
                if side:
                    side(i)
                for j in range(m):
                    stage(parts(i * m + (j + 1)))
                    one(i * m + j)
                assert not st["side"]
            rest = range(turns * m, n)
        else:
            rest = range(n)
        for i in rest:
            if i + 1 < n:
                stage(parts(i + 1))
            elif then:
                then()
            one(i)

    def wv(ap):
        return ap.rearrange("(k p) n -> p k n", p=P)

    def cols(v, c0, n):
        return v[:, :, bass.ds(c0, n)]

    def vector_load(dst, src):
        return p.up(SY.dma_start(dst, src), vecs, 16)

    b1 = ExitStack()
    hb = sb(b1, "hidden_both", [P, 2, KD, T])
    t1tab = sb(b1, "table1", [P, 2 * T + 2 * T + GRID])
    pad = sb(b1, "rpb_rows", [NA_H * 7, 2 * GRID])
    side_w = sb(b1, "side_weights", [P, SIDE_W])
    side_acc = sb(b1, "side_sums", [P, 2 * SIDE1])

    f0 = ExitStack()
    rows = sb(f0, "vector_rows", [P, 6, P])
    groups = [
        [a["c"].rearrange("o (k p) -> (o k) p", p=P), a["c_ctx"].rearrange("(k p) -> k p", p=P),
         a["c_2"].rearrange("o (k p) -> (o k) p", p=P), a["ln_g"].rearrange("l j (k p) -> (l j k) p", p=P),
         a["ln_b"].rearrange("l j (k p) -> (l j k) p", p=P), a["final_norm_2"].rearrange("(k p) -> k p", p=P),
         a["dn_norm_2"]],
        [a["ada_b"].rearrange("l (k p) -> (l k) p", p=P)],
        [a["ada_b_2"][0:1].rearrange("l (k p) -> (l k) p", p=P), a["ln_ffn1_2"].rearrange("l (k p) -> (l k) p", p=P),
         a["ln_mix_2"].rearrange("l (k p) -> (l k) p", p=P), a["ln_ffn2_2"].rearrange("l (k p) -> (l k) p", p=P)],
        [a["ada_b_2"][1:2].rearrange("l (k p) -> (l k) p", p=P)] ,
        [a["conv_w_2"][0].rearrange("j (k p) -> (j k) p", p=P)],
        [a["conv_w_2"][1].rearrange("j (k p) -> (j k) p", p=P)],
    ]
    C_LNG, C_LNB, C_FIN, C_DNN = 24, 56, 88, 96
    vector_load(table0[:, :], a["table0"])
    vector_load(ret_dec[:, :], a["ret_decay"].rearrange("d h -> (d h)").partition_broadcast(P))
    vector_load(alog[:, :, :].rearrange("p l h -> p (l h)"), a["a_log_2"].rearrange("l h -> (l h)").partition_broadcast(P))
    vector_load(dtb[:, :, :].rearrange("p l h -> p (l h)"), a["dt_bias_2"].rearrange("l h -> (l h)").partition_broadcast(P))
    tok = sb(f0, "tokens", [P, 2, 2, D])
    x_in = p.sem("tokens_arrived")
    for g, srcs in enumerate(groups):
        r0 = 0
        for s_ in srcs:
            vector_load(rows[r0:r0 + s_.shape[0], g, :], s_)
            r0 += s_.shape[0]
    for half, src in enumerate((a["x"], a["ctx"])):
        p.up(SY.dma_start(tok[:, half, :, :], src[0].rearrange("(a p) n -> p a n", p=P)), x_in, 16)
    p.wait("pe", p.at(vecs))
    for g, srcs in enumerate(groups):
        r0 = sum(s_.shape[0] for s_ in srcs)
        t = p.do("pe", TE.transpose, AB[g % 4][:, 0:r0], rows[0:r0, g, :], ident[0:r0, 0:r0],
                 after=[*p.now("dve")] if g >= 4 else [])
        dve(V.tensor_copy, par[:, g, 0:r0], AB[g % 4][:, 0:r0], after=[t])
        if g == 0:
            act(cact[:, :], par[:, 0, 0:3 * KD], ACT.Silu, after=[*p.now("dve")])
    for e in ("dve", "act"):
        p.wait(e, p.at(vecs))

    def ada_first(wk, dst, bias):
        with ExitStack() as f:
            row = sb(f, "modulation_rows", [2, 2 * D])

            def one(n):
                s, _ = load([cols(wk, n * T, T)])
                i = st["set"]
                st["set"] = 1 - i
                ws = raw[s][:, :].rearrange("p (k c) -> p k c", k=KD)
                p.wait("pe", p.at(arrived[s]), p.at(slot_read[(s - 2) % RING]))
                for k in range(KD):
                    m = TE.matmul(GB[i][0][0:2, 0:T], cact[:, k:k + KD + 1:KD], ws[:, k, :], start=k == 0,
                                  stop=k == KD - 1)
                t = p.up(m, "done_pe")
                dve(V.tensor_copy, row[:, bass.ds(n * T, T)], GB[i][0][0:2, 0:T], after=[t], also=slot_read[s])
            p.wait("pe", *p.now("act"))
            with p.loop(2 * KD // 2 // RING) as i:
                for j in range(RING):
                    one(i * RING + j)
            p.wait("pe", *p.now("dve"))
            for n in range(2 * KD):
                m = TE.transpose(AB[0][:, 2 * n:2 * n + 2], row[:, n * P:(n + 1) * P], ident[0:2, 0:2])
            t = p.up(m, "done_pe")
            dve(V.tensor_tensor, dst, AB[0][:, 0:4 * KD].rearrange("p (n v) -> p n v", v=2),
                bias.unsqueeze(2).broadcast_to([P, 2 * KD, 2]), ALU.add, after=[t])
            p.fence()

    side_in = [p.sem(f"side_arrived{i}") for i in range(3)]
    side_read = [p.sem(f"side_read{i}", "dve") for i in range(3)]

    def side_steps(wk, c0, width, vec_cols):
        nb = 3 if width <= SIDE_W // 3 else 2

        def step(k):
            i = k % nb
            buf = side_w[:, i * (SIDE_W // nb):i * (SIDE_W // nb) + width]
            p.wait("sp", *[p.at(x) for x in (side_read[i:i + 1] if nb == 3 or k > 1 else side_read)])
            p.up(SY.dma_start(buf, wk[:, k, bass.ds(c0, width)]), side_in[i], 16)
            p.wait("dve", p.at(side_in[i]), *p.now("dve"), *p.now("pe") if k == 0 else [])
            for n, v in enumerate(vec_cols):
                acc, c = side_acc[:, n * width:(n + 1) * width], cact[:, v + k:v + k + 1]
                also = side_read[i] if n == len(vec_cols) - 1 else None
                if k == 0:
                    dve(V.tensor_scalar, acc, buf, c, None, ALU.mult, also=also)
                else:
                    dve(V.scalar_tensor_tensor, acc, buf, c, acc, ALU.mult, ALU.add, also=also)
        return [lambda k=k: step(k) for k in range(KD)]

    def side_finish(width, dst, bias):
        n = width // P
        bank, raised = GB[st["set"]][0], evac[st["set"]]
        p.wait("pe", *p.now("dve"))
        for v in range(len(dst)):
            for c in range(n):
                m = TE.matmul(bank[:, v * n + c:v * n + c + 1], side_acc[:, v * width + c * P:v * width + (c + 1) * P], ones[:, 0:1],
                              start=True, stop=True)
        t = p.up(m, "done_pe")
        for v, d_ in enumerate(dst):
            dve(V.tensor_tensor, d_, bank[:, v * n:(v + 1) * n], bias, ALU.add, after=[t], also=raised)

    def column_sums(bank, src, n, width):
        for k in range(n):
            m = TE.matmul(bank, ones, src(k), start=k == 0, stop=k == n - 1)
        return p.up(m, "done_pe")

    def rsqrt(dst, src, scale, eps, after):
        t = dve(V.tensor_scalar, dst, src, scale, eps, ALU.mult, ALU.add, after=after)
        t = act(dst, dst, ACT.Sqrt, after=[t])
        return dve(V.reciprocal, dst, dst, after=[t])

    def bc(x, n):
        return x.unsqueeze(1).broadcast_to([P, n, x.shape[1]])

    def layer_norm(hx, gcol, bcol):
        p.wait("pe", *p.now("dve"))
        t = column_sums(AB[0][:, 0:T], lambda k: hx[:, k, :], KD, T)
        t = dve(V.tensor_scalar, stat[0][:, 0:T], AB[0][:, 0:T], 1.0 / D, None, ALU.mult, after=[t])
        for q in range(2):
            x = hx[:, 4 * q:4 * q + 4, :]
            t = dve(V.tensor_tensor, x, x, bc(stat[0][:, 0:T], 4), ALU.subtract, after=[t])
            t2 = act(sq[:, 4 * q:4 * q + 4, :], x, ACT.Square, after=[t], settled=True)
        p.wait("pe", t2)
        t = column_sums(AB[1][:, 0:T], lambda k: sq[:, k, :], KD, T)
        t = rsqrt(stat[1][:, 0:T], AB[1][:, 0:T], 1.0 / D, LN_EPS, [t])
        for q in range(2):
            x = hx[:, 4 * q:4 * q + 4, :]
            t2 = dve(V.tensor_tensor, x, x, bc(stat[1][:, 0:T], 4), ALU.mult, after=[t])
        for k in range(KD):
            t = dve(V.tensor_scalar, hx[:, k, :], hx[:, k, :], gcol[:, k:k + 1], bcol[:, k:k + 1],
                    ALU.mult, ALU.add, after=[t2])
        return t

    def split_affine_chunks(chunks, after):
        late = None
        for n, (x, scale, shift, hi, lo) in enumerate(chunks):
            th = act(hi, x, ACT.Identity, scale=scale, bias=shift, after=after, settled=True)
            t = dve(V.tensor_scalar, sq[:, n, :], x, scale, shift, ALU.mult, ALU.add, after=after)
            if late:
                dve(V.tensor_tensor, *late[0], ALU.subtract, after=late[1])
            late = ((lo, sq[:, n, :], hi.bitcast(F32)), [t, th])
        return dve(V.tensor_tensor, *late[0], ALU.subtract, after=late[1])

    def split(x, hi, lo, after, settled=False):
        th = act(hi, x, ACT.Copy, after=after, settled=settled)
        return dve(V.tensor_tensor, lo, x, hi.bitcast(F32), ALU.subtract, after=[th])

    def gate_up_slab(gate_up, i):
        return [cols(g_, i * P, P) for g_ in gate_up]

    def feed_forward(gate_up, w_down, act_, out_one, side=None):
        with ExitStack() as f:
            mid = [sb(f, p_ + nm(), [P, KF, T], F32R) for p_ in ("ffn_hi", "ffn_lo")]
            gate = [sb(f, nm(), [P, T]) for _ in range(2)]
            prod = [sb(f, nm(), [P, T]) for _ in range(2)]

            def up_one(i):
                q = st["set"]
                b = st["staged"][0][1]
                w = wview(b, KD, T)

                def compute(_, bank, __):
                    for c in range(2):
                        m = feature_major(bank[0][:, c * T:(c + 1) * T], w, c * P, act_, slice(0, T))
                    return m

                def evacuate(bank, t, raised):
                    t1 = act(gate[q][:, :], bank[0][:, 0:T], ACT.Silu, after=[t])
                    t2 = dve(V.tensor_tensor, prod[q][:, :], gate[q][:, :], bank[0][:, T:2 * T], ALU.mult,
                             after=[t1], also=raised)
                    hi, lo = (x[:, bass.ds(i, 1), :].rearrange("p a t -> p (a t)") for x in mid)
                    split(prod[q][:, :], hi, lo, [t2], settled=True)
                slab(compute, evacuate, also_after=len(st["side"]) == KD)
            HK = KF // 2
            wd = [w_down[:, 0:HK, :], w_down[:, HK:KF, :]]

            def parts(i, j):
                return [cols(wd[j % 2], i * 2 * P + (j // 2) * P, P)]
            stream(KF, lambda i: gate_up_slab(gate_up, i), up_one, m=2 * RING if side else RING, side=side, staged=True,
                   then=lambda: stage(parts(0, 0)))
            p.wait("pe", *p.now("dve"))

            def four(i, nxt):
                for j in range(4):
                    if j < 3:
                        stage(parts(i, j + 1))
                    elif nxt is not None:
                        stage(parts(nxt, 0))
                    w = wview(st["staged"][0][1], HK, P)

                    def compute(_, bank, __):
                        return feature_major(bank[0][:, (j // 2) * T:(j // 2 + 1) * T], w, 0, mid, slice(0, T),
                                             kc=HK, k0=(j % 2) * HK, first=j % 2 == 0, last=j % 2 == 1)

                    def evacuate(bank, t, raised):
                        out_one(i * 2, bank[0][:, 0:T], t, None)
                        out_one(i * 2 + 1, bank[0][:, T:2 * T], t, raised)
                    if j == 3:
                        slab(compute, evacuate)
                    else:
                        slab(compute, None, keep_set=True, also_after=len(st["side"]) == KD)
            if side:
                for i in range(KD // 2):
                    if i % 2 == 0:
                        side(2 + i // 2)
                    four(i, i + 1 if i < KD // 2 - 1 else None)
                assert not st["side"]
            else:
                with p.loop(KD // 2 - 1) as i:
                    four(i, i + 1)
                four(KD // 2 - 1, None)

    names = [0]

    def nm():
        names[0] += 1
        return f"tmp{names[0]}"

    cosT, sinT, dist, colwin = t1tab[:, 0:T], t1tab[:, T:2 * T], t1tab[:, 2 * T:4 * T], t1tab[:, 4 * T:4 * T + GRID]
    tab_t = p.up(SY.dma_start(t1tab[:, :], a["table1"]), p.sem("table1_arrived"), 16)

    pad_d = nc.dram_tensor("rpb_padded", [NA_H, 7, 2 * GRID], F32)
    exp_d = nc.dram_tensor("rpb_expanded", [GRID, NA_H * 7, GRID], F32)
    bias_sem = p.sem("bias_tables")
    t = pool(G.memset, pad[:, :], 0.0)
    p.wait("pool", t)
    for hh in range(NA_H):
        t = p.up(G.dma_start(pad[hh * 7:hh * 7 + 7, GRID - 16:GRID - 16 + NA_COLS], a["na_rpb"][hh, 4:11, :]),
                 bias_sem, 16)
    p.wait("pool", t)
    t = p.up(G.dma_start(pad_d[:, :, :].rearrange("h j c -> (h j) c"), pad[:, :]), bias_sem, 16)
    p.wait("pool", t)
    with p.loop(GRID) as c:
        p.up(G.dma_start(exp_d[bass.ds(c, 1), :, :].rearrange("o r c -> (o r) c"),
                         pad_d[:, :, bass.ds(GRID - 1 - c, GRID)].rearrange("h j c -> (h j) c")), bias_sem, 16)
    bias_t = p.at(bias_sem)
    p.wait("pe", p.at(x_in))
    for half in range(2):
        for tt in range(2):
            for q in range(2):
                bank = AB[2 * tt + q]
                p.wait("pe", *p.now("dve"))
                for k in range(4):
                    m = TE.transpose(bank[:, k * P:(k + 1) * P], tok[:, half, tt, (4 * q + k) * P:(4 * q + k + 1) * P],
                                     ident)
                t = p.up(m, "done_pe")
                dve(V.tensor_copy, hb[:, half, 4 * q:4 * q + 4, tt * P:(tt + 1) * P],
                    bank[:, :].rearrange("p (k t) -> p k t", k=4), after=[t])
    p.fence()
    f0.close()

    def tail(layer, half, w13, w2, side=None):
        hx = sb_half(half)
        w13v = wv(w13)
        gate_up = [w13v[:, :, 0:FF], w13v[:, :, FF:2 * FF]]
        stage(gate_up_slab(gate_up, 0))
        gb = lambda c, j: par[:, 0, c + (layer * 2 + j) * KD:c + (layer * 2 + j + 1) * KD]
        t = layer_norm(hx, gb(C_LNG, 0), gb(C_LNB, 0))
        with ExitStack() as f:
            af = [sb(f, nm(), [P, KD, T], F32R) for _ in range(2)]
            t = split_affine_chunks([(hx[:, k, :], cur[:, 4 * KD + k:4 * KD + k + 1], cur[:, 3 * KD + k:3 * KD + k + 1],
                                      af[0][:, k, :], af[1][:, k, :]) for k in range(KD)],
                                    [*p.now("dve")])
            p.wait("pe", t)

            def out_one(c, psum, t, raised):
                hc = hx[:, bass.ds(c, 1), :].rearrange("p a t -> p (a t)")
                g_ = small[:, 0:1]
                t0 = dve(V.tensor_copy, g_, cur[:, bass.ds(c + 5 * KD, 1)], after=[*p.now("dve")])
                t0 = dve(V.tensor_scalar, hc, hc, ALPHA, None, ALU.mult)
                dve(V.scalar_tensor_tensor, hc, psum, g_, hc, ALU.mult, ALU.add, after=[t, t0], also=raised)
            feed_forward(gate_up, wv(w2), af, out_one, side)
        layer_norm(hx, gb(C_LNG, 1), gb(C_LNB, 1))
        p.fence()

    def sb_half(half):
        return hb[:, bass.ds(half, 1), :, :].rearrange("p a k t -> p (a k) t")

    def modulation_of(layer, vec, n=6):
        t = dve(V.tensor_copy, cur[:, 0:n * KD],
                mods1[:, layer, 0:n * KD, bass.ds(vec, 1)].rearrange("p c v -> p (c v)"), after=[*p.now("dve")])
        for c in (1, 4)[:n // 2]:
            t = dve(V.tensor_scalar, cur[:, c * KD:(c + 1) * KD], cur[:, c * KD:(c + 1) * KD], 1.0, None, ALU.add,
                    after=[t])
        return t

    def both_modulated(layer, am):
        for half in range(2):
            t = modulation_of(layer, half, 2)
            p.wait("dve", t, *p.now("act"))
            sl = slice(half * T, (half + 1) * T)
            split_affine_chunks([(hb[:, half, k, :], cur[:, KD + k:KD + k + 1], cur[:, k:k + 1],
                                  am[0][:, k, sl], am[1][:, k, sl]) for k in range(KD)], [t])
            p.fence()

    ada_first(wv(a["ada_w"][0]), mods1[:, 0, 0:2 * KD, :], par[:, 1, 0:2 * KD])
    with ExitStack() as f:
        am = [sb(f, nm(), [P, KD, 2 * T], F32R) for _ in range(2)]
        y = sb(f, "mixer_out", [P, KD, 2 * T])
        tmp = stat[1:3]
        both_modulated(0, am)
        dve(V.memset, y[:, :, :], 0.0)
        lg = small[:, 8:16]
        t = act(lg, ret_dec[:, :], ACT.Exp, after=[p.at(vecs)])
        dve(V.tensor_scalar, lg, lg, -1.0, None, ALU.mult, after=[t])
        Pc = sb(f, "ret_probs_ctx", [P, 2, T])
        Pm = sb(f, "ret_probs", [P, 4, T])
        o = sb(f, "ret_out", [P, 4, 2 * T])
        p.fence()
        wi = wv(a["ret_w_in"])
        with p.loop(RET_H) as hd:
            end, ends = None, []
            for layer, width, c0 in ((1, SIDE1, 0), (1, SIDE1, 0), (0, D // 2, 2 * KD), (0, D // 2, 2 * KD)):
                g_ = len(ends) % 2
                ends.append(0)
                nq = width // P
                chunk = (hd * 2 + g_) * nq + c0
                steps = side_steps(wv(a["ada_w"][layer]), chunk * P, width, (0, KD))
                if end:
                    st["side"].append(end)
                    st["ends"].append(end)
                st["side"] += [lambda x=steps[i:i + 2]: [y() for y in x] for i in (0, 2, 4, 6)]
                end = lambda layer=layer, width=width, chunk=chunk, nq=nq: side_finish(
                    width, [mods1[:, layer, bass.ds(chunk, nq), v_:v_ + 1].rearrange("p n v -> p (n v)")
                            for v_ in range(2)], par[:, 1, bass.ds(chunk + 6 * KD * layer, nq)])
            with ExitStack() as g1:
                q, k_ = (h[:, 4 * i:4 * i + 4, :].rearrange("p (c a) t -> p c (a t)", a=2) for i in range(2))
                v = sb(g1, nm(), [P, 4, RET_DV])
                stage([cols(wi, hd * RET_DK, RET_DK)])
                for which, dst in enumerate((q, k_)):
                    nxt = [cols(wi, hd * RET_DK + D, RET_DK)] if which == 0 else \
                          [cols(wi, hd * RET_DV + 2 * D, T)]
                    stage(nxt)
                    w = wview(st["staged"][0][1], KD, T)

                    def compute(_, bank, __):
                        for c in range(2):
                            m = feature_major(bank[c][:, :], w, c * P, am, slice(0, 2 * T))
                        return m

                    def evacuate(bank, t, raised):
                        for c in range(2):
                            act(dst[:, c, T:2 * T], bank[c][:, T:2 * T], ACT.Copy, after=[t])
                        x1, x2 = bank[0][:, 0:T], bank[1][:, 0:T]
                        A, B = tmp[0], tmp[1]
                        t1 = dve(V.tensor_tensor, A[:, 0:T], x1, cosT, ALU.mult, after=[t, tab_t, *p.now("dve"), *p.now("act")])
                        t1 = dve(V.tensor_tensor, A[:, T:2 * T], x2, sinT, ALU.mult)
                        t1 = dve(V.tensor_tensor, B[:, 0:T], x1, sinT, ALU.mult)
                        t1 = dve(V.tensor_tensor, B[:, T:2 * T], x2, cosT, ALU.mult)
                        dve(V.tensor_tensor, dst[:, 0, 0:T], A[:, 0:T], A[:, T:2 * T], ALU.subtract, after=[t1])
                        dve(V.tensor_tensor, dst[:, 1, 0:T], B[:, 0:T], B[:, T:2 * T], ALU.add,
                            after=[*p.now("act")], also=raised)
                    slab(compute, evacuate, also_after=True)
                for j in range(2):
                    if j == 0:
                        stage([cols(wi, hd * RET_DV + (2 * D + T), T)])
                    else:
                        stage([cols(wi, hd * RET_DV + 4 * D, T)])
                    w = wview(st["staged"][0][1], KD, T)

                    def compute(_, bank, __):
                        for tt in range(4):
                            m = token_major(bank[tt // 2][:, (tt % 2) * T:(tt % 2 + 1) * T], w, 0, T, am, tt * P)
                        return m

                    def evacuate(bank, t, raised):
                        for c in range(2):
                            dve(V.tensor_copy, v[:, 2 * c:2 * c + 2, j * T:(j + 1) * T],
                                bank[c][:, :].rearrange("p (a n) -> p a n", a=2), after=[t],
                                also=raised if c else None)
                    slab(compute, evacuate, also_after=True)
                lf = small[:, 16:17]
                lb = small[:, 17:18]
                t = dve(V.tensor_copy, lf, lg[:, bass.ds(hd, 1)], after=[*p.now("dve")])
                t = dve(V.tensor_scalar, lb, lg[:, bass.ds(hd + RET_H, 1)], -1.0, None, ALU.mult)
                A, B = tmp[0][:, :], tmp[1][:, :]
                self_, cross = (Pm[:, i:i + 2, :].rearrange("p a t -> p (a t)") for i in (0, 2))
                C, Pc_ = cross, Pc[:, :, :].rearrange("p a t -> p (a t)")
                dve(V.tensor_scalar, A, dist, -float(T), 0.0, ALU.add, ALU.max)
                dve(V.tensor_scalar, B, dist, -float(T), 0.0, ALU.add, ALU.min)
                t = dve(V.tensor_scalar, Pc_, dist, -2.0 * T, None, ALU.add, after=[*p.now("pe")])
                act(A, A, ACT.Exp, scale=lf, after=[t])
                act(B, B, ACT.Exp, scale=lb)
                act(Pc_, Pc_, ACT.Exp, scale=lb)
                decays = act(C, dist, ACT.Exp, scale=lf)
                dve(V.scalar_tensor_tensor, A, dist, float(T), A, ALU.is_ge, ALU.mult, after=[decays])
                t = dve(V.scalar_tensor_tensor, B, dist, float(T), B, ALU.is_le, ALU.mult)
                dve(V.tensor_tensor, self_, A, B, ALU.add, after=[t])
                dve(V.tensor_tensor, cross, C, Pc_, ALU.add)
                p.wait("pe", *p.now("dve"), *p.now("act"))
                for i in range(4):
                    for c in range(2):
                        m = TE.matmul(AB[i // 2][:, (i % 2) * T:(i % 2 + 1) * T], k_[:, c, i * P:(i + 1) * P],
                                      q[:, c, 0:T], start=c == 0, stop=c == 1)
                for i in range(2):
                    for c in range(2):
                        m = TE.matmul(AB[2][:, i * T:(i + 1) * T], k_[:, c, T + i * P:T + (i + 1) * P],
                                      q[:, c, T:2 * T], start=c == 0, stop=c == 1)
                t = p.up(m, "done_pe")
                fl = lambda x: x.rearrange("p a t -> p (a t)")
                dve(V.scalar_tensor_tensor, fl(Pc[:, :, :]), AB[2][:, :], RET_DK ** -0.5, self_, ALU.mult, ALU.mult,
                    after=[t])
                for i in range(2):
                    t = dve(V.scalar_tensor_tensor, fl(Pm[:, 2 * i:2 * i + 2, :]), AB[i][:, :], RET_DK ** -0.5,
                            fl(Pm[:, 2 * i:2 * i + 2, :]), ALU.mult, ALU.mult)
                p.wait("pe", t)
                for c in range(4):
                    for i in range(4):
                        TE.matmul(AB[c][:, 0:T], v[:, i, c * P:(c + 1) * P], Pm[:, i, :], start=i == 0, stop=i == 3)
                    for i in range(2):
                        m = TE.matmul(AB[c][:, T:2 * T], v[:, 2 + i, c * P:(c + 1) * P], Pc[:, i, :],
                                      start=i == 0, stop=i == 1)
                    t = p.up(m, "done_pe")
                    t1 = dve(V.tensor_copy, o[:, c, :], AB[c][:, :], after=[t])
                    t2 = act(sq[:, 2 * c:2 * c + 2, :].rearrange("p a t -> p (a t)"), o[:, c, :], ACT.Square, after=[t1])
                    side_work(True)
                p.wait("pe", t2)
                t = column_sums(AB[0][:, :], lambda k: sq[:, 2 * k:2 * k + 2, :].rearrange("p a t -> p (a t)"), 4, 512)
                t = rsqrt(stat[0][:, :], AB[0][:, :], 1.0 / RET_DV, RMS_EPS, [t])
                t = dve(V.tensor_tensor, o[:, :, :], o[:, :, :], bc(stat[0][:, :], 4), ALU.mult, after=[t])
            with ExitStack() as g2:
                z = [sb(g2, nm(), [P, 4, 2 * T], F32R) for _ in range(2)]
                wo = a["ret_w_out"].rearrange("(g k p) n -> g p k n", p=P, k=4)
                wo_h = wo[bass.ds(hd, 1), :, :, :].rearrange("g p k n -> p (g k) n")
                for j in range(2):
                    stage([cols(wi, hd * RET_DV + (4 * D + T), T)] if j == 0 else [cols(wo_h, 0, T)])
                    w = wview(st["staged"][0][1], KD, T)

                    def compute(_, bank, __):
                        for c in range(2):
                            m = feature_major(bank[c][:, :], w, c * P, am, slice(0, 2 * T))
                        return m

                    def evacuate(bank, t, raised):
                        for c in range(2):
                            A = tmp[c][:, :]
                            n = 2 * j + c
                            t1 = act(A, bank[c][:, :], ACT.Silu, after=[t, *p.now("dve")])
                            t1 = dve(V.tensor_tensor, A, A, o[:, n, :], ALU.mult, after=[t1],
                                     also=raised if c else None)
                            split(A, z[0][:, n, :], z[1][:, n, :], [t1])
                    slab(compute, evacuate, also_after=True)
                for j in range(4):
                    if j < 3:
                        stage([cols(wo_h, (j + 1) * T, T)])
                    w = wview(st["staged"][0][1], 4, T)
                    p.wait("pe", *p.now("dve")) if j == 0 else None

                    def compute(_, bank, __):
                        for c in range(2):
                            m = feature_major(bank[c][:, :], w, c * P, z, slice(0, 2 * T), kc=4)
                        return m

                    def evacuate(bank, t, raised):
                        for c in range(2):
                            yc = y[:, 2 * j + c, :]
                            dve(V.tensor_tensor, yc, yc, bank[c][:, :], ALU.add, after=[t],
                                also=raised if c else None)
                    slab(compute, evacuate)
            assert not st["side"]
            end()
            p.fence()
        for half in range(2):
            hx = hb[:, half, :, :]
            t = dve(V.tensor_scalar, hx, hx, ALPHA, None, ALU.mult, after=[*p.now("dve")])
            for k in range(KD):
                dve(V.scalar_tensor_tensor, hx[:, k, :], y[:, k, half * T:(half + 1) * T],
                    mods1[:, 0, 2 * KD + k, half:half + 1], hx[:, k, :], ALU.mult, ALU.add, after=[t])
        p.fence()

    def dump(src):
        with ExitStack() as f:
            rows_out = [sb(f, nm(), [P, D]) for _ in range(2)]
            for tt in range(2):
                for q in range(2):
                    p.wait("pe", *p.now("dve"))
                    for k in range(4):
                        m = TE.transpose(AB[2 * tt + q][:, k * P:(k + 1) * P], src[:, 4 * q + k, tt * P:(tt + 1) * P], ident)
                    t = p.up(m, "done_pe")
                    t = dve(V.tensor_copy, rows_out[tt][:, q * 512:(q + 1) * 512], AB[2 * tt + q][:, :], after=[t])
                p.wait("sp", t)
                p.up(SY.dma_start(out[0, tt * P:(tt + 1) * P, :], rows_out[tt][:, :]), stored, 16)
            p.wait("sp", p.at(stored))
            p.wait("pool", p.at(bias_sem))
    stored = p.sem("stored")

    if upto == 1:
        dump(hb[:, 0, :, :]); return
    SW = 9 * D // 8

    def side2(layer, block):
        steps = side_steps(wv(a["ada_w_2"][layer]), block * SW, SW, (2 * KD,))
        n = SW // P

        def finish():
            side_finish(SW, [mods2[:, layer, bass.ds(block * n, n)]], par[:, 2 + layer, bass.ds(block * n, n)])
        return steps, finish

    def add_side2(layer, block):
        assert not st["side"]
        steps, finish = side2(layer, block)
        st["ends"].append(finish)
        st["side"] = steps + [finish]

    def side2_of(layer):
        return lambda block: side2(layer, block)

    def attention(pairs, parts, project, bias_of, bias_done, scores, chunks, probs, transposed, value_pair, values, dst,
                  side=None, then=None):
        def one_pair(n, even, ahead, further):
            if even:
                st["slot"] = slot0
            p.wait("pe", p.at(evac[st["set"] ^ 1]), p.at(bias_done))
            tS = [p.up(scores(AB[i], i // 2, i % 2), "done_pe") for i in range(4)]
            if side:
                assert not st["side"]
                side(n)[1]()
                if ahead:
                    st["side"] = side(n + 1)[0]
            if ahead:
                bias_of(n + 1, [tS[3]])
            if further:
                stage(parts(n + 2))
            if then and not ahead:
                then()
            dst_v, src_v = value_pair(n)
            dve(V.tensor_copy, dst_v, src_v, after=[tS[0]])
            sums = lambda i: small[:, 24 + i:25 + i]
            tE = []
            for i in range(4):
                w_ = chunks(i % 2) * P
                nmx = small[:, 20 + i:21 + i]
                t = dve(V.tensor_reduce, nmx, AB[i][:, 0:w_], axis=AX.X, op=ALU.max, negate=True, after=[tS[i]])
                tE.append(act(probs[i][:, 0:w_], AB[i][:, 0:w_], ACT.Exp, bias=nmx, accum_out=sums(i), after=[t]))
                if i and st["side"]:
                    st["side"].pop(0)()
            tN = []
            for i in range(4):
                w_ = chunks(i % 2) * P
                t = dve(V.reciprocal, sums(i), sums(i), after=[tE[i]])
                tN.append(dve(V.tensor_scalar, probs[i][:, 0:w_], probs[i][:, 0:w_], sums(i), None, ALU.mult, after=[t]))
            if ahead:
                project(n + 1)
            tT = []
            for i in range(4):
                p.wait("pe", tN[i])
                for s_ in range(chunks(i % 2)):
                    m = TE.transpose(AB[i][:, s_ * P:(s_ + 1) * P], probs[i][:, s_ * P:(s_ + 1) * P], ident)
                t = p.up(m, "done_pe")
                d_, s_ = transposed(i // 2, i % 2, AB[i])
                tT.append(act(d_, s_, ACT.Copy, after=[t]) if i % 2 else dve(V.tensor_copy, d_, s_, after=[t]))
                if st["side"]:
                    st["side"].pop(0)()
            bank, raised = GB[st["set"]][0][:, 0:T], evac[st["set"]]
            for e in range(2):
                p.wait("pe", *tT[2 * e:2 * e + 2], p.at(raised))
                m = values(bank, e)
            t = p.up(m, "done_pe")
            ob = stat[0][:, 0:T]
            t = dve(V.tensor_copy, ob, bank, after=[t, *p.now("act")], also=raised)
            hi, lo = (x[:, bass.ds(n, 1), :].rearrange("p a t -> p (a t)") for x in dst)
            split(ob, hi, lo, [t], settled=True)
        bias_of(0, p.now("pe"))
        slot0 = st["slot"]
        stage(parts(0))
        stage(parts(1))
        project(0)
        turns = pairs // 2 - 1
        with p.loop(turns) as i:
            for e in range(2):
                one_pair(i * 2 + e, e == 0, True, True)
        for e in range(2):
            one_pair(2 * turns + e, e == 0, e == 0, False)

    with p.loop(2) as half:
        modulation_of(0, half)
        tail(0, half, a["ffn_w13"][0], a["ffn_w2"][0], lambda q: add_side2(0, half * 4 + q))
    if upto == 2:
        dump(hb[:, 0, :, :]); return

    with ExitStack() as f:
        am = [sb(f, nm(), [P, KD, 2 * T], F32R) for _ in range(2)]
        both_modulated(1, am)
        oc = [sb(f, nm(), [P, KD, T], F32R) for _ in range(2)]
        q = sb(f, nm(), [P, T])
        k_ = sb(f, nm(), [P, 2 * T])
        v = sb(f, "na_v", [P, 4, D])
        vp = sb(f, "na_v_pair", [P, 4, P])
        U = sb(f, "na_bias", [P, 2, 6, GRID])
        probs = [sq[:, 2 * i:2 * i + 2, :].rearrange("p a t -> p (a t)") for i in range(4)]
        PT = h.rearrange("p (e s) t -> p e s t", e=2)
        wq, w_out = wv(a["na_w_qkv"]), wv(a["na_w_out"])

        def values(i):
            w = wview(st["staged"][0][1], KD, T)

            def compute(_, bank, __):
                for tt in range(4):
                    m = token_major(bank[tt // 2][:, (tt % 2) * T:(tt % 2 + 1) * T], w, 0, T, am, tt * P)
                return m

            def evacuate(bank, t, raised):
                for c in range(2):
                    dve(V.tensor_copy, v[:, 2 * c:2 * c + 2, bass.ds(i * T, T)],
                        bank[c][:, :].rearrange("p (a n) -> p a n", a=2), after=[t], also=raised if c else None)
            slab(compute, evacuate, also_after=True)
        st["side"] = side2(1, 0)[0]
        stream(4, lambda i: [cols(wq, i * T + 2 * D, T)], values)

        u_sem = p.sem("na_bias_arrived")
        u_done = p.sem("na_bias_ready", "pool")
        p.wait("pool", bias_t)
        ex = exp_d[:, :, :].rearrange("c (g e j) k -> g c e j k", g=NA_H // 2, e=2)

        def na_bias(n, free):
            p.wait("pool", *free)
            for half in range(2):
                for e in range(2):
                    src = ex[bass.ds(n, 1), :, e, 1 - half:7 - half, :].rearrange("g c j k -> c (g j) k")
                    p.up(G.dma_start(U[half * GRID:(half + 1) * GRID, e, :, :], src), u_sem, 16)
            u = U[:, :, :, :].rearrange("p e j k -> p (e j) k")
            pool(G.tensor_tensor, out=u, in0=u, in1=bc(colwin, 12), op=ALU.add, after=[p.at(u_sem), tab_t], also=u_done)

        def na_project(n):
            w = wview(st["staged"][0][1], KD, T)

            def compute(_, bank, __):
                feature_major(bank[0][:, 0:T], w, 0, am, slice(0, T))
                return feature_major(bank[1][:, :], w, P, am, slice(0, 2 * T))

            def evacuate(bank, t, raised):
                t1 = act(k_[:, :], bank[1][:, :], ACT.Copy, after=[t])
                dve(V.tensor_scalar, q[:, :], bank[0][:, 0:T], (D // NA_H) ** -0.5, None, ALU.mult, after=[t, t1],
                    also=raised)
            slab(compute, evacuate)

        def na_scores(bank, e, tt):
            r_, jj = slice(e * GRID, e * GRID + GRID), 2 - 2 * tt
            TE.matmul(bank[:, :], q[r_, tt * P:(tt + 1) * P], k_[r_, :], start=True, stop=False)
            return TE.matmul(bank[:, 0:T], ident, U[:, e, jj:jj + 4, :].rearrange("p j k -> p (j k)"),
                             start=False, stop=True)

        def na_transposed(e, tt, bank):
            return PT[:, e, :, tt * P:(tt + 1) * P], bank[:, :].rearrange("p (s t) -> p s t", s=4)

        def na_values(bank, e):
            r_ = slice(e * GRID, e * GRID + GRID)
            for s_ in range(4):
                m = TE.matmul(bank[r_, 0:T], vp[:, s_, r_], PT[:, e, s_, :], start=s_ == 0, stop=s_ == 3)
            return m
        attention(NA_H // 2, lambda n: [cols(wq, n * P, P), cols(wq, n * P + D, P)], na_project, na_bias, u_done,
                  na_scores, lambda tt: 4, probs, na_transposed,
                  lambda n: (vp[:, :, :], v[:, :, bass.ds(n * P, P)]), na_values, oc, side2_of(1),
                  then=lambda: stage([cols(w_out, 0, T)]))
        hx = hb[:, 0, :, :]
        modulation_of(1, 0)
        dve(V.tensor_scalar, hx, hx, ALPHA, None, ALU.mult, after=[*p.now("dve")])
        p.wait("dve", *p.now("dve"))
        p.wait("pe", *p.now("dve"))
        def residual(src, wvw, kc, hx, gate_cols, scale=None):
            def one(i):
                w = wview(st["staged"][0][1], kc, T)

                def compute(_, bank, __):
                    for c in range(2):
                        m = feature_major(bank[0][:, c * T:(c + 1) * T], w, c * P, src, slice(0, T), kc=kc)
                    return m

                def evacuate(bank, t, raised):
                    for c in range(2):
                        n = i * 2 + c
                        dve(V.scalar_tensor_tensor, hx[:, n, :], bank[0][:, c * T:(c + 1) * T],
                            gate_cols[:, n:n + 1], hx[:, n, :], ALU.mult, ALU.add, after=[t],
                            also=raised if c else None)
                slab(compute, evacuate)
            stream(4, lambda i: [cols(wvw, i * T, T)], one, staged=True)
        residual(oc, w_out, KD, hx, cur[:, 2 * KD:3 * KD])
        p.fence()
    if upto == 3:
        dump(hb[:, 0, :, :]); return
    tail(1, 0, a["ffn_w13"][1], a["ffn_w2"][1])
    dve(V.tensor_copy, h[:, :, :], hb[:, 0, :, :], after=[*p.now("dve")])
    p.fence()
    b1.close()
    if upto == 4:
        dump(h); return

    b2 = ExitStack()
    NT2 = TRI * 2 + P + T + TRI * 2 + (NLEV - 1) * HALF + DA_H
    t2tab = sb(b2, "table2", [P, NT2])
    p.wait("sp", *[v for e in p.last for v in p.now(e)])
    tab2 = p.up(SY.dma_start(t2tab[:, :], a["table2"]), p.sem("table2_arrived"), 16)
    off = [0]

    def take(n):
        x = t2tab[:, off[0]:off[0] + n]
        off[0] += n
        return x
    da_dist, da_lnc, gt_m, le_m, incl, strict = (take(n) for n in (TRI, TRI, P, T, TRI, TRI))
    lev = [take(HALF) for _ in range(NLEV - 1)]
    slope = take(DA_H)
    for e in ("dve", "act", "pool", "pe"):
        p.wait(e, tab2)
    lng = sb(b2, "norm_gains", [P, 2, 3, KD])
    convw = sb(b2, "conv_taps", [P, 2, 4, 3, DN_H])
    for l in range(2):
        dve(V.tensor_copy, lng[:, l, :, :], par[:, 2, 9 * KD:15 * KD].rearrange("p (j l k) -> p l j k", j=3, l=2)[:, l])
        dve(V.tensor_copy, convw[:, l, :, :, :].rearrange("p j x h -> p (j x h)"), par[:, 4 + l, 0:96])
    dnn = par[:, 0, C_DNN:C_DNN + 2]
    gl = sb(b2, "gains_now", [P, 3, KD])
    dnn_now = sb(b2, "dn_norm_now", [P, 1])
    cw_l = sb(b2, "conv_now", [P, 4, 3, DN_H])
    p.fence()

    square_sum = sb(b2, "square_sum", [P, T])
    square = sb(b2, "square", [P, T])
    square_read = p.sem("square_added", "pool")

    def add_square(hc):
        t = act(square[:, :], hc, ACT.Square, after=[*p.now("dve"), p.at(square_read)], settled=True)
        pool(G.tensor_tensor, out=square_sum[:, :], in0=square_sum[:, :], in1=square[:, :], op=ALU.add,
             after=[t, p.at(square_read)], also=square_read)

    def rms_scale(dst):
        p.wait("pe", *p.now("dve"), *p.now("act"), p.at(square_read))
        t = p.up(TE.matmul(AB[0][:, 0:T], ones, square_sum[:, :], start=True, stop=True), "done_pe")
        pool(G.memset, square_sum[:, :], 0.0, after=[t], also=square_read, settled=True)
        return rsqrt(dst, AB[0][:, 0:T], 1.0 / D, RMS_EPS, [t])

    def normed(hx, j, am):
        tr = rms_scale(stat[0][:, 0:T])
        ts = []
        for k in range(KD + 1):
            if k < KD:
                ts.append(dve(V.scalar_tensor_tensor, sq[:, k, :], hx[:, k, :],
                              cur[:, (3 * j + 1) * KD + k:(3 * j + 1) * KD + k + 1], stat[0][:, 0:T], ALU.mult, ALU.mult,
                              after=[tr]))
                sh = cur[:, 3 * j * KD + k:3 * j * KD + k + 1]
                th = act(am[0][:, k, :], sq[:, k, :], ACT.Identity, bias=sh, after=[ts[k]], settled=True)
            if k:
                dve(V.scalar_tensor_tensor, am[1][:, k - 1, :], sq[:, k - 1, :], before[0], am[0][:, k - 1, :].bitcast(F32),
                    ALU.add, ALU.subtract, after=[before[1]])
            before = (sh, th)
        p.wait("pe", *p.now("dve"))

    def lv(ap, l, pat="l (k p) n -> l p k n"):
        return ap.rearrange(pat, p=P)[bass.ds(l, 1)].rearrange("l p k n -> p (l k) n")

    def macaron(l, j, wg, wu, wd):
        with ExitStack() as f:
            am = [sb(f, nm(), [P, KD, T], F32R) for _ in range(2)]
            gate_up = [lv(wg, l), lv(wu, l)]
            stage(gate_up_slab(gate_up, 0))
            normed(h, j, am)

            def out_one(c, psum, t, raised):
                hc = h[:, bass.ds(c, 1), :].rearrange("p a t -> p (a t)")
                g_ = small[:, 0:1]
                t0 = dve(V.tensor_copy, g_, cur[:, bass.ds(c + (3 * j + 2) * KD, 1)], after=[*p.now("dve")])
                dve(V.scalar_tensor_tensor, hc, psum, g_, hc, ALU.mult, ALU.add, after=[t, t0], also=raised)
                add_square(hc)
            feed_forward(gate_up, lv(wd, l), am, out_one)
            p.fence()

    KB = DA_W // P
    conv_read = [p.sem(n, "act") for n in ("conv_qk_read", "conv_v_read")]
    prep_a, prep_d = p.sem("head_qk_ready", "act"), p.sem("head_steps_ready", "dve")
    head_done = [p.sem(f"head_done{b}", "dve") for b in range(2)]
    da_done = p.sem("da_bias_ready", "dve")

    def mixer(l):
        with ExitStack() as f:
            u = [sb(f, nm(), [P, KD, T], F32R) for _ in range(2)]
            ya = sb(f, "branch_a", [P, KD, T])
            zo = sb(f, "dn_gate_out", [P, DN_H, T])
            beta = sb(f, "beta", [P, 2, DN_H])
            gdec = sb(f, "log_decay", [P, 2, DN_H])
            rk = sb(f, "key_scale", [P, 2, 2, DN_H])
            rqb = sb(f, "query_scale_beta", [P, 2, 2, DN_H])
            wi = lv(a["w_in_2"], l)

            def dn_parts(hd, j):
                c = (2 * D, IN_Z) if j else (0, D)
                return [cols(wi, hd * P + c[0], P), cols(wi, hd * P + c[1], P)]

            def da_v_parts(i):
                return [cols(wi, i * T + (IN_DA + 2 * DA_W), T)]

            def gate_parts(i):
                return [cols(wi, i * P + IN_GATE, P), cols(wi, i * P + (IN_GATE + D), P)]
            w_a, w_b, w_o = (lv(a[n], l) for n in ("w_a_2", "w_b_2", "w_o_2"))
            stage([cols(wi, IN_BA, 2 * DN_H)])
            normed(h, 1, u)
            stage(dn_parts(0, 0))
            wba = wview(st["staged"][0][1], KD, 2 * DN_H)
            ba = sb(f, "beta_decay_in", [P, 2, 2 * DN_H])

            def compute(_, bank, __):
                for tt in range(2):
                    m = token_major(bank[0][:, tt * 16:(tt + 1) * 16], wba, 0, 16, u, tt * P)
                return m

            def evacuate(bank, t, raised):
                dve(V.tensor_copy, ba[:, :, :].rearrange("p a n -> p (a n)"), bank[0][:, 0:32], after=[t], also=raised)
            slab(compute, evacuate)
            act(beta[:, :, :], ba[:, :, 0:DN_H], ACT.Sigmoid, after=[*p.now("dve")])
            s0, s1, s2, s3, s4 = (small[:, 0:16], small[:, 16:32], small[:, 32:48], small[:, 48:64], stat[1][:, 0:16])
            r3 = lambda x: x.rearrange("p (a n) -> p a n", a=2)
            t = dve(V.tensor_tensor, r3(s0), ba[:, :, DN_H:2 * DN_H],
                    dtb[:, bass.ds(l, 1), :].broadcast_to([P, 2, DN_H]), ALU.add, after=[*p.now("dve")])
            chain = lambda op, *x, **k_: dve(op, *x, after=[*p.now("dve"), *p.now("act")], **k_)
            t = act(s1, s0, ACT.Abs, after=[*p.now("dve")])
            act(s1, s1, ACT.Exp, scale=-1.0, after=[t])
            chain(V.tensor_scalar, s2, s1, 2.0, None, ALU.add)
            chain(V.reciprocal, s2, s2)
            chain(V.tensor_tensor, s2, s2, s1, ALU.mult)
            chain(V.tensor_tensor, s3, s2, s2, ALU.mult)
            chain(V.tensor_scalar, s4, s3, 1.0 / 15, None, ALU.mult)
            for n in (13, 11, 9, 7, 5, 3):
                chain(V.scalar_tensor_tensor, s4, s4, 1.0 / n, s3, ALU.add, ALU.mult)
            chain(V.scalar_tensor_tensor, s4, s4, 1.0, s2, ALU.add, ALU.mult)
            chain(V.tensor_scalar, s0, s0, 0.0, None, ALU.max)
            chain(V.scalar_tensor_tensor, s4, s4, 2.0, s0, ALU.mult, ALU.add)
            act(s1[:, 0:DN_H], alog[:, bass.ds(l, 1), :].rearrange("p a n -> p (a n)"), ACT.Exp, after=[*p.now("dve")], settled=True)
            chain(V.scalar_tensor_tensor, gdec[:, :, :], r3(s4), -1.0, bc(s1[:, 0:DN_H], 2), ALU.mult, ALU.mult)
            p.fence()

            with ExitStack() as f2:
                vb = sb(f2, "dn_v_beta", [P, DN_H, 2, P])
                MT = sb(f2, "dn_m_t", [P, DN_H, TRI])
                Aqk = sb(f2, "dn_qk", [P, DN_H, TRI])
                with ExitStack() as f3:
                    qa = sb(f3, "dn_q", [P, DN_H, T])
                    ka = sb(f3, "dn_k", [P, DN_H, T])
                    with ExitStack() as f4:
                        cin = sb(f4, "conv_in", [P, 3, T + 3])
                        cy = sb(f4, "conv_out", [P, 3, T])
                        cw = sb(f4, "taps", [P, 4, 3])
                        dve(V.memset, cin[:, :, 0:3], 0.0)
                        p.fence()
                        row = lambda x, hd: x[:, bass.ds(hd, 1), 0:T].rearrange("p a t -> p (a t)")

                        def convolve(xs, t, reader, raised=None):
                            for jj in range(4):
                                for x in xs:
                                    src, tap = cin[:, x, jj:jj + T], cw[:, jj, x:x + 1]
                                    if jj == 0:
                                        t1 = dve(V.tensor_scalar, cy[:, x, :], src, tap, None, ALU.mult, after=[*t, reader],
                                                 also=raised)
                                    else:
                                        t1 = dve(V.scalar_tensor_tensor, cy[:, x, :], src, tap, cy[:, x, :], ALU.mult,
                                                 ALU.add, after=[tt_[x]])
                                    tt_[x] = t1
                        tt_ = {}

                        def one(hd, j):
                            w = wview(st["staged"][0][1], KD, T)

                            def compute(_, bank, __):
                                for c in range(2):
                                    m = feature_major(bank[c][:, 0:T], w, c * P, u, slice(0, T))
                                return m

                            def evacuate(bank, t, raised):
                                silu = lambda dst, src, after, **k_: act(dst, src, ACT.Silu, after=after, settled=True, **k_)
                                if j == 0:
                                    t1 = dve(V.tensor_copy, cw[:, :, :],
                                             cw_l[:, :, :, bass.ds(hd, 1)].rearrange("p j x h -> p j (x h)"))
                                    dve(V.tensor_copy, cin[:, 0, 3:], bank[0][:, 0:T], after=[t])
                                    t2 = dve(V.tensor_copy, cin[:, 1, 3:], bank[1][:, 0:T], also=raised)
                                    convolve((0, 1), [t1, t2], p.at(conv_read[0]))
                                    silu(row(qa, hd), cy[:, 0, :], [tt_[1]])
                                    silu(row(ka, hd), cy[:, 1, :], [], also=conv_read[0])
                                else:
                                    t2 = dve(V.tensor_copy, cin[:, 2, 3:], bank[0][:, 0:T], after=[t])
                                    t1 = silu(row(zo, hd), bank[1][:, 0:T], [t])
                                    convolve((2,), [t1, t2], p.at(conv_read[1]), raised)
                                    silu(row(Aqk, hd), cy[:, 2, :], [tt_[2]], also=conv_read[1])
                            slab(compute, evacuate)

                        def two_heads(i, last):
                            for j in range(4):
                                if j < 3:
                                    stage(dn_parts(i * 2 + (j + 1) // 2, (j + 1) % 2))
                                elif not last:
                                    stage(dn_parts(i * 2 + 2, 0))
                                one(i * 2 + j // 2, j % 2)
                        with p.loop(DN_H // 2 - 1) as i:
                            two_heads(i, False)
                        two_heads(DN_H // 2 - 1, True)
                    p.wait("pe", *p.now("act"))
                    for n in range(4):
                        tt, h0 = n // 2, (n % 2) * 4
                        for i in range(4):
                            m = TE.transpose(AB[n][:, i * P:(i + 1) * P], Aqk[:, h0 + i, tt * P:(tt + 1) * P], ident)
                        t = p.up(m, "done_pe")
                        dve(V.tensor_tensor, vb[:, h0:h0 + 4, tt, :], AB[n][:, :].rearrange("p (a n) -> p a n", a=4),
                            beta[:, tt, h0:h0 + 4].unsqueeze(2).broadcast_to([P, 4, P]), ALU.mult, after=[t])
                    for n, src in enumerate((qa, ka)):
                        t = act(sq[:, :, :], src[:, :, :], ACT.Square, after=[*p.now("pe"), *p.now("act")])
                        p.wait("pe", t)
                        for tt in range(2):
                            for hh in range(DN_H):
                                c = (n * 2 + tt) * DN_H + hh
                                m = TE.matmul(banks[0][:, c:c + 1], sq[:, hh, tt * P:(tt + 1) * P], ones[:, 0:1],
                                              start=True, stop=True)
                        t = p.up(m, "done_pe")
                    fl4 = lambda x: x.rearrange("p a b n -> p (a b n)")
                    t = rsqrt(fl4(rk[:, :, :, :]), banks[0][:, 0:4 * DN_H], 1.0, RMS_EPS, [t])
                    dve(V.tensor_scalar, rqb[:, 0, :, :], rk[:, 0, :, :], P ** -0.5, None, ALU.mult, after=[t])
                    dve(V.tensor_tensor, rqb[:, 1, :, :], rk[:, 1, :, :], beta[:, :, :], ALU.mult, after=[t])
                    p.fence()
                    with ExitStack() as f4:
                        two_of = lambda name, shape: [sb(f4, f"{name}{b}", shape) for b in range(2)]
                        G0, E = two_of("decay_steps", [P, TRI]), two_of("decay_exp", [P, TRI])
                        Eb = [two_of(f"decay_masked{n}", [P, TRI]) for n in range(2)]
                        sc = two_of("head_scalars", [P, 2, 4])
                        qh = two_of("head_qk", [P, 2, T])
                        bank_of = [AB, banks[0:4]]

                        def prepare(hd, b):
                            one_h, free = bass.ds(hd, 1), p.at(head_done[b])
                            for n, x in enumerate((gdec[:, :, one_h], rk[:, 1, :, one_h], rqb[:, 0, :, one_h],
                                                   rqb[:, 1, :, one_h])):
                                t = dve(V.tensor_copy, sc[b][:, :, n:n + 1], x, after=[free])
                            act(qh[b][:, 0, :], qa[:, one_h, :].rearrange("p a t -> p (a t)"), ACT.Copy, after=[free],
                                settled=True)
                            act(qh[b][:, 1, :], ka[:, one_h, :].rearrange("p a t -> p (a t)"), ACT.Copy, also=prep_a)
                            dve(V.tensor_scalar, G0[b][:, 0:T], le_m, sc[b][:, 0, 0:1], None, ALU.mult, after=[t])
                            dve(V.tensor_scalar, G0[b][:, T:TRI], le_m[:, 0:P], sc[b][:, 1, 0:1], None, ALU.mult, also=prep_d)

                        def one_head(hd, b, last):
                            one_h, bank = bass.ds(hd, 1), bank_of[b]
                            p.wait("pe", p.at(prep_d), p.at(head_done[b]))
                            TE.matmul(bank[0][:, 0:T], gt_m, G0[b][:, 0:T], start=True, stop=False)
                            TE.matmul(bank[0][:, P:T], ones, G0[b][:, T:TRI], start=False, stop=True)
                            m = TE.matmul(bank[0][:, T:TRI], gt_m, G0[b][:, T:TRI], start=True, stop=True)
                            tD = p.up(m, "done_pe")
                            for n in range(2):
                                for tt in range(2):
                                    m = TE.matmul(bank[1][:, (2 * n + tt) * P:(2 * n + tt + 1) * P],
                                                  sc[b][:, tt, 2 + n:3 + n].broadcast_to([P, P]), ident, start=True, stop=True)
                            p.wait("pe", p.at(prep_a))
                            kk = qh[b][:, 1, :]
                            for n in range(2):
                                TE.matmul(bank[2 + n][:, 0:T], kk[:, 0:P], qh[b][:, n, :], start=True, stop=True)
                                m = TE.matmul(bank[2 + n][:, T:TRI], kk[:, P:T], qh[b][:, n, P:T], start=True, stop=True)
                            tK = p.up(m, "done_pe")
                            if not last:
                                prepare(hd + 1, 1 - b)
                            t = act(E[b][:, :], bank[0][:, 0:TRI], ACT.Exp, after=[tD])
                            for n, mask in ((0, incl), (1, strict)):
                                dst, Em = (Aqk, MT)[n], Eb[n][b]
                                t1 = pool(G.tensor_tensor, out=Em[:, :], in0=E[b][:, :], in1=mask, op=ALU.mult, after=[t])
                                fac = bank[1][:, n * T:(n + 1) * T]
                                dve(V.tensor_tensor, Em[:, 0:T], Em[:, 0:T], fac, ALU.mult, after=[t1, tK])
                                t2 = dve(V.tensor_tensor, Em[:, T:TRI], Em[:, T:TRI], fac[:, P:T], ALU.mult)
                                for tt, s_ in ((0, slice(0, T)), (1, slice(T, TRI))):
                                    dve(V.scalar_tensor_tensor, dst[:, one_h, s_].rearrange("p a t -> p (a t)"),
                                        bank[2 + n][:, s_], sc[b][:, tt, 1:2], Em[:, s_], ALU.mult, ALU.mult, after=[t2],
                                        also=head_done[b] if n and tt else None)
                        prepare(0, 0)
                        with p.loop(DN_H // 2 - 1) as i:
                            for b in range(2):
                                one_head(i * 2 + b, b, False)
                        for b in range(2):
                            one_head(DN_H - 2 + b, b, b == 1)
                        p.fence()
                with ExitStack() as f3:
                    XT = sb(f3, "inv_t", [P, 2, DN_H, P])
                    Xc = sb(f3, "inv_tiles", [P, 2, DN_H, HALF])
                    XTc = sb(f3, "inv_tiles_t", [P, 2, DN_H, HALF])
                    Y = [sb(f3, nm(), [P, DN_H, HALF]) for _ in range(2)]
                    fl = lambda x: x.rearrange("p a t -> p (a t)")
                    rows_of = [slice(0, HALF), slice(HALF, P)]
                    blk = [slice(i * HALF, (i + 1) * HALF) for i in range(DN_H)]

                    def each_tile(bank, lhs, rhs):
                        p.settle("pe")
                        for r_ in rows_of:
                            for i in range(DN_H):
                                m = TE.matmul(bank[r_, blk[i]], lhs(i, r_), rhs(i, r_), start=True, stop=True)
                        return p.up(m, "done_pe")
                    joined = []
                    for tt in range(2):
                        for r_ in rows_of:
                            t = dve(V.tensor_tensor, XTc[r_, tt], MT[r_, :, tt * T + r_.start:tt * T + r_.stop],
                                    lev[0][r_, :].unsqueeze(1).broadcast_to([HALF, DN_H, HALF]), ALU.mult)
                        for r_ in rows_of:
                            t = dve(V.tensor_tensor, XTc[r_, tt], ident[r_, r_].unsqueeze(1).broadcast_to([HALF, DN_H, HALF]),
                                    XTc[r_, tt], ALU.subtract, after=[t])
                        p.wait("pe", t)
                        t = each_tile(AB[2 * tt], lambda i, r_: XTc[r_, tt, i, :], lambda i, r_: ident[r_, r_])
                        joined.append(act(fl(Xc[:, tt]), AB[2 * tt][:, :], ACT.Copy, after=[t]))
                    for j in range(1, NLEV - 1):
                        ty = []
                        for tt in range(2):
                            p.wait("pe", joined[tt])
                            t = each_tile(AB[2 * tt], lambda i, r_: MT[r_, i, tt * T + r_.start:tt * T + r_.stop],
                                          lambda i, r_: Xc[r_, tt, i, :])
                            ty.append(dve(V.tensor_tensor, Y[tt][:, :, :], AB[2 * tt][:, :].rearrange("p (a n) -> p a n", a=DN_H),
                                          bc(lev[j], DN_H), ALU.mult, after=[t]))
                        for tt in range(2):
                            p.wait("pe", ty[tt])
                            t1 = each_tile(AB[2 * tt + 1], lambda i, r_: XTc[r_, tt, i, :], lambda i, r_: Y[tt][r_, i, :])
                            t2 = each_tile(banks[2 * tt], lambda i, r_: Y[tt][r_, i, :], lambda i, r_: XTc[r_, tt, i, :])
                            x, xt = fl(Xc[:, tt]), fl(XTc[:, tt])
                            dve(V.tensor_tensor, x, x, AB[2 * tt + 1][:, :], ALU.subtract, after=[t1])
                            joined[tt] = dve(V.tensor_tensor, xt, xt, banks[2 * tt][:, :], ALU.subtract, after=[t2])
                    top, low = rows_of
                    t = pool(G.memset, XT[low, :, :, 0:HALF], 0.0, settled=True)
                    for tt in range(2):
                        p.wait("pe", joined[tt])
                        p.settle("pe")
                        for i in range(DN_H):
                            m = TE.matmul(AB[2 * tt][low, blk[i]], MT[top, i, tt * T + HALF:tt * T + P], Xc[top, tt, i, :],
                                          start=True, stop=True)
                        t = p.up(m, "done_pe")
                        ty[tt] = act(fl(Y[tt])[low, :], AB[2 * tt][low, :], ACT.Copy, after=[t])
                        for r_ in rows_of:
                            dve(V.tensor_copy, XT[r_, tt, :, r_], XTc[r_, tt], after=[joined[tt]])
                    for tt in range(2):
                        p.wait("pe", ty[tt])
                        p.settle("pe")
                        for i in range(DN_H):
                            m = TE.matmul(AB[2 * tt + 1][top, blk[i]], Y[tt][low, i, :], XTc[low, tt, i, :],
                                          start=True, stop=True)
                        t = p.up(m, "done_pe")
                        dve(V.tensor_scalar, XT[top, tt, :, low], AB[2 * tt + 1][top, :].rearrange("p (a n) -> p a n", a=DN_H),
                            -1.0, None, ALU.mult, after=[t])
                    p.fence()
                    groups = [(gi, 4 * gi, (AB, banks[0:4])[gi]) for gi in range(2)]
                    vn = [[x[:, gi].rearrange("p (a c) n -> p a (c n)", c=2) for gi in range(2)] for x in (Xc, XTc)]
                    heads = range(4)
                    col4 = [slice(i * P, (i + 1) * P) for i in heads]

                    def for_groups(last, issue):
                        ts = []
                        for gi, h0, bank in groups:
                            if last:
                                p.wait("pe", last[gi])
                            for i in heads:
                                m = issue(gi, h0, bank, i)
                            ts.append(p.up(m, "done_pe"))
                        return ts
                    t = for_groups(None, lambda gi, h0, bank, i: TE.matmul(
                        bank[0][:, col4[i]], XT[:, 0, h0 + i, :], vb[:, h0 + i, 0, :], start=True, stop=True))
                    t = [act(fl(vn[0][gi]), bank[0][:, :], ACT.Copy, after=[t[gi]]) for gi, h0, bank in groups]
                    t = for_groups(t, lambda gi, h0, bank, i: TE.matmul(
                        bank[1][:, col4[i]], MT[:, h0 + i, P:T], vn[0][gi][:, i, :], start=True, stop=True))
                    t = [dve(V.tensor_tensor, vb[:, h0:h0 + 4, 1, :], vb[:, h0:h0 + 4, 1, :],
                             bank[1][:, :].rearrange("p (a n) -> p a n", a=4), ALU.subtract, after=[t[gi]])
                         for gi, h0, bank in groups]
                    t = for_groups(t, lambda gi, h0, bank, i: TE.matmul(
                        bank[0][:, col4[i]], XT[:, 1, h0 + i, :], vb[:, h0 + i, 1, :], start=True, stop=True))
                    t = [act(fl(vn[1][gi]), bank[0][:, :], ACT.Copy, after=[t[gi]]) for gi, h0, bank in groups]

                    def out_of(gi, h0, bank, i):
                        o_ = bank[2 + i // 2][:, (i % 2) * T:(i % 2 + 1) * T]
                        TE.matmul(o_, vn[0][gi][:, i, :], Aqk[:, h0 + i, 0:T], start=True, stop=False)
                        return TE.matmul(o_[:, P:T], vn[1][gi][:, i, :], Aqk[:, h0 + i, T:TRI], start=False, stop=True)
                    t = for_groups(t, out_of)
                    flat = lambda x: x.rearrange("p a t -> p (a t)")
                    tq = []
                    for gi, h0, bank in groups:
                        for i in range(2):
                            t1 = act(flat(sq[:, h0 + 2 * i:h0 + 2 * i + 2, :]), bank[2 + i][:, :], ACT.Square, after=[t[gi]])
                            zz = flat(zo[:, h0 + 2 * i:h0 + 2 * i + 2, :])
                            dve(V.scalar_tensor_tensor, zz, bank[2 + i][:, :], dnn_now[:, 0:1], zz, ALU.mult, ALU.mult,
                                after=[t1])
                        tq.append(t1)
                    tS = for_groups(tq, lambda gi, h0, bank, i: [TE.matmul(
                        AB[0][:, 2 * (h0 + i) + tt:2 * (h0 + i) + tt + 1], sq[:, h0 + i, tt * P:(tt + 1) * P],
                        ones[:, 0:1], start=True, stop=True) for tt in range(2)][1])
                    rz = small[:, 0:2 * DN_H]
                    t = rsqrt(rz, AB[0][:, 0:2 * DN_H], 1.0 / P, RMS_EPS, [tS[1]])
                    t = for_groups([t, t], lambda gi, h0, bank, i: [TE.matmul(
                        bank[i // 2][:, (2 * (i % 2) + tt) * P:(2 * (i % 2) + tt + 1) * P],
                        rz[:, 2 * (h0 + i) + tt:2 * (h0 + i) + tt + 1].broadcast_to([P, P]), ident,
                        start=True, stop=True) for tt in range(2)][1])
                    for gi, h0, bank in groups:
                        for i in range(2):
                            zz = flat(zo[:, h0 + 2 * i:h0 + 2 * i + 2, :])
                            dve(V.tensor_tensor, zz, zz, bank[i][:, :], ALU.mult, after=[t[gi], *p.now("dve")])
                    stage([cols(w_a, 0, T)])
                    p.fence()

            def project(src, wvw, kc, dst, then):
                def one(i):
                    w = wview(st["staged"][0][1], kc, T)

                    def compute(_, bank, __):
                        for c in range(2):
                            m = feature_major(bank[0][:, c * T:(c + 1) * T], w, c * P, src, slice(0, T), kc=kc)
                        return m

                    def evacuate(bank, t, raised):
                        dve(V.tensor_copy, dst[:, 2 * i:2 * i + 2, :].rearrange("p a t -> p (a t)"), bank[0][:, :],
                            after=[t], also=raised)
                    slab(compute, evacuate)
                stream(4, lambda i: [cols(wvw, i * T, T)], one, staged=True, then=then)

            with ExitStack() as f2:
                os_ = [sb(f2, nm(), [P, KD, T], F32R) for _ in range(2)]
                for k in range(0, KD, 2):
                    t = split(zo[:, k:k + 2, :], os_[0][:, k:k + 2, :], os_[1][:, k:k + 2, :], [])
                p.wait("pe", t)
                project(os_, w_a, KD, ya, lambda: stage(da_v_parts(0)))
                p.fence()
            yb = zo
            with ExitStack() as f2:
                ob = [sb(f2, nm(), [P, KB, T], F32R) for _ in range(2)]
                v = sb(f2, "da_v", [P, 2, DA_W])
                vp = sb(f2, "da_v_pair", [P, 2, P])
                qk = sb(f2, "da_qk", [P, 2, T])
                bias = sb(f2, "da_bias", [P, 2, TRI])
                probs = [sb(f2, nm(), [P, T]) for _ in range(4)]
                PT = sb(f2, "da_probs_t", [P, 2, TRI])
                sl = sb(f2, "slopes_now", [P, 2])

                def one(i):
                    w = wview(st["staged"][0][1], KD, T)

                    def compute(_, bank, __):
                        for tt in range(2):
                            m = token_major(bank[0][:, tt * T:(tt + 1) * T], w, 0, T, u, tt * P)
                        return m

                    def evacuate(bank, t, raised):
                        dve(V.tensor_copy, v[:, :, i * T:(i + 1) * T], bank[0][:, :].rearrange("p (a n) -> p a n", a=2),
                            after=[t], also=raised)
                    slab(compute, evacuate)
                stream(3, da_v_parts, one, staged=True)

                def da_bias(n, free):
                    t = dve(V.tensor_copy, sl[:, :], slope[:, bass.ds(n * 2, 2)], after=[*p.now("dve")])
                    for e in range(2):
                        dve(V.scalar_tensor_tensor, bias[:, e, :], da_dist, sl[:, e:e + 1], da_lnc, ALU.mult, ALU.add,
                            after=[t, *free], also=da_done)

                def da_project(n):
                    w = wview(st["staged"][0][1], KD, T)

                    def compute(_, bank, __):
                        for c in range(2):
                            m = feature_major(bank[c][:, 0:T], w, c * P, u, slice(0, T))
                        return m

                    def evacuate(bank, t, raised):
                        t1 = act(qk[:, 1, :], bank[1][:, 0:T], ACT.Copy, after=[t])
                        dve(V.tensor_scalar, qk[:, 0, :], bank[0][:, 0:T], DA_DH ** -0.5, None, ALU.mult, after=[t, t1],
                            also=raised)
                    slab(compute, evacuate)

                def da_scores(bank, e, tt):
                    r_, n = slice(e * DA_DH, (e + 1) * DA_DH), (tt + 1) * P
                    TE.matmul(bank[:, 0:n], qk[r_, 0, tt * P:(tt + 1) * P], qk[r_, 1, 0:n], start=True, stop=False)
                    return TE.matmul(bank[:, 0:n], ident, bias[:, e, tt * P:tt * P + n], start=False, stop=True)

                def da_transposed(e, tt, bank):
                    return (PT[:, e, P:TRI], bank[:, 0:T]) if tt else (PT[:, e, 0:P], bank[:, 0:P])

                def da_values(bank, e):
                    r_ = slice(e * DA_DH, (e + 1) * DA_DH)
                    TE.matmul(bank[r_, 0:T], vp[:, 0, r_], PT[:, e, 0:T], start=True, stop=False)
                    return TE.matmul(bank[r_, P:T], vp[:, 1, r_], PT[:, e, T:TRI], start=False, stop=True)
                attention(KB, lambda n: [cols(wi, n * P + IN_DA, P), cols(wi, n * P + (IN_DA + DA_W), P)], da_project,
                          da_bias, da_done, da_scores, lambda tt: tt + 1, probs, da_transposed,
                          lambda n: (vp[:, :, :], v[:, :, bass.ds(n * P, P)]), da_values, ob,
                          then=lambda: stage([cols(w_b, 0, T)]))
                p.wait("pe", *p.now("dve"))
                project(ob, w_b, KB, yb, lambda: stage(gate_parts(0)))
                p.fence()
            with ExitStack() as f2:
                mg = [sb(f2, nm(), [P, KD, T], F32R) for _ in range(2)]
                sg = [sb(f2, nm(), [P, 2 * T]) for _ in range(2)]
                mt_ = [sb(f2, nm(), [P, T]) for _ in range(2)]

                def one(i):
                    q_ = st["set"]
                    w = wview(st["staged"][0][1], KD, T)

                    def compute(_, bank, __):
                        for c in range(2):
                            m = feature_major(bank[0][:, c * T:(c + 1) * T], w, c * P, u, slice(0, T))
                        return m

                    def evacuate(bank, t, raised):
                        s_ = sg[q_]
                        t1 = act(s_[:, :], bank[0][:, :], ACT.Sigmoid, after=[t])
                        dve(V.tensor_tensor, mt_[q_][:, :], s_[:, 0:T], ya[:, i, :], ALU.mult, after=[t1], also=raised)
                        t1 = dve(V.tensor_tensor, s_[:, T:2 * T], s_[:, T:2 * T], yb[:, i, :], ALU.mult)
                        t1 = dve(V.tensor_tensor, mt_[q_][:, :], mt_[q_][:, :], s_[:, T:2 * T], ALU.add, after=[t1])
                        split(mt_[q_][:, :], mg[0][:, i, :], mg[1][:, i, :], [t1])
                    slab(compute, evacuate)
                stream(KD, gate_parts, one, staged=True, then=lambda: stage([cols(w_o, 0, T)]))
                p.wait("pe", *p.now("dve"))

                def two(i):
                    w = wview(st["staged"][0][1], KD, T)

                    def compute(_, bank, __):
                        for c in range(2):
                            m = feature_major(bank[0][:, c * T:(c + 1) * T], w, c * P, mg, slice(0, T))
                        return m

                    def evacuate(bank, t, raised):
                        for c in range(2):
                            n = 2 * i + c
                            dve(V.scalar_tensor_tensor, h[:, n, :], bank[0][:, c * T:(c + 1) * T],
                                cur[:, 5 * KD + n:5 * KD + n + 1], h[:, n, :], ALU.mult, ALU.add, after=[t],
                                also=raised if c else None)
                            add_square(h[:, n, :])
                    slab(compute, evacuate)
                stream(4, lambda i: [cols(w_o, i * T, T)], two, staged=True)
                p.fence()

    t = pool(G.memset, square_sum[:, :], 0.0, also=square_read)
    for k in range(KD):
        add_square(h[:, k, :])
    n_layers = 2
    with p.loop(n_layers) as l:
        one_l = bass.ds(l, 1)
        dve(V.tensor_copy, gl[:, :, :], lng[:, one_l, :, :].rearrange("p a j k -> p (a j) k"))
        dve(V.tensor_copy, cw_l[:, :, :, :].rearrange("p j x h -> p (j x h)"),
            convw[:, one_l, :, :, :].rearrange("p a j x h -> p (a j x h)"))
        t = dve(V.tensor_copy, dnn_now[:, :], dnn[:, one_l])
        p.wait("dve", t)
        t = dve(V.tensor_copy, cur[:, :], mods2[:, one_l, :].rearrange("p a n -> p (a n)"), after=[*p.now("dve")])
        for j in range(3):
            sc_, gt_ = cur[:, (3 * j + 1) * KD:(3 * j + 2) * KD], cur[:, (3 * j + 2) * KD:(3 * j + 3) * KD]
            dve(V.scalar_tensor_tensor, sc_, sc_, 1.0, gl[:, j, :], ALU.add, ALU.mult, after=[t])
            if j != 1:
                dve(V.tensor_scalar, gt_, gt_, 0.5, None, ALU.mult, after=[t])
        p.fence()
        macaron(l, 0, a["ffn1_wg_2"], a["ffn1_wu_2"], a["ffn1_wd_2"])
        if upto != 5:
            mixer(l)
            macaron(l, 2, a["ffn2_wg_2"], a["ffn2_wu_2"], a["ffn2_wd_2"])
    if upto < 99:
        dump(h); return
    t = rms_scale(stat[0][:, 0:T])
    for k in range(KD):
        dve(V.scalar_tensor_tensor, h[:, k, :], h[:, k, :], par[:, 0, C_FIN + k:C_FIN + k + 1], stat[0][:, 0:T],
            ALU.mult, ALU.mult, after=[t])
    dump(h)
    b2.close()


USED = ["x", "c", "ctx", "c_ctx", "ada_w", "ada_b", "ln_g", "ln_b", "ffn_w13", "ffn_w2", "ret_w_in", "ret_decay",
        "ret_w_out", "na_w_qkv", "na_rpb", "na_w_out", "c_2", "ada_w_2", "ada_b_2", "ln_ffn1_2", "ln_mix_2",
        "ln_ffn2_2", "ffn1_wg_2", "ffn1_wu_2", "ffn1_wd_2", "w_in_2", "conv_w_2", "a_log_2", "dt_bias_2",
        "dn_norm_2", "w_a_2", "w_b_2", "w_o_2", "ffn2_wg_2", "ffn2_wu_2", "ffn2_wd_2", "final_norm_2"]


def program(nc, arrays, counted, upto=99):
    aps = {n: nc.dram_tensor("in_" + n, list(v.shape), F32, kind="ExternalInput").ap() for n, v in arrays.items()}
    out = nc.dram_tensor("hidden_out", [1, T, D], F32, kind="ExternalOutput").ap()
    build(nc, aps, out, counted, upto)


def kernel(**inputs):
    import concourse.bacc as _bacc
    from concourse.bass_utils import run_bass_kernel_spmd as _run

    arrays = {n: np.ascontiguousarray(inputs[n]) for n in USED}
    for n, t in enumerate(shape_tables()):
        arrays[f"table{n}"] = t
    counted = {}
    for _ in range(2):
        nc = _bacc.Bacc("TRN2", target_bir_lowering=False, num_devices=1)
        program(nc, arrays, counted)
    r = _run(nc, [{"in_" + n: v for n, v in arrays.items()}], core_ids=[0])
    return r.results[0]["hidden_out"]
```
